# Optimizing a Trainium2 kernel written in Bass

```python
import math
import jax, jax.numpy as jnp
from jax import lax
import numpy as np

D_MODEL = 1024
BATCH = 1
SEQ = 256
DEPTH = 2

HEAD_DIM = 64
A_HEADS = D_MODEL // (4 * HEAD_DIM)
A_VDIM = 2 * HEAD_DIM
B_HEADS = D_MODEL // (2 * HEAD_DIM)
C_HEADS = D_MODEL // HEAD_DIM
Q_BLOCK = 128
N_GROUPS = 4
EXPERTS_PER_GROUP = 4
N_EXPERTS = N_GROUPS * EXPERTS_PER_GROUP
TOP_K = 2
D_EXPERT = D_MODEL
MOE_BLOCK = 128
EPS = 1e-6
N_EVEN = (DEPTH + 1) // 2
N_ODD = DEPTH // 2

kernel_name = 'hybrid_diff_stickbreak_fox_hmoe'

def rms_norm(x, g):
    xf = x.astype(jnp.float32)
    y = xf * lax.rsqrt(jnp.mean(xf * xf, axis=-1, keepdims=True) + EPS)
    return (y * g.astype(jnp.float32)).astype(x.dtype)

def to_heads(x, n, d):
    b, s, _ = x.shape
    return x.reshape(b, s, n, d).transpose(0, 2, 1, 3)

def from_heads(x):
    b, h, s, d = x.shape
    return x.transpose(0, 2, 1, 3).reshape(b, s, h * d)

def to_blocks(x):
    b, h, s = x.shape[:3]
    y = x.reshape((b, h, s // Q_BLOCK, Q_BLOCK) + x.shape[3:])
    return jnp.moveaxis(y, 2, 0)

def from_blocks(y):
    y = jnp.moveaxis(y, 0, 2)
    b, h, nb, q = y.shape[:4]
    return y.reshape((b, h, nb * q) + y.shape[4:])

def alibi_slopes(n):
    return np.array([2.0 ** (-8.0 * (i + 1) / n) for i in range(n)], dtype=np.float32)

def diff_attention(q1, q2, k1, k2, v, lam):
    s_len = q1.shape[2]
    scale = HEAD_DIM ** -0.5
    kpos = jnp.arange(s_len)
    slopes = jnp.asarray(alibi_slopes(A_HEADS))

    def block(args):
        qb1, qb2, i = args
        tpos = i * Q_BLOCK + jnp.arange(Q_BLOCK)
        dist = (tpos[:, None] - kpos[None, :]).astype(jnp.float32)
        causal = dist >= 0
        bias = -slopes[:, None, None] * dist

        def probs(qb, k):
            sc = jnp.einsum('bhqd,bhkd->bhqk', qb, k).astype(jnp.float32) * scale + bias
            return jax.nn.softmax(jnp.where(causal, sc, -jnp.inf), axis=-1)

        p = probs(qb1, k1) - lam * probs(qb2, k2)
        return jnp.einsum('bhqk,bhkd->bhqd', p.astype(v.dtype), v)

    nb = s_len // Q_BLOCK
    out = lax.map(block, (to_blocks(q1), to_blocks(q2), jnp.arange(nb)))
    return from_blocks(out)

def stick_breaking_attention(q, k, v):
    s_len = q.shape[2]
    scale = HEAD_DIM ** -0.5
    kpos = jnp.arange(s_len)

    def block(args):
        qb, i = args
        tpos = i * Q_BLOCK + jnp.arange(Q_BLOCK)
        before = tpos[:, None] > kpos[None, :]
        z = jnp.einsum('bhqd,bhkd->bhqk', qb, k).astype(jnp.float32) * scale
        log_beta = jax.nn.log_sigmoid(z)
        log_keep = jnp.where(before, jax.nn.log_sigmoid(-z), 0.0)
        acc = lax.cumsum(log_keep, axis=3, reverse=True) - log_keep
        w = jnp.where(before, jnp.exp(log_beta + acc), 0.0)
        return jnp.einsum('bhqk,bhkd->bhqd', w.astype(v.dtype), v)

    nb = s_len // Q_BLOCK
    out = lax.map(block, (to_blocks(q), jnp.arange(nb)))
    return from_blocks(out)

def forgetting_attention(q, k, v, cum_logf):
    s_len = q.shape[2]
    scale = HEAD_DIM ** -0.5
    kpos = jnp.arange(s_len)

    def block(args):
        qb, fb, i = args
        tpos = i * Q_BLOCK + jnp.arange(Q_BLOCK)
        causal = tpos[:, None] >= kpos[None, :]
        sc = jnp.einsum('bhqd,bhkd->bhqk', qb, k).astype(jnp.float32) * scale
        sc = sc + (fb[..., :, None] - cum_logf[..., None, :])
        p = jax.nn.softmax(jnp.where(causal, sc, -jnp.inf), axis=-1)
        return jnp.einsum('bhqk,bhkd->bhqd', p.astype(v.dtype), v)

    nb = s_len // Q_BLOCK
    out = lax.map(block, (to_blocks(q), to_blocks(cum_logf), jnp.arange(nb)))
    return from_blocks(out)

def even_mixer(h, w_in, q_gain, k_gain, lam_q1, lam_k1, lam_q2, lam_k2, subln_g, w_out, layer):
    b, s, _ = h.shape
    qa = A_HEADS * 2 * HEAD_DIM
    va = A_HEADS * A_VDIM
    qb = B_HEADS * HEAD_DIM
    cuts = list(np.cumsum([qa, qa, va, qb, qb]))
    proj = h @ w_in
    a_q, a_k, a_v, b_q, b_k, b_v = jnp.split(proj, cuts, axis=-1)
    a_q = rms_norm(a_q.reshape(b, s, A_HEADS, 2, HEAD_DIM), q_gain)
    a_k = rms_norm(a_k.reshape(b, s, A_HEADS, 2, HEAD_DIM), k_gain)
    q1 = a_q[..., 0, :].transpose(0, 2, 1, 3)
    q2 = a_q[..., 1, :].transpose(0, 2, 1, 3)
    k1 = a_k[..., 0, :].transpose(0, 2, 1, 3)
    k2 = a_k[..., 1, :].transpose(0, 2, 1, 3)
    lam_init = 0.8 - 0.6 * math.exp(-0.3 * layer)
    f32 = jnp.float32
    lam = (jnp.exp(jnp.sum(lam_q1.astype(f32) * lam_k1.astype(f32)))
           - jnp.exp(jnp.sum(lam_q2.astype(f32) * lam_k2.astype(f32))) + lam_init)
    o_a = diff_attention(q1, q2, k1, k2, to_heads(a_v, A_HEADS, A_VDIM), lam)
    o_a = rms_norm(o_a, subln_g) * (1.0 - lam_init)
    o_b = stick_breaking_attention(to_heads(b_q, B_HEADS, HEAD_DIM),
                                   to_heads(b_k, B_HEADS, HEAD_DIM),
                                   to_heads(b_v, B_HEADS, HEAD_DIM))
    o = jnp.concatenate([from_heads(o_a), from_heads(o_b)], axis=-1)
    return o @ w_out

def odd_mixer(h, w_in, b_f, q_gain, k_gain, w_out):
    b, s, _ = h.shape
    w = C_HEADS * HEAD_DIM
    proj = h @ w_in
    q, k, v, f = jnp.split(proj, [w, 2 * w, 3 * w], axis=-1)
    q = rms_norm(q.reshape(b, s, C_HEADS, HEAD_DIM), q_gain).transpose(0, 2, 1, 3)
    k = rms_norm(k.reshape(b, s, C_HEADS, HEAD_DIM), k_gain).transpose(0, 2, 1, 3)
    v = to_heads(v, C_HEADS, HEAD_DIM)
    log_f = jax.nn.log_sigmoid(f.astype(jnp.float32) + b_f.astype(jnp.float32))
    cum = jnp.cumsum(log_f, axis=1).transpose(0, 2, 1)
    o = forgetting_attention(q, k, v, cum)
    return from_heads(o) @ w_out

def hier_moe(h, w_group, b_group, w_router, b_router, w_gate, w_up, w_down):
    b, s, d = h.shape
    xt = h.reshape(-1, d)
    n = xt.shape[0]
    f32 = jnp.float32
    g_logits = (xt @ w_group).astype(f32) + b_group.astype(f32)
    g_probs = jax.nn.softmax(g_logits, axis=-1)
    g_idx = jnp.argmax(g_logits, axis=-1).astype(jnp.int32)
    g_w = jnp.take_along_axis(g_probs, g_idx[:, None], axis=1)
    e_logits = ((xt @ w_router).astype(f32) + b_router.astype(f32)).reshape(n, N_GROUPS, EXPERTS_PER_GROUP)
    e_in = jnp.take_along_axis(e_logits, g_idx[:, None, None], axis=1)[:, 0]
    top_v, top_i = lax.top_k(e_in, TOP_K)
    top_w = jax.nn.softmax(top_v, axis=-1) * g_w
    expert = g_idx[:, None] * EXPERTS_PER_GROUP + top_i.astype(jnp.int32)
    nk = n * TOP_K
    e_flat = expert.reshape(-1)
    w_flat = top_w.reshape(-1)
    tok_flat = jnp.arange(nk, dtype=jnp.int32) // TOP_K
    order = jnp.argsort(e_flat)
    e_sorted = e_flat[order]
    counts = jnp.bincount(e_flat, length=N_EXPERTS)
    starts = jnp.cumsum(counts) - counts
    padded = (counts + MOE_BLOCK - 1) // MOE_BLOCK * MOE_BLOCK
    pad_ends = jnp.cumsum(padded)
    pad_starts = pad_ends - padded
    dest = pad_starts[e_sorted] + jnp.arange(nk) - starts[e_sorted]
    n_blocks = -(-nk // MOE_BLOCK) + N_EXPERTS
    p = n_blocks * MOE_BLOCK
    tok_buf = jnp.zeros((p,), jnp.int32).at[dest].set(tok_flat[order])
    w_buf = jnp.zeros((p,), f32).at[dest].set(w_flat[order])
    x_buf = xt[tok_buf].reshape(n_blocks, MOE_BLOCK, d)
    blk_e = jnp.searchsorted(pad_ends, jnp.arange(n_blocks) * MOE_BLOCK, side='right')
    blk_e = jnp.minimum(blk_e, N_EXPERTS - 1)

    def expert_block(args):
        xb, e = args
        return (jax.nn.silu(xb @ w_gate[e]) * (xb @ w_up[e])) @ w_down[e]

    y_buf = lax.map(expert_block, (x_buf, blk_e)).reshape(p, d)
    y_buf = y_buf * w_buf[:, None].astype(y_buf.dtype)
    out = jax.ops.segment_sum(y_buf, tok_buf, num_segments=n)
    return out.reshape(b, s, d).astype(h.dtype)

def setup_inputs(seed: int = 0) -> dict:
    key = jax.random.key(seed)
    ks = iter(jax.random.split(key, 32))
    nrm = lambda shape, scale: jax.random.normal(next(ks), shape, jnp.float32) * scale
    gain = lambda shape: 1.0 + nrm(shape, 0.02)
    d = D_MODEL
    return {
        'x': nrm((BATCH, SEQ, d), 1.0),
        'norm_mix_g': gain((DEPTH, d)),
        'norm_ffn_g': gain((DEPTH, d)),
        'ab_w_in': nrm((N_EVEN, d, 3 * d), d ** -0.5),
        'a_q_gain': gain((N_EVEN, HEAD_DIM)),
        'a_k_gain': gain((N_EVEN, HEAD_DIM)),
        'a_lam_q1': nrm((N_EVEN, HEAD_DIM), 0.1),
        'a_lam_k1': nrm((N_EVEN, HEAD_DIM), 0.1),
        'a_lam_q2': nrm((N_EVEN, HEAD_DIM), 0.1),
        'a_lam_k2': nrm((N_EVEN, HEAD_DIM), 0.1),
        'a_subln_g': gain((N_EVEN, A_VDIM)),
        'ab_w_out': nrm((N_EVEN, d, d), d ** -0.5),
        'c_w_in': nrm((N_ODD, d, 3 * d + C_HEADS), d ** -0.5),
        'c_b_f': jax.random.uniform(next(ks), (N_ODD, C_HEADS), jnp.float32, 2.0, 5.0),
        'c_q_gain': gain((N_ODD, HEAD_DIM)),
        'c_k_gain': gain((N_ODD, HEAD_DIM)),
        'c_w_out': nrm((N_ODD, d, d), d ** -0.5),
        'moe_w_group': nrm((DEPTH, d, N_GROUPS), d ** -0.5),
        'moe_b_group': nrm((DEPTH, N_GROUPS), 0.01),
        'moe_w_router': nrm((DEPTH, d, N_EXPERTS), d ** -0.5),
        'moe_b_router': nrm((DEPTH, N_EXPERTS), 0.01),
        'moe_w_gate': nrm((DEPTH, N_EXPERTS, d, D_EXPERT), d ** -0.5),
        'moe_w_up': nrm((DEPTH, N_EXPERTS, d, D_EXPERT), d ** -0.5),
        'moe_w_down': nrm((DEPTH, N_EXPERTS, D_EXPERT, d), D_EXPERT ** -0.5),
    }

def reference(x, norm_mix_g, norm_ffn_g, ab_w_in, a_q_gain, a_k_gain, a_lam_q1, a_lam_k1,
              a_lam_q2, a_lam_k2, a_subln_g, ab_w_out, c_w_in, c_b_f, c_q_gain, c_k_gain,
              c_w_out, moe_w_group, moe_b_group, moe_w_router, moe_b_router, moe_w_gate,
              moe_w_up, moe_w_down):
    for layer in range(DEPTH):
        i = layer // 2
        h = rms_norm(x, norm_mix_g[layer])
        if layer % 2 == 0:
            mix = even_mixer(h, ab_w_in[i], a_q_gain[i], a_k_gain[i], a_lam_q1[i], a_lam_k1[i],
                             a_lam_q2[i], a_lam_k2[i], a_subln_g[i], ab_w_out[i], layer)
        else:
            mix = odd_mixer(h, c_w_in[i], c_b_f[i], c_q_gain[i], c_k_gain[i], c_w_out[i])
        x = x + mix
        h = rms_norm(x, norm_ffn_g[layer])
        x = x + hier_moe(h, moe_w_group[layer], moe_b_group[layer], moe_w_router[layer],
                         moe_b_router[layer], moe_w_gate[layer], moe_w_up[layer], moe_w_down[layer])
    return x


_drawn_inputs = setup_inputs


def setup_inputs(seed=0):
    import zlib

    import numpy as np

    out = dict(_drawn_inputs(seed))
    spreads = {}
    factors = {'a_lam_k2': 3.506,
     'c_q_gain': 8.0,
     'c_k_gain': 5.213,
     'moe_b_group': 4.358,
     'moe_b_router': 5.781}
    for name, (base, spread) in spreads.items():
        noise = np.random.default_rng([zlib.crc32(name.encode()), seed]).standard_normal(out[name].shape)
        drawn = base * np.exp(spread * noise) if base else spread * noise
        out[name] = __import__('jax').numpy.asarray(drawn.astype(out[name].dtype))
    for name, factor in factors.items():
        out[name] = (out[name] * factor).astype(out[name].dtype)
    return out
```

```python
import math
from contextlib import ExitStack

import concourse.bass as bass
from concourse import mybir

F32 = mybir.dt.float32
BF16 = mybir.dt.bfloat16
I32 = mybir.dt.int32
ALU = mybir.AluOpType
ACT = mybir.ActivationFunctionType
AX_X = mybir.AxisListType.X

P = 128
D = 1024
T = 256
NT = T // P
NC = D // P
HALF = D // 2
SUB = NC // 2
COLS = 512
UNITS = 6
UNIT = SUB * D
HD = 64
A_HEADS, B_HEADS, C_HEADS = 4, 8, 16
JOBS = 8
N_GROUPS, PER_GROUP = 4, 4
N_EXPERTS = N_GROUPS * PER_GROUP
NR = N_GROUPS + N_EXPERTS
SLOTS = 64
ROUNDS = T // SLOTS
EPS = 1e-6
NEG = -1e30
SW = 3 * P
LAYERS = 2
LAM_INIT = 0.8 - 0.6 * math.exp(-0.3 * 0)
STEPS = 2 * UNITS
SCALE = HD ** -0.5

EVEN_UNITS = [("norm", 0), ("norm", 4), ("v", 0), ("scaled", 8), ("plain", 12), ("v", HALF)]
ODD_UNITS = [("norm", 0), ("norm", 4), ("norm", 8), ("norm", 12), ("v", 0), ("v", HALF)]
PLAN = [EVEN_UNITS, ODD_UNITS]

class LayerSignals:

    def __init__(self, nc, ctx, layer):
        def sem(name):
            return ctx.enter_context(nc.semaphore(f"{name}_{layer}"))

        self.squares_summed = sem("squares_summed")
        self.rsq_in = sem("rsq_in")
        self.rsq_guess = sem("rsq_guess")
        self.hn_ready = sem("hn_ready")
        self.ht_psum = sem("ht_psum")
        self.ht_ready = sem("ht_ready")
        self.proj_psum = sem("proj_psum")
        self.proj_out = sem("proj_out")
        self.squared = sem("squared")
        self.sumsq_psum = sem("sumsq_psum")
        self.root_done = sem("root_done")
        self.root_spread = sem("root_spread")
        self.root_applied = sem("root_applied")
        self.scores_psum = sem("scores_psum")
        self.max_ready = sem("max_ready")
        self.exp_done = sem("exp_done")
        self.p_ready = sem("p_ready")
        self.t_psum = sem("t_psum")
        self.pt_act = sem("pt_act")
        self.o_psum = sem("o_psum")
        self.o_ready = sem("o_ready")
        self.out_psum = sem("out_psum")
        self.x_mixed = sem("x_mixed")
        self.logits_psum = sem("logits_psum")
        self.logits_ready = sem("logits_ready")
        self.rt_shift = sem("rt_shift")
        self.rt_exp = sem("rt_exp")
        self.rt_gap = sem("rt_gap")
        self.rt_gap_exp = sem("rt_gap_exp")
        self.chosen = sem("chosen")
        self.rank_psum = sem("rank_psum")
        self.slots_ready = sem("slots_ready")
        self.take_ready = sem("take_ready")
        self.gathered = sem("gathered")
        self.xt_ready = sem("xt_ready")
        self.gate_exp = sem("gate_exp")
        self.gate_plus = sem("gate_plus")
        self.gate_inv = sem("gate_inv")
        self.gate_act = sem("gate_act")
        self.hid_ready = sem("hid_ready")
        self.give_ready = sem("give_ready")
        self.giveT_psum = sem("giveT_psum")
        self.giveT_ready = sem("giveT_ready")
        self.hidT_psum = sem("hidT_psum")
        self.hidT_ready = sem("hidT_ready")
        self.y_ready = sem("y_ready")
        self.scattered = sem("scattered")
        self.moe_out = sem("moe_out")
        self.unit_loaded = [sem(f"unit_loaded{u}") for u in range(UNITS)]
        self.unit_used = [sem(f"unit_used{u}") for u in range(UNITS)]
        if layer % 2 == 0:
            self.b_ln = sem("b_ln")
            self.o_squared = sem("o_squared")
            self.o_sumsq = sem("o_sumsq")
            self.sub_spread = sem("sub_spread")
            self.sub_applied = sem("sub_applied")
        else:
            self.pt_dve = sem("pt_dve")
            self.forget_psum = sem("forget_psum")
            self.forget_abs = sem("forget_abs")
            self.forget_ln = sem("forget_ln")
            self.cum_ready = sem("cum_ready")


def trunk(nc, x, norm_mix_g, norm_ffn_g, ab_w_in, a_q_gain, a_k_gain, a_lam_q1, a_lam_k1, a_lam_q2,
          a_lam_k2, a_subln_g, ab_w_out, c_w_in, c_b_f, c_q_gain, c_k_gain, c_w_out, moe_w_group,
          moe_b_group, moe_w_router, moe_b_router, moe_w_gate, moe_w_up, moe_w_down, out):
    with ExitStack() as ctx:
        def sb(name, shape, dt=F32):
            return ctx.enter_context(nc.sbuf_tensor(name, shape, dt))

        def sem(name):
            return ctx.enter_context(nc.semaphore(name))

        ring = sb("ring", [P, UNITS, UNIT])
        w_out_sb = sb("w_out_sb", [P, NC, D])
        x_sb = sb("x_sb", [P, NT, D])
        hn = sb("hn", [P, NT, D])
        oT = hn[:, :, :].rearrange("p a (b t) -> p (a b) t", t=T)
        hT = sb("hT", [P, NC, T])
        o_squares = hT[:, 0:A_HEADS, :]
        qkT = sb("qkT", [P, 16, T])
        v_sb = sb("v_sb", [P, NT, D])
        probs = sb("probs", [P, 4, SW])
        pT = sb("pT", [P, 4, SW])
        pT_flat = pT[:, :, :].rearrange("p a b -> p (a b)")
        squares = [pT_flat[:, COLS * i:COLS * (i + 1)] for i in range(2)]
        probs_flat = probs[:, :, :].rearrange("p a b -> p (a b)")
        ident = sb("ident", [P, P])
        ident_bf = sb("ident_bf", [P, P], BF16)
        ones_bf = sb("ones_bf", [P, P], BF16)
        before_bf = sb("before_bf", [P, P], BF16)
        neg_from = sb("neg_from", [P, P])
        neg_ones = sb("neg_ones", [P, P])
        strict = sb("strict", [P, P])
        mask_causal = sb("mask_causal", [P, SW], BF16)
        mask_strict = sb("mask_strict", [P, SW], BF16)
        dist = probs_flat[:, 0:SW]
        bias_a = sb("bias_a", [P, A_HEADS, SW], BF16)
        slide = sb("slide", [P, 62])
        slide_all = sb("slide_all", [P, 64])
        sel_head = sb("sel_head", [96, C_HEADS], BF16)
        slot_id = sb("slot_id", [P, 2, SLOTS])
        desc4 = sb("desc4", [P, 4])
        gain_mix = sb("gain_mix", [P, LAYERS, NC])
        gain_ffn = sb("gain_ffn", [P, LAYERS, NC])
        g_qk = sb("g_qk", [P, LAYERS, 2])
        g_sub = sb("g_sub", [P, 1])
        lam_in = probs_flat[:, SW:SW + 4 * HD].rearrange("p (a b) -> p a b", a=4)
        lam_prod = probs_flat[:, SW + 4 * HD:SW + 6 * HD].rearrange("p (a b) -> p a b", a=2)
        lam_s = sb("lam_s", [P, 4])
        neg_lam = sb("neg_lam", [P, 1])
        wf3 = sb("wf3", [P, NC, 96])
        b_f = sb("b_f", [96, 1])
        w_rt = sb("w_rt", [P, LAYERS, NC, NR])
        b_rt = sb("b_rt", [P, LAYERS, NR])
        ssq = sb("ssq", [P, NT])
        root_x = sb("root_x", [P, T])
        root_ln = sb("root_ln", [P, T])
        root_y = sb("root_y", [P, T])
        root_t = root_ln
        nmax = sb("nmax", [P, 2, 4])
        rsum = sb("rsum", [P, 2, 4])
        rinv = sb("rinv", [P, 2, 4])
        forget = [probs_flat[0:96, T * i:T * (i + 1)] for i in range(5)]
        cum = [sb(f"cum{i}", [96, T], BF16) for i in range(3)]
        cum_pos = sb("cum_pos", [96, T], BF16)
        cum_neg = sb("cum_neg", [96, T], BF16)
        v_flat = v_sb[:, :, :].rearrange("p a b -> p (a b)")
        lg = v_flat[:, 0:NT * NR].rearrange("p (t n) -> p t n", t=NT)
        rt = v_flat[:, 64:64 + 14 * NT * 4].rearrange("p (k t n) -> p k t n", k=14, t=NT)
        picked = v_flat[:, 192:224].rearrange("p (t g e) -> p t g e", t=NT, g=N_GROUPS)
        chosen_f = v_flat[:, 224:256].rearrange("p (t e) -> p t e", t=NT)
        weight_of = v_flat[:, 256:256 + NT * (ROUNDS * N_EXPERTS + 1)].rearrange("p (t e) -> p t e", t=NT)
        chosen_bf = sb("chosen_bf", [P, NT, N_EXPERTS], BF16)
        most = sb("most", [P, 2])
        slot_of = sb("slot_of", [P, NT, ROUNDS * N_EXPERTS + 1])
        n_turns = sb("n_turns", [P, LAYERS], I32)
        qk_flat = qkT[:, :, :].rearrange("p a b -> p (a b)")
        xT = qk_flat[:, 0:512].rearrange("p (c s) -> p c s", c=NC)
        take = qk_flat[:, 512:768].rearrange("p (t s) -> p t s", t=NT)
        give = qk_flat[:, 768:1024].rearrange("p (t s) -> p t s", t=NT)
        giveT = qk_flat[:, 1024:1280]
        gate_e = qk_flat[:, 1536:2048]
        sig = qk_flat[:, 2048:2560]
        hid = qk_flat[:, 2560:3072]
        hidT = qk_flat[:, 3072:3584].rearrange("p (s t) -> p s t", s=SUB)
        y_sb = qk_flat[:, 3584:4096]

        bank = [ctx.enter_context(nc.psum_tensor(f"bank{i}", [P, COLS], F32)) for i in range(8)]
        ACC, GATE, UP, Y, MISC = bank[0:4], bank[4], bank[5], bank[6], bank[7]
        O_BANK, SUM_BANK = bank[6], bank[7]

        pool_step = sem("pool_step")
        consts_made = sem("consts_made")
        act_step = sem("act_step")
        dve_step = sem("dve_step")
        x_loaded = sem("x_loaded")
        gains_loaded = sem("gains_loaded")
        params_loaded = sem("params_loaded")
        router_loaded = sem("router_loaded")
        forget_loaded = sem("forget_loaded")
        forget_zeroed = sem("forget_zeroed")
        tables_made = sem("tables_made")
        lam_sums = sem("lam_sums")
        lam_exp = sem("lam_exp")
        out_stored = sem("out_stored")
        wout_loaded = sem("wout_loaded")
        layers = []
        for i in range(LAYERS):
            layers.append(LayerSignals(nc, ctx, i))
        CONSTS = 16
        GAINS, PARAMS = 16 * 8, 16 * 13
        ROUTER, FORGET, WIN = 16 * 12, 16 * 9, 16 * 2

        w_in = [ab_w_in[0], c_w_in[0]]
        w_out = [ab_w_out[0], c_w_out[0]]
        norm_steps = [sum(2 for k, _ in units if k == "norm") for units in PLAN]
        SUBLN = 4

        def is_b(layer, job):
            return layer == 0 and job >= A_HEADS

        def rows(w):
            return w.rearrange("(h p s) n -> h p s n", h=2, s=SUB)

        def win_view(u):
            return ring[:, u, :].rearrange("p (c n) -> p c n", c=NC)

        def expert_rhs(u, s, half):
            return ring[:, u, s * D + HALF * half:s * D + HALF * (half + 1)]

        def maps_before(layer, job):
            return job + max(0, job - A_HEADS) if layer == 0 else 2 * job

        def roots_before(layer, which):
            names = ("mix", "qk", "sub", "ffn") if layer == 0 else ("mix", "qk", "ffn")
            return names.index(which) + 1

        def spread(column, shape):
            return column.to_broadcast(shape)

        def by_chunk(t, h, s):
            return hn[:, t, HALF * h:HALF * (h + 1)].rearrange("p (q s) -> p s q", s=SUB)[:, s, :]

        def gains(table, layer, h, n):
            g = table[:, layer, SUB * h:SUB * (h + 1)]
            return g.rearrange("p (c a) -> p c a", a=1).to_broadcast([P, SUB, n])

        def map_cols(i):
            return slice(0, P) if i == 0 else slice(P, SW)

        block = ctx.enter_context(nc.Block())

        @block.sync
        def _(sp):
            for t in range(NT):
                sp.dma_start(x_sb[:, t, :], x[0, t * P:(t + 1) * P, :]).then_inc(x_loaded, 16)

            def load(dst, src, signal):
                sp.dma_start(dst, src).then_inc(signal, 16)

            def load_win(layer, u):
                for h in range(2):
                    sp.dma_start(win_view(u)[:, SUB * h:SUB * (h + 1), :],
                                 rows(w_in[layer])[h, :, :, COLS * u:COLS * (u + 1)]
                                 ).then_inc(layers[layer].unit_loaded[u], 16)

            def load_wout(layer):
                sp.dma_start(w_out_sb[:, :, :], w_out[layer].rearrange("(c p) n -> p c n", p=P)
                             ).then_inc(wout_loaded, 16)

            def load_unit(layer, u, e):
                w = (moe_w_gate, moe_w_up, moe_w_down)[u // 2][layer]
                src = w[bass.ds(e, 1)].rearrange("e (h p s) n -> (e h) p (s n)", h=2, s=SUB)[u % 2]
                sp.dma_start(ring[:, u, :], src).then_inc(layers[layer].unit_loaded[u], 16)

            for i in range(LAYERS):
                for g, dst in ((norm_mix_g, gain_mix), (norm_ffn_g, gain_ffn)):
                    for h in range(2):
                        load(dst[:, i, SUB * h:SUB * (h + 1)],
                             g[i].rearrange("(h p s) -> h p s", h=2, s=SUB)[h], gains_loaded)
            for u in range(UNITS):
                load_win(0, u)
            for i, (q, k) in enumerate(((a_q_gain, a_k_gain), (c_q_gain, c_k_gain))):
                for j, g in enumerate((q, k)):
                    for m in range(2):
                        load(g_qk[HD * m:HD * (m + 1), i, j:j + 1],
                             g[0].rearrange("(p a) -> p a", a=1), params_loaded)
            load(g_sub[:, :], a_subln_g[0].rearrange("(p a) -> p a", a=1), params_loaded)
            for j, g in enumerate((a_lam_q1, a_lam_k1, a_lam_q2, a_lam_k2)):
                load(lam_in[:, j, :], g[0].partition_broadcast(P), params_loaded)
            load_wout(0)
            for i in range(LAYERS):
                load(b_rt[:, i, 0:N_GROUPS], moe_b_group[i].partition_broadcast(P), router_loaded)
                load(b_rt[:, i, N_GROUPS:NR], moe_b_router[i].partition_broadcast(P), router_loaded)
                for w, c, n in ((moe_w_group, 0, N_GROUPS), (moe_w_router, N_GROUPS, N_EXPERTS)):
                    for h in range(2):
                        load(w_rt[:, i, SUB * h:SUB * (h + 1), c:c + n], rows(w[i])[h],
                             router_loaded)
            sp.wait_ge(forget_zeroed, 2)
            for g in range(3):
                load(b_f[32 * g:32 * g + C_HEADS, :], c_b_f[0].rearrange("(p a) -> p a", a=1),
                     forget_loaded)
                for h in range(2):
                    load(wf3[:, SUB * h:SUB * (h + 1), 32 * g:32 * g + C_HEADS],
                         rows(c_w_in[0])[h, :, :, 3 * D:3 * D + C_HEADS], forget_loaded)
            for layer in range(LAYERS):
                s = layers[layer]
                for u in range(UNITS):
                    sp.wait_ge(s.proj_psum, 2 * u + 2)
                    load_unit(layer, u, 0)
                if layer + 1 < LAYERS:
                    sp.wait_ge(s.out_psum, 4)
                    load_wout(layer + 1)
                sp.wait_ge(s.slots_ready, 1)
                turns = sp.value_load(n_turns[0:1, layer:layer + 1], min_val=N_EXPERTS,
                                      max_val=ROUNDS * N_EXPERTS)
                with sp.Fori(1, turns) as v:
                    for u in range(UNITS):
                        sp.wait_ge(s.unit_used[u], v)
                        sp.nop(nofuse=True)
                        load_unit(layer, u, v & (N_EXPERTS - 1))
                if layer + 1 < LAYERS:
                    for u in range(UNITS):
                        sp.wait_ge(s.unit_used[u], turns)
                        load_win(layer + 1, u)
            for q in range(4):
                sp.wait_ge(layers[-1].moe_out, q + 1)
                t, h = q // 2, q % 2
                sp.dma_start(out[0, t * P:(t + 1) * P, HALF * h:HALF * (h + 1)],
                             x_sb[:, t, HALF * h:HALF * (h + 1)]).then_inc(out_stored, 16)
            sp.wait_ge(out_stored, 64)

        @block.gpsimd
        def _(pool):
            steps = [0]

            def own(ins):
                steps[0] += 1
                ins.then_inc(pool_step, 1)
                pool.wait_ge(pool_step, steps[0])

            made_before = [0]

            def made(ins):
                made_before[0] += 1
                ins.then_inc(consts_made, 1)
                pool.wait_ge(consts_made, made_before[0])

            def select(out_ap, in_ap, pattern, cmp, base, mult, fill):
                return pool.affine_select(out=out_ap, in_=in_ap, pattern=pattern, compare_op=cmp,
                                          fill=fill, base=base, channel_multiplier=mult)

            own(pool.memset(ident[:, :], 0.0))
            made(select(ident[:, :], ident[:, :], [[-1, P]], ALU.not_equal, 0, 1, 1.0
                   ))
            own(pool.memset(ident_bf[:, :], 0.0))
            made(select(ident_bf[:, :], ident_bf[:, :], [[-1, P]], ALU.not_equal, 0, 1, 1.0
                   ))
            own(pool.memset(slide[:, :], 0.0))
            made(pool.memset(slide[0:HD, 30:31], 1.0))
            made(pool.memset(slide[HD:P, 31:32], 1.0))
            own(pool.memset(slide_all[:, :], 0.0))
            made(pool.memset(slide_all[:, 31:32], 1.0))
            made(pool.iota(dist[:, 0:P], [[-1, P]], base=0, channel_multiplier=1,
                      allow_small_or_imprecise_dtypes=True))
            made(pool.iota(dist[:, P:SW], [[-1, T]], base=P, channel_multiplier=1,
                      allow_small_or_imprecise_dtypes=True))
            own(pool.memset(mask_causal[:, :], 0.0))
            made(select(mask_causal[:, 0:P], mask_causal[:, 0:P], [[-1, P]], ALU.is_ge, 0, 1, NEG
                   ))
            made(select(mask_causal[:, 2 * P:SW], mask_causal[:, 2 * P:SW], [[-1, P]], ALU.is_ge, 0, 1,
                   NEG))
            own(pool.memset(mask_strict[:, :], 0.0))
            made(select(mask_strict[:, 0:P], mask_strict[:, 0:P], [[1, P]], ALU.is_gt, 0, -1, NEG
                   ))
            made(select(mask_strict[:, 2 * P:SW], mask_strict[:, 2 * P:SW], [[1, P]], ALU.is_gt, 0, -1,
                   NEG))
            own(pool.memset(neg_ones[:, :], -1.0))
            made(select(neg_from[:, :], neg_ones[:, :], [[-1, P]], ALU.is_ge, 0, 1, 0.0
                   ))
            own(pool.memset(ones_bf[:, :], 1.0))
            made(select(before_bf[:, :], ones_bf[:, :], [[1, P]], ALU.is_gt, 0, -1, 0.0
                   ))
            made(select(strict[:, :], ones_bf[:, :], [[1, P]], ALU.is_gt, 0, -1, 0.0
                   ))
            made(pool.iota(slot_id[:, :, :], [[0, 2], [1, SLOTS]], base=0, channel_multiplier=0,
                      allow_small_or_imprecise_dtypes=True))
            own(pool.memset(sel_head[:, :], 0.0))
            for g in range(3):
                part = sel_head[32 * g:32 * (g + 1), :]
                last = select(part, part, [[-1, C_HEADS]], ALU.not_equal, 0, 1, 1.0)
                own(last)
            made(pool.iota(desc4[:, :], [[-1, 4]], base=4, channel_multiplier=0,
                      allow_small_or_imprecise_dtypes=True))

        @block.scalar
        def _(act):
            act.preload_act_table_set("natural_log_exp_and_others")

            steps = [0]

            def own(ins):
                steps[0] += 1
                ins.then_inc(act_step, 1)
                act.wait_ge(act_step, steps[0])

            def sum_squares(s, t):
                act.activation(qk_flat[:, D * t:D * (t + 1)], x_sb[:, t, :], ACT.Square,
                               accum_out=ssq[:, t:t + 1]).then_inc(s.squares_summed, 1)

            def root_guess(s, n, r, c):
                act.wait_ge(s.rsq_in, n)
                own(act.activation(root_ln[0:r, 0:c], root_x[0:r, 0:c], ACT.Ln))
                act.activation(root_y[0:r, 0:c], root_ln[0:r, 0:c], ACT.Exp, scale=-0.5
                               ).then_inc(s.rsq_guess, 1)

            def slots_free(layer, j):
                s = layers[layer]
                if j >= 2 and is_b(layer, j - 2):
                    act.wait_ge(s.o_psum, j - 1)
                elif j >= 2:
                    act.wait_ge(s.t_psum, maps_before(layer, j - 1))

            def exponentials(layer, j):
                s = layers[layer]
                for m in range(2):
                    slot = 2 * (j % 2) + m
                    if is_b(layer, j):
                        act.wait_ge(s.scores_psum, 2 * j + m + 1)
                        if j >= 2 and is_b(layer, j - 2):
                            act.wait_ge(s.t_psum, maps_before(layer, j - 1))
                        elif j >= 2:
                            act.wait_ge(s.o_psum, j - 1)
                        z = pT[:, slot, :]
                        own(act.activation(z, bank[2 + slot][:, 0:SW], ACT.Abs))
                        own(act.activation(z, z, ACT.Exp, scale=-1.0))
                        act.activation(z, z, ACT.Ln, bias=1.0).then_inc(s.b_ln, 1)
                        continue
                    act.wait_ge(s.max_ready, 2 * j + m + 1)
                    if m == 0:
                        slots_free(layer, j)
                    b = bank[2 + slot]
                    for i in range(NT):
                        k = 2 * m + i
                        last = act.activation(probs[:, slot, map_cols(i)], b[:, map_cols(i)], ACT.Exp,
                                              bias=nmax[:, j % 2, k:k + 1],
                                              accum_out=rsum[:, j % 2, k:k + 1])
                    last.then_inc(s.exp_done, 1)

            def second(layer, j):
                s = layers[layer]
                if is_b(layer, j):
                    slots_free(layer, j)
                    for m in range(2):
                        slot = 2 * (j % 2) + m
                        act.wait_ge(s.t_psum, maps_before(layer, j) + m + 1)
                        act.activation(probs[:, slot, :], bank[2 + slot][:, 0:SW], ACT.Exp
                                       ).then_inc(s.exp_done, 1)
                    return
                act.wait_ge(s.t_psum, maps_before(layer, j) + 1)
                if j >= 2:
                    act.wait_ge(s.o_psum, j - 1)
                act.activation(pT[:, 2 * (j % 2), :], bank[0][:, 0:SW], ACT.Copy).then_inc(s.pt_act, 1)

            def output(layer, j):
                s = layers[layer]
                act.wait_ge(s.o_psum, j + 1)
                act.activation(oT[:, j, :], O_BANK[:, 0:T], ACT.Copy).then_inc(s.o_ready, 1)
                if layer == 0 and j < A_HEADS:
                    act.wait_ge(s.o_ready, j + 1)
                    act.activation(o_squares[:, j, :], oT[:, j, :], ACT.Square
                                   ).then_inc(s.o_squared, 1)

            for layer in range(LAYERS):
                s = layers[layer]
                for t in range(NT):
                    if layer == 0:
                        act.wait_ge(x_loaded, 16 * NT)
                    else:
                        act.wait_ge(layers[layer - 1].moe_out, 4)
                    sum_squares(s, t)
                root_guess(s, roots_before(layer, "mix"), P, NT)
                done = 0
                for j in range(STEPS):
                    kind, first = PLAN[layer][j // 2]
                    if kind == "norm":
                        act.wait_ge(s.proj_out, j + 1)
                        if done >= 2:
                            act.wait_ge(s.sumsq_psum, done - 1)
                        c = first + 2 * (j % 2)
                        act.activation(squares[done % 2],
                                       qkT[:, c:c + 2, :].rearrange("p a b -> p (a b)"), ACT.Square
                                       ).then_inc(s.squared, 1)
                        done += 1
                root_guess(s, roots_before(layer, "qk"), 32, T)
                if layer == 0:
                    act.wait_ge(lam_sums, 1)
                    act.activation(lam_s[:, 2:4], lam_s[:, 0:2], ACT.Exp).then_inc(lam_exp, 1)
                if layer == 1:
                    act.wait_ge(s.forget_abs, 1)
                    own(act.activation(forget[2], forget[1], ACT.Exp, scale=-1.0))
                    act.activation(forget[3], forget[2], ACT.Ln, bias=1.0).then_inc(s.forget_ln, 1)
                for i in range(JOBS + 2):
                    if layer == 0 and i == SUBLN + 3:
                        root_guess(s, roots_before(layer, "sub"), 32, T)
                    if i < JOBS:
                        exponentials(layer, i)
                    if 1 <= i < JOBS + 1:
                        second(layer, i - 1)
                    if i >= 2:
                        output(layer, i - 2)
                for t in range(NT):
                    act.wait_ge(s.x_mixed, 2 * (t + 1))
                    sum_squares(s, t)
                root_guess(s, roots_before(layer, "ffn"), P, NT)
                act.wait_ge(s.rt_shift, 1)
                act.activation(rt[:, 2], rt[:, 1], ACT.Exp).then_inc(s.rt_exp, 1)
                act.wait_ge(s.rt_gap, 1)
                act.activation(rt[:, 12, :, 1:2], rt[:, 12, :, 0:1], ACT.Exp).then_inc(s.rt_gap_exp, 1)
                act.wait_ge(s.slots_ready, 1)
                turns = act.value_load(n_turns[0:1, layer:layer + 1], min_val=N_EXPERTS,
                                       max_val=ROUNDS * N_EXPERTS)
                with act.Fori(0, turns) as v:
                    act.wait_ge(s.unit_used[1], v + 1)
                    act.activation(gate_e, GATE[:, :], ACT.Exp, scale=-1.0).then_inc(s.gate_exp, 1)
                    act.wait_ge(s.giveT_psum, v + 1)
                    act.activation(giveT, GATE[:, 0:T], ACT.Copy).then_inc(s.giveT_ready, 1)
                    act.wait_ge(s.unit_used[5], v + 1)
                    act.activation(y_sb, Y[:, :], ACT.Copy).then_inc(s.y_ready, 1)

        @block.vector
        def _(dve):
            steps = [0]

            def own(ins):
                steps[0] += 1
                ins.then_inc(dve_step, 1)
                dve.wait_ge(dve_step, steps[0])

            ts, tt, stt = nc.vector.tensor_scalar, nc.vector.tensor_tensor, nc.vector.scalar_tensor_tensor

            def root(s, n, src, r, c, count):
                xs, ys, tmp = root_x[0:r, 0:c], root_y[0:r, 0:c], root_t[0:r, 0:c]
                ts(xs, src, 1.0 / count, EPS, ALU.mult, ALU.add).then_inc(s.rsq_in, 1)
                dve.wait_ge(s.rsq_guess, n)
                own(stt(tmp, xs, -0.5, ys, ALU.mult, ALU.mult))
                own(tt(tmp, tmp, ys, ALU.mult))
                return stt(ys, tmp, 1.5, ys, ALU.add, ALU.mult)

            def normalise(layer, which, table):
                s = layers[layer]
                n = 0 if which == "mix" else 1
                dve.wait_ge(s.squares_summed, NT * (n + 1))
                own(root(s, roots_before(layer, which), ssq[:, :], P, NT, D))
                for t in range(NT):
                    ts(hn[:, t, :], x_sb[:, t, :], root_y[:, t:t + 1], None, ALU.mult
                       ).then_inc(s.hn_ready, 1)
                if layer == 0 and n == 0:
                    dve.wait_ge(gains_loaded, GAINS)
                for g in range(4):
                    t, h = g // 2, g % 2
                    dve.wait_ge(s.ht_psum, 4 * n + g + 1)
                    tt(hT[:, SUB * h:SUB * (h + 1), P * t:P * (t + 1)],
                       bank[2 + g][:, :].rearrange("p (c t) -> p c t", c=SUB),
                       gains(table, layer, h, P), ALU.mult).then_inc(s.ht_ready, 1)

            def make_tables():
                dve.wait_ge(params_loaded, PARAMS)
                dve.wait_ge(consts_made, CONSTS)
                own(ts(g_qk[:, :, 0:1], g_qk[:, :, 0:1], SCALE, None, ALU.mult))
                own(ts(g_sub[:, :], g_sub[:, :], 1.0 - LAM_INIT, None, ALU.mult))
                for m in range(2):
                    last = tt(lam_prod[:, m, :], lam_in[:, 2 * m, :], lam_in[:, 2 * m + 1, :], ALU.mult)
                own(last)
                nc.vector.tensor_reduce(lam_s[:, 0:2], lam_prod, AX_X, ALU.add).then_inc(lam_sums, 1)
                for h in range(A_HEADS):
                    slope = 2.0 ** (-8.0 * (h + 1) / A_HEADS)
                    stt(bias_a[:, h, :], dist, -slope, mask_causal[:, :], ALU.mult, ALU.add
                        ).then_inc(tables_made, 1)
                dve.wait_ge(lam_exp, 1)
                own(tt(neg_lam[:, :], lam_s[:, 3:4], lam_s[:, 2:3], ALU.subtract))
                own(ts(neg_lam[:, :], neg_lam[:, :], -LAM_INIT, None, ALU.add))

            def first(layer, j):
                s = layers[layer]
                if is_b(layer, j):
                    return
                for m in range(2):
                    slot = 2 * (j % 2) + m
                    dve.wait_ge(s.scores_psum, 2 * j + m + 1)
                    for i in range(NT):
                        k = 2 * m + i
                        last = nc.vector.tensor_reduce(nmax[:, j % 2, k:k + 1],
                                                       bank[2 + slot][:, map_cols(i)], AX_X, ALU.max,
                                                       negate=True)
                    last.then_inc(s.max_ready, 1)

            def second(layer, j):
                s = layers[layer]
                slot = 2 * (j % 2)
                if is_b(layer, j):
                    for m in range(2):
                        dve.wait_ge(s.b_ln, 2 * (j - A_HEADS) + m + 1)
                        z = pT[:, slot + m, :]
                        own(stt(z, bank[2 + slot + m][:, 0:SW], 0.0, z, ALU.max, ALU.add))
                        diagonal = z.rearrange("p (b k) -> p b k", b=3)[:, 0:3:2, :]
                        tt(diagonal, diagonal,
                           strict[:, :].rearrange("p (a k) -> p a k", a=1).to_broadcast([P, 2, P]),
                           ALU.mult).then_inc(s.p_ready, 1)
                    return
                dve.wait_ge(s.exp_done, 2 * j + 2)
                own(nc.vector.reciprocal(rinv[:, j % 2, :], rsum[:, j % 2, :]))
                if layer == 0:
                    own(ts(rinv[:, j % 2, 2:4], rinv[:, j % 2, 2:4], neg_lam[:, :], None, ALU.mult))
                    for i in range(NT):
                        p1 = probs[:, slot, map_cols(i)]
                        last = ts(p1, p1, rinv[:, j % 2, i:i + 1], None, ALU.mult)
                    own(last)
                    for i in range(NT):
                        p1, p2 = probs[:, slot, map_cols(i)], probs[:, slot + 1, map_cols(i)]
                        last = stt(p1, p2, rinv[:, j % 2, 2 + i:3 + i], p1, ALU.mult, ALU.add)
                    last.then_inc(s.p_ready, 1)
                    return
                for m in range(2):
                    for i in range(NT):
                        k = 2 * m + i
                        p1 = probs[:, slot + m, map_cols(i)]
                        last = ts(p1, p1, rinv[:, j % 2, k:k + 1], None, ALU.mult)
                    last.then_inc(s.p_ready, 1)

            def third(layer, j):
                s = layers[layer]
                if layer == 0:
                    return
                dve.wait_ge(s.t_psum, maps_before(layer, j) + 2)
                if j >= 2:
                    dve.wait_ge(s.o_psum, j - 1)
                nc.vector.tensor_copy(pT[:, 2 * (j % 2) + 1, :], bank[1][:, 0:SW]).then_inc(s.pt_dve, 1)

            def forget_gate(s):
                z, az, _, ln1, lf = forget
                dve.wait_ge(s.forget_psum, 1)
                dve.wait_ge(forget_loaded, FORGET)
                own(ts(z, SUM_BANK[0:96, 0:T], b_f[:, :], None, ALU.add))
                stt(az, z, -1.0, z, ALU.mult, ALU.max).then_inc(s.forget_abs, 1)
                dve.wait_ge(s.forget_ln, 1)
                own(stt(lf, z, 0.0, ln1, ALU.min, ALU.subtract))
                own(nc.vector.tensor_tensor_scan(z, ones_bf[0:96, 0:1].to_broadcast([96, T]), lf, 0.0,
                                                 ALU.mult, ALU.add))
                own(nc.vector.tensor_copy(cum[0][:, :], z))
                own(tt(z, z, cum[0][:, :], ALU.subtract))
                own(nc.vector.tensor_copy(cum[1][:, :], z))
                own(tt(z, z, cum[1][:, :], ALU.subtract))
                own(nc.vector.tensor_copy(cum[2][:, :], z))
                for g in range(3):
                    r = slice(32 * g, 32 * (g + 1))
                    nc.vector.tensor_copy(cum_pos[r, :], cum[g][r, :])
                    last = ts(cum_neg[r, :], cum[g][r, :], -1.0, None, ALU.mult)
                last.then_inc(s.cum_ready, 1)

            def first_of(row_max, values, out_ap):
                own(tt(rt[:, 3], values, spread(row_max, [P, NT, 4]), ALU.is_equal))
                d = desc4[:, :].rearrange("p (a k) -> p a k", a=1).to_broadcast([P, NT, 4])
                own(tt(rt[:, 4], rt[:, 3], d, ALU.mult))
                own(nc.vector.tensor_reduce(rt[:, 5, :, 0:1], rt[:, 4], AX_X, ALU.max))
                own(tt(out_ap, d, spread(rt[:, 5, :, 0:1], [P, NT, 4]), ALU.is_equal))

            def route(layer):
                s = layers[layer]
                reduce = nc.vector.tensor_reduce
                dve.wait_ge(s.logits_psum, 1)
                own(tt(lg[:, :, :], MISC[:, 0:NT * NR].rearrange("p (t n) -> p t n", t=NT),
                       b_rt[:, layer:layer + 1, :].to_broadcast([P, NT, NR]), ALU.add))
                groups = lg[:, :, 0:N_GROUPS]
                experts = lg[:, :, N_GROUPS:NR].rearrange("p t (g e) -> p t g e", g=N_GROUPS)
                own(reduce(rt[:, 0, :, 0:1], groups, AX_X, ALU.max))
                tt(rt[:, 1], groups, spread(rt[:, 0, :, 0:1], [P, NT, 4]), ALU.subtract
                   ).then_inc(s.rt_shift, 1)
                first_of(rt[:, 0, :, 0:1], groups, rt[:, 6])
                in_group = rt[:, 6].rearrange("p t (g a) -> p t g a", a=1).to_broadcast(
                    [P, NT, N_GROUPS, PER_GROUP])
                for t in range(NT):
                    last = tt(picked[:, t], experts[:, t], in_group[:, t], ALU.mult)
                own(last)
                own(reduce(rt[:, 7], picked[:, :, :, :].rearrange("p t g e -> p t e g"), AX_X, ALU.add))
                own(reduce(rt[:, 8, :, 0:1], rt[:, 7], AX_X, ALU.max))
                first_of(rt[:, 8, :, 0:1], rt[:, 7], rt[:, 9])
                own(stt(rt[:, 10], rt[:, 9], NEG, rt[:, 7], ALU.mult, ALU.add))
                own(reduce(rt[:, 8, :, 1:2], rt[:, 10], AX_X, ALU.max))
                first_of(rt[:, 8, :, 1:2], rt[:, 10], rt[:, 11])
                tt(rt[:, 12, :, 0:1], rt[:, 8, :, 1:2], rt[:, 8, :, 0:1], ALU.subtract
                   ).then_inc(s.rt_gap, 1)
                dve.wait_ge(s.rt_exp, 1)
                own(reduce(rt[:, 13, :, 0:1], rt[:, 2], AX_X, ALU.add))
                dve.wait_ge(s.rt_gap_exp, 1)
                own(stt(rt[:, 13, :, 1:2], rt[:, 12, :, 1:2], 1.0, rt[:, 13, :, 0:1], ALU.add, ALU.mult))
                own(nc.vector.reciprocal(rt[:, 13, :, 2:3], rt[:, 13, :, 1:2]))
                own(tt(rt[:, 13, :, 3:4], rt[:, 13, :, 2:3], rt[:, 12, :, 1:2], ALU.mult))
                own(tt(rt[:, 3], rt[:, 9], spread(rt[:, 13, :, 2:3], [P, NT, 4]), ALU.mult))
                own(tt(rt[:, 4], rt[:, 11], spread(rt[:, 13, :, 3:4], [P, NT, 4]), ALU.mult))
                own(tt(rt[:, 3], rt[:, 3], rt[:, 4], ALU.add))
                own(tt(rt[:, 4], rt[:, 9], rt[:, 11], ALU.add))
                for t in range(NT):
                    def over_groups(value):
                        return value[:, t:t + 1, :].to_broadcast([P, N_GROUPS, PER_GROUP])
                    tt(chosen_f[:, t].rearrange("p (g e) -> p g e", g=N_GROUPS), in_group[:, t],
                       over_groups(rt[:, 4]), ALU.mult)
                    last = tt(weight_of[:, t, 0:N_EXPERTS].rearrange("p (g e) -> p g e", g=N_GROUPS),
                              in_group[:, t], over_groups(rt[:, 3]), ALU.mult)
                own(last)
                nc.vector.tensor_copy(chosen_bf[:, :, :], chosen_f[:, :, :]).then_inc(s.chosen, 1)
                for r in range(1, ROUNDS):
                    nc.vector.tensor_copy(weight_of[:, :, N_EXPERTS * r:N_EXPERTS * (r + 1)],
                                          weight_of[:, :, 0:N_EXPERTS])
                nc.vector.tensor_copy(weight_of[:, :, ROUNDS * N_EXPERTS:], weight_of[:, :, 0:1])
                dve.wait_ge(s.rank_psum, 1)
                own(stt(picked[:, :, :, :].rearrange("p t g e -> p t (g e)"),
                        Y[:, 0:NT * N_EXPERTS].rearrange("p (t e) -> p t e", t=NT), 1.0,
                        chosen_f[:, :, :], ALU.add, ALU.mult))
                for r in range(ROUNDS):
                    last = ts(slot_of[:, :, N_EXPERTS * r:N_EXPERTS * (r + 1)],
                              picked[:, :, :, :].rearrange("p t g e -> p t (g e)"),
                              -1.0 - SLOTS * r, None, ALU.add)
                own(last)
                own(reduce(most[:, 0:1], Y[:, NT * N_EXPERTS:(NT + 1) * N_EXPERTS], AX_X, ALU.max))
                own(ts(most[:, 1:2], most[:, 0:1], float(SLOTS), float((ROUNDS - 1) * N_EXPERTS),
                       ALU.is_gt, ALU.mult))
                ts(n_turns[:, layer:layer + 1], most[:, 1:2], float(N_EXPERTS), None, ALU.add
                   ).then_inc(s.slots_ready, 1)

            own(nc.vector.memset(wf3[:, :, :], 0.0))
            nc.vector.memset(b_f[:, :], 0.0).then_inc(forget_zeroed, 1)
            nc.vector.memset(slot_of[:, :, ROUNDS * N_EXPERTS:], -1.0).then_inc(forget_zeroed, 1)

            for layer in range(LAYERS):
                s = layers[layer]
                normalise(layer, "mix", gain_mix)
                spreads = norm_steps[layer]
                applied = 0
                for j in range(STEPS):
                    kind, at = PLAN[layer][j // 2]
                    dve.wait_ge(s.proj_psum, j + 1)
                    if kind == "v":
                        dst = v_sb[:, j % 2, at:at + COLS]
                    else:
                        c = at + 2 * (j % 2)
                        dst = qkT[:, c:c + 2, :].rearrange("p a b -> p (a b)")
                    if kind == "scaled":
                        ts(dst, bank[j % 2][:, :], SCALE, None, ALU.mult).then_inc(s.proj_out, 1)
                    else:
                        nc.vector.tensor_copy(dst, bank[j % 2][:, :]).then_inc(s.proj_out, 1)
                    if j == norm_steps[layer]:
                        dve.wait_ge(s.sumsq_psum, norm_steps[layer])
                        root(s, roots_before(layer, "qk"), SUM_BANK[0:32, 0:T], 32, T, HD
                             ).then_inc(s.root_done, 1)
                        if layer == 0:
                            make_tables()
                    first_spread = STEPS - 2
                    if j >= first_spread:
                        for g in range(applied, min(spreads, applied + 4)):
                            dve.wait_ge(s.root_spread, g + 1)
                            is_k = 1 if 2 * g >= spreads else 0
                            q2 = qkT[:, 2 * g:2 * g + 2, :].rearrange("p a b -> p (a b)")
                            stt(q2, q2, g_qk[:, layer, is_k:is_k + 1], bank[2 + g % 4][:, :],
                                ALU.mult, ALU.mult).then_inc(s.root_applied, 1)
                            applied = g + 1
                if layer == 1:
                    forget_gate(s)
                for i in range(JOBS + 2):
                    if layer == 0 and i == SUBLN + 3:
                        dve.wait_ge(s.o_sumsq, SUBLN)
                        root(s, roots_before(layer, "sub"), SUM_BANK[0:32, 0:T], 32, T, P
                             ).then_inc(s.root_done, 1)
                    b_now = i < JOBS and is_b(layer, i)
                    if i < JOBS and not b_now:
                        first(layer, i)
                    if 1 <= i < JOBS + 1:
                        second(layer, i - 1)
                        third(layer, i - 1)
                    if b_now:
                        first(layer, i)
                if layer == 0:
                    for g in range(2):
                        dve.wait_ge(s.sub_spread, g + 1)
                        o2 = oT[:, 2 * g:2 * g + 2, :].rearrange("p a b -> p (a b)")
                        stt(o2, o2, g_sub[:, :], bank[g][:, :], ALU.mult, ALU.mult
                            ).then_inc(s.sub_applied, 1)
                for q in range(4):
                    dve.wait_ge(s.out_psum, q + 1)
                    xq = x_sb[:, q // 2, HALF * (q % 2):HALF * (q % 2 + 1)]
                    tt(xq, bank[2 + q][:, :], xq, ALU.add).then_inc(s.x_mixed, 1)
                if layer == 0:
                    dve.wait_ge(router_loaded, ROUTER)
                normalise(layer, "ffn", gain_ffn)
                route(layer)

                def make_take(n):
                    for t in range(NT):
                        last = ts(take[:, t, :], slot_id[:, :, :].rearrange("p a b -> p (a b)"),
                                  slot_of[:, t, bass.ds(n, 1)], None, ALU.is_equal)
                    last.then_inc(s.take_ready, 1)

                def make_give(n):
                    for t in range(NT):
                        last = ts(give[:, t, :], slot_id[:, :, :].rearrange("p a b -> p (a b)"),
                                  slot_of[:, t, bass.ds(n, 1)], weight_of[:, t, bass.ds(n, 1)],
                                  ALU.is_equal, ALU.mult)
                    last.then_inc(s.give_ready, 1)

                def leave_gathered():
                    for h, b in enumerate((MISC, Y)):
                        last = tt(xT[:, SUB * h:SUB * (h + 1), :],
                           b[:, :].rearrange("p (c t) -> p c t", c=SUB)[:, :, 0:SLOTS],
                           gains(gain_ffn, layer, h, SLOTS), ALU.mult)
                    last.then_inc(s.xt_ready, 1)

                dve.wait_ge(s.slots_ready, 1)
                turns = dve.value_load(n_turns[0:1, layer:layer + 1], min_val=N_EXPERTS,
                                       max_val=ROUNDS * N_EXPERTS)
                make_take(0)
                make_give(0)
                dve.wait_ge(s.gathered, 1)
                leave_gathered()
                with dve.Fori(0, turns) as v:
                    make_take(v + 1)
                    dve.wait_ge(s.gate_exp, v + 1)
                    ts(sig, gate_e, 1.0, None, ALU.add).then_inc(s.gate_plus, 1)
                    dve.wait_ge(s.gate_plus, v + 1)
                    nc.vector.reciprocal(sig, sig).then_inc(s.gate_inv, 1)
                    dve.wait_ge(s.gate_inv, v + 1)
                    tt(sig, GATE[:, :], sig, ALU.mult).then_inc(s.gate_act, 1)
                    dve.wait_ge(s.gate_act, v + 1)
                    dve.wait_ge(s.unit_used[3], v + 1)
                    tt(hid, UP[:, :], sig, ALU.mult).then_inc(s.hid_ready, 1)
                    dve.wait_ge(s.gathered, v + 2)
                    leave_gathered()
                    dve.wait_ge(s.giveT_psum, v + 1)
                    make_give(v + 1)
                    dve.wait_ge(s.hidT_psum, v + 1)
                    nc.vector.tensor_copy(hidT, MISC[:, :].rearrange("p (s t) -> p s t", s=SUB)
                                          ).then_inc(s.hidT_ready, 1)
                dve.wait_ge(s.scattered, turns)
                for q in range(4):
                    nc.vector.tensor_copy(x_sb[:, q // 2, HALF * (q % 2):HALF * (q % 2 + 1)],
                                          ACC[q][:, :]).then_inc(s.moe_out, 1)

        @block.tensor
        def _(pe):
            mm = nc.tensor.matmul

            def tokens_across(s, n):
                for g in range(4):
                    t, h = g // 2, g % 2
                    pe.wait_ge(s.hn_ready, NT * n + t + 1)
                    for c in range(SUB):
                        last = nc.tensor.transpose(bank[2 + g][:, P * c:P * (c + 1)],
                                                   by_chunk(t, h, c), ident[:, :])
                    last.then_inc(s.ht_psum, 1)

            def scores(layer, j):
                s = layers[layer]
                banks = [bank[2 + 2 * (j % 2) + m] for m in range(2)]
                if layer == 0:
                    cq, ck = (j, A_HEADS + j) if j < A_HEADS else (4 + j, 8 + j)
                else:
                    cq, ck = j, JOBS + j
                if j >= 2:
                    pe.wait_ge(s.exp_done, 2 * (j - 1))
                if is_b(layer, j):
                    for m in range(2):
                        r = slice(HD * m, HD * (m + 1))
                        mm(banks[m][:, 0:T], qkT[r, ck, 0:P], qkT[r, cq, 0:T], start=True,
                           stop=False, skip_group_check=True)
                    for m in range(2):
                        r = slice(HD * m, HD * (m + 1))
                        mm(banks[m][:, T:SW], qkT[r, ck, P:T], qkT[r, cq, P:T], start=False,
                           stop=False, skip_group_check=True).then_inc(s.scores_psum, 1)
                    return
                for m in range(2):
                    if layer == 0:
                        mm(banks[m][:, 0:SW], ident_bf[:, :], bias_a[:, j, :], start=True, stop=False,
                           skip_group_check=True)
                        continue
                    mm(banks[m][:, 0:SW], ident_bf[:, :], mask_causal[:, :], start=True, stop=False,
                       skip_group_check=True)
                    head = sel_head[:, 2 * j + m:2 * j + m + 1]
                    for i in range(NT):
                        keys = P * (i + 1)
                        mm(banks[m][:, map_cols(i)], head.to_broadcast([96, P]), cum_neg[:, 0:keys],
                           start=False, stop=False, skip_group_check=True)
                        mm(banks[m][:, map_cols(i)], cum_pos[:, P * i:P * (i + 1)],
                           head.to_broadcast([96, keys]), start=False, stop=False,
                           skip_group_check=True)
                for i in range(NT):
                    for m in range(2):
                        r = slice(HD * m, HD * (m + 1))
                        last = mm(banks[m][:, map_cols(i)], qkT[r, cq, P * i:P * (i + 1)],
                                  qkT[r, ck, 0:P * (i + 1)], start=False, stop=(i == NT - 1),
                                  skip_group_check=True)
                        if i == NT - 1:
                            last.then_inc(s.scores_psum, 1)

            def across(layer, j):
                s = layers[layer]
                n = maps_before(layer, j)
                for m in range(maps_before(layer, j + 1) - n):
                    slot = 2 * (j % 2) + m
                    pe.wait_ge(s.p_ready, n + m + 1)
                    if is_b(layer, j):
                        b, soft = bank[2 + slot], pT[:, slot, :]
                        mm(b[:, 0:SW], neg_from[:, :], soft, start=False, stop=False,
                           skip_group_check=True)
                        mm(b[:, P:T], neg_ones[:, :], soft[:, T:SW], start=False, stop=False,
                           skip_group_check=True)
                        mm(b[:, 0:SW], ident_bf[:, :], mask_strict[:, :], start=False, stop=True,
                           skip_group_check=True).then_inc(s.t_psum, 1)
                        continue
                    if j >= 1:
                        pe.wait_ge(s.pt_dve if m else s.pt_act, j)
                    for k in range(3):
                        last = nc.tensor.transpose(bank[m][:, P * k:P * (k + 1)],
                                                   probs[:, slot, P * k:P * (k + 1)], ident[:, :])
                    last.then_inc(s.t_psum, 1)

            def weighted_values(layer, j):
                s = layers[layer]
                if is_b(layer, j):
                    pe.wait_ge(s.exp_done, 2 * j + 2)
                else:
                    pe.wait_ge(s.pt_act, j + 1)
                    if layer == 1:
                        pe.wait_ge(s.pt_dve, j + 1)
                if j >= 1:
                    pe.wait_ge(s.o_ready, j)
                source = probs if is_b(layer, j) else pT
                slot = 2 * (j % 2)
                if layer == 0 and j < A_HEADS:
                    heads = [(slice(0, P), P * j, P)]
                else:
                    at = HALF + P * (j - A_HEADS) if layer == 0 else P * j
                    heads = [(slice(HD * m, HD * (m + 1)), at + HD * m, HD) for m in range(2)]
                for k in range(NT):
                    for m, (r, col, n) in enumerate(heads):
                        w = source[:, slot + m, 0:T] if k == 0 else source[:, slot + m, T:SW]
                        last = mm(O_BANK[r, P * k:T], v_sb[:, k, col:col + n], w, start=(k == 0),
                                  stop=(k == NT - 1), skip_group_check=True)
                last.then_inc(s.o_psum, 1)

            def sub_sum(s, j):
                pe.wait_ge(s.o_squared, j + 1)
                mm(SUM_BANK[0:32, 0:T], slide_all[:, 31 - j:63 - j], o_squares[:, j, :],
                   start=(j == 0), stop=(j == SUBLN - 1)).then_inc(s.o_sumsq, 1)

            pe.wait_ge(consts_made, CONSTS)
            for layer in range(LAYERS):
                s = layers[layer]
                tokens_across(s, 0)
                pe.wait_ge(s.ht_ready, 4)
                normed, spreads = norm_steps[layer], 0

                def spread_roots(g0, g1):
                    for g in range(g0, g1):
                        if g >= 4:
                            pe.wait_ge(s.root_applied, g - 3)
                        for c in range(2):
                            for m in range(2):
                                k = 2 * (2 * g + c) + m
                                last = mm(bank[2 + g % 4][HD * m:HD * (m + 1), T * c:T * (c + 1)],
                                          ident[0:32, k:k + 1].to_broadcast([32, HD]),
                                          root_y[0:32, :], start=True, stop=True)
                        last.then_inc(s.root_spread, 1)

                for j in range(STEPS):
                    kind, at = PLAN[layer][j // 2]
                    u = j // 2
                    if j % 2 == 0:
                        pe.wait_ge(s.unit_loaded[u], WIN)
                    if j >= 2:
                        pe.wait_ge(s.proj_out, j - 1)
                    w = win_view(u)
                    if kind == "v":
                        t = j % 2
                        for c in range(NC):
                            last = mm(bank[j % 2][:, :], hT[:, c, P * t:P * (t + 1)], w[:, c, :],
                                      start=(c == 0), stop=(c == NC - 1))
                    else:
                        for half in range(2):
                            col = P * (2 * (j % 2) + half)
                            for c in range(NC):
                                last = mm(bank[j % 2][:, T * half:T * (half + 1)],
                                          w[:, c, col:col + P], hT[:, c, :], start=(c == 0),
                                          stop=(c == NC - 1))
                    last.then_inc(s.proj_psum, 1)
                    if 1 <= j <= normed:
                        pe.wait_ge(s.squared, j)
                        for half in range(2):
                            c = 2 * (j - 1) + half
                            last = mm(SUM_BANK[0:32, 0:T], slide[:, 30 - 2 * c:62 - 2 * c],
                                      squares[(j - 1) % 2][:, T * half:T * (half + 1)],
                                      start=(c == 0), stop=(c == 2 * normed - 1))
                        last.then_inc(s.sumsq_psum, 1)
                    if j >= STEPS - 2:
                        if j == STEPS - 2:
                            pe.wait_ge(s.root_done, 1)
                        upto = min(normed, spreads + 4)
                        spread_roots(spreads, upto)
                        spreads = upto
                if layer == 1:
                    pe.wait_ge(forget_loaded, FORGET)
                    for c in range(NC):
                        last = mm(SUM_BANK[0:96, 0:T], wf3[:, c, :], hT[:, c, :], start=(c == 0),
                                  stop=(c == NC - 1))
                    last.then_inc(s.forget_psum, 1)
                    pe.wait_ge(s.cum_ready, 1)
                else:
                    pe.wait_ge(tables_made, A_HEADS)
                pe.wait_ge(s.root_applied, normed)
                pe.wait_ge(s.proj_out, STEPS)
                for i in range(JOBS + 2):
                    if i < JOBS:
                        scores(layer, i)
                    if 1 <= i < JOBS + 1:
                        across(layer, i - 1)
                    if i >= 2:
                        weighted_values(layer, i - 2)
                    if layer == 0 and 3 <= i < 3 + SUBLN:
                        sub_sum(s, i - 3)
                if layer == 0:
                    pe.wait_ge(s.root_done, 2)
                    for g in range(2):
                        for c in range(2):
                            h = 2 * g + c
                            last = mm(bank[g][:, T * c:T * (c + 1)],
                                      ident[0:32, h:h + 1].to_broadcast([32, P]), root_y[0:32, :],
                                      start=True, stop=True)
                        last.then_inc(s.sub_spread, 1)
                    pe.wait_ge(s.sub_applied, 2)
                pe.wait_ge(wout_loaded, 16 * (layer + 1))
                pe.wait_ge(s.o_ready, JOBS)
                pe.wait_ge(s.exp_done, 2 * JOBS)
                for q in range(4):
                    t, h = q // 2, q % 2
                    for c in range(NC):
                        last = mm(bank[2 + q][:, :], oT[:, c, P * t:P * (t + 1)],
                                  w_out_sb[:, c, HALF * h:HALF * (h + 1)], start=(c == 0),
                                  stop=(c == NC - 1))
                    last.then_inc(s.out_psum, 1)

                tokens_across(s, 1)
                pe.wait_ge(s.ht_ready, 8)
                if layer == 0:
                    pe.wait_ge(router_loaded, ROUTER)
                for i in range(NT):
                    for c in range(NC):
                        last = mm(MISC[:, NR * i:NR * (i + 1)], hT[:, c, P * i:P * (i + 1)],
                                  w_rt[:, layer, c, :], start=(c == 0), stop=(c == NC - 1))
                last.then_inc(s.logits_psum, 1)
                for q in range(4):
                    last = mm(ACC[q][:, :], ident[:, :],
                              x_sb[:, q // 2, HALF * (q % 2):HALF * (q % 2 + 1)], start=True,
                              stop=False, skip_group_check=True)
                pe.wait_ge(s.chosen, 1)
                ranks = [(0, [(before_bf, 0)]), (1, [(ones_bf, 0), (before_bf, 1)]),
                         (2, [(ones_bf, 0), (ones_bf, 1)])]
                for k, terms in ranks:
                    for n, (w, t) in enumerate(terms):
                        last = mm(Y[:, N_EXPERTS * k:N_EXPERTS * (k + 1)], w[:, :], chosen_bf[:, t, :],
                                  start=(n == 0), stop=(n == len(terms) - 1))
                last.then_inc(s.rank_psum, 1)

                def gather():
                    for c in range(NC):
                        b = MISC if c < SUB else Y
                        k = c % SUB
                        for t in range(NT):
                            last = mm(b[:, P * k:P * (k + 1)], by_chunk(t, c // SUB, k),
                                      take[:, t, :], start=(t == 0), stop=(t == NT - 1))
                    last.then_inc(s.gathered, 1)

                def two_halves(b, left, units):
                    for h, u in enumerate(units):
                        pe.wait_ge(s.unit_loaded[u], v * 16 + (WIN + 16))
                        for k in range(SUB):
                            for half in range(2):
                                last = mm(b[SLOTS * half:SLOTS * (half + 1), :], left(h, k),
                                          expert_rhs(u, k, half), start=(h == 0 and k == 0),
                                          stop=(h == 1 and k == SUB - 1))
                        last.then_inc(s.unit_used[u], 1)
                    return last

                pe.wait_ge(s.slots_ready, 1)
                turns = pe.value_load(n_turns[0:1, layer:layer + 1], min_val=N_EXPERTS,
                                      max_val=ROUNDS * N_EXPERTS)
                pe.wait_ge(s.take_ready, 1)
                gather()
                with pe.Fori(0, turns) as v:
                    pe.wait_ge(s.xt_ready, v + 1)
                    two_halves(GATE, lambda h, k: xT[:, SUB * h + k, :], (0, 1))
                    two_halves(UP, lambda h, k: xT[:, SUB * h + k, :], (2, 3))
                    pe.wait_ge(s.take_ready, v + 2)
                    gather()
                    pe.wait_ge(s.give_ready, v + 1)
                    pe.wait_ge(s.gate_act, v + 1)
                    for t in range(NT):
                        last = nc.tensor.transpose(GATE[:, P * t:P * (t + 1)], give[:, t, :], ident[:, :])
                    last.then_inc(s.giveT_psum, 1)
                    pe.wait_ge(s.hid_ready, v + 1)
                    pe.wait_ge(s.xt_ready, v + 2)
                    for k in range(SUB):
                        part = hid.rearrange("p (q s) -> p s q", s=SUB)[:, k, :]
                        last = nc.tensor.transpose(MISC[:, P * k:P * (k + 1)], part, ident[:, :])
                    last.then_inc(s.hidT_psum, 1)
                    pe.wait_ge(s.hidT_ready, v + 1)
                    two_halves(Y, lambda h, k: hidT[:, k, SLOTS * h:SLOTS * (h + 1)], (4, 5))
                    pe.wait_ge(s.y_ready, v + 1)
                    pe.wait_ge(s.giveT_ready, v + 1)
                    for t in range(NT):
                        for half in range(2):
                            r = slice(SLOTS * half, SLOTS * (half + 1))
                            last = mm(ACC[2 * t + half][:, :], giveT[r, P * t:P * (t + 1)], y_sb[r, :],
                                      start=False, stop=False, skip_group_check=True)
                    last.then_inc(s.scattered, 1)


INPUTS = ["x", "norm_mix_g", "norm_ffn_g", "ab_w_in", "a_q_gain", "a_k_gain", "a_lam_q1", "a_lam_k1",
          "a_lam_q2", "a_lam_k2", "a_subln_g", "ab_w_out", "c_w_in", "c_b_f", "c_q_gain", "c_k_gain",
          "c_w_out", "moe_w_group", "moe_b_group", "moe_w_router", "moe_b_router", "moe_w_gate",
          "moe_w_up", "moe_w_down"]


def kernel(**inputs):
    import numpy as np
    from concourse import bacc
    from concourse.bass_utils import run_bass_kernel_spmd

    nc = bacc.Bacc("TRN2", target_bir_lowering=False, num_devices=1)
    arrays, args = {}, []
    for name in INPUTS:
        a = np.ascontiguousarray(inputs[name])
        arrays[f"in_{name}"] = a
        args.append(nc.dram_tensor(f"in_{name}", a.shape, mybir.dt.from_np(a.dtype),
                                   kind="ExternalInput").ap())
    args.append(nc.dram_tensor("out_0", (1, T, D), F32, kind="ExternalOutput").ap())
    trunk(nc, *args)
    r = run_bass_kernel_spmd(nc, [arrays], core_ids=[0])
    return r.results[0]["out_0"]
```

```python
import math
from contextlib import ExitStack

import concourse.bass as bass
from concourse import mybir

F32 = mybir.dt.float32
F32R = mybir.dt.float32r
BF16 = mybir.dt.bfloat16
I32 = mybir.dt.int32
ALU = mybir.AluOpType
ACT = mybir.ActivationFunctionType
AX_X = mybir.AxisListType.X

P = 128
D = 1024
T = 256
NT = T // P
NC = D // P
HALF = D // 2
SUB = NC // 2
COLS = 512
UNITS = 6
UNIT = SUB * D
HD = 64
A_HEADS, B_HEADS, C_HEADS = 4, 8, 16
JOBS = 8
N_GROUPS, PER_GROUP = 4, 4
N_EXPERTS = N_GROUPS * PER_GROUP
NR = N_GROUPS + N_EXPERTS
RING = 8
QUAD = 4
LAPS = QUAD * UNITS // RING
SLOTS = 64
ROUNDS = T // SLOTS
EPS = 1e-6
NEG = -1e30
SW = 3 * P
LAYERS = 2
LAM_INIT = 0.8 - 0.6 * math.exp(-0.3 * 0)
STEPS = 2 * UNITS
SCALE = HD ** -0.5

EVEN_UNITS = [("norm", 0), ("norm", 4), ("v", 0), ("scaled", 8), ("plain", 12), ("v", HALF)]
ODD_UNITS = [("norm", 0), ("norm", 4), ("norm", 8), ("norm", 12), ("v", 0), ("v", HALF)]
PLAN = [EVEN_UNITS, ODD_UNITS]

class LayerSignals:

    def __init__(self, nc, ctx, layer):
        def sem(name):
            return ctx.enter_context(nc.semaphore(f"{name}_{layer}"))

        self.squares_summed = sem("squares_summed")
        self.rsq_in = sem("rsq_in")
        self.rsq_guess = sem("rsq_guess")
        self.hn_ready = sem("hn_ready")
        self.ht_psum = sem("ht_psum")
        self.ht_ready = sem("ht_ready")
        self.h_high = sem("h_high")
        self.h_low = sem("h_low")
        self.w_high = sem("w_high")
        self.w_low = sem("w_low")
        self.proj_psum = sem("proj_psum")
        self.proj_out = sem("proj_out")
        self.squared = sem("squared")
        self.sumsq_psum = sem("sumsq_psum")
        self.root_done = sem("root_done")
        self.root_spread = sem("root_spread")
        self.root_applied = sem("root_applied")
        self.scores_psum = sem("scores_psum")
        self.max_ready = sem("max_ready")
        self.exp_done = sem("exp_done")
        self.p_ready = sem("p_ready")
        self.t_psum = sem("t_psum")
        self.pt_act = sem("pt_act")
        self.o_psum = sem("o_psum")
        self.o_ready = sem("o_ready")
        self.out_psum = sem("out_psum")
        self.x_mixed = sem("x_mixed")
        self.slots_ready = sem("slots_ready")
        self.take_ready = sem("take_ready")
        self.gathered = sem("gathered")
        self.xt_ready = sem("xt_ready")
        self.gate_exp = sem("gate_exp")
        self.gate_plus = sem("gate_plus")
        self.gate_inv = sem("gate_inv")
        self.gate_act = sem("gate_act")
        self.hid_ready = sem("hid_ready")
        self.give_ready = sem("give_ready")
        self.giveT_psum = sem("giveT_psum")
        self.giveT_ready = sem("giveT_ready")
        self.hidT_psum = sem("hidT_psum")
        self.hidT_ready = sem("hidT_ready")
        self.y_ready = sem("y_ready")
        self.scattered = sem("scattered")
        self.moe_out = sem("moe_out")
        self.unit_loaded = [sem(f"unit_loaded{u}") for u in range(RING)]
        self.unit_used = [sem(f"unit_used{u}") for u in range(RING)]
        if layer % 2 == 0:
            self.b_ln = sem("b_ln")
            self.o_squared = sem("o_squared")
            self.o_sumsq = sem("o_sumsq")
            self.sub_spread = sem("sub_spread")
            self.sub_applied = sem("sub_applied")
        else:
            self.pt_dve = sem("pt_dve")
            self.forget_psum = sem("forget_psum")
            self.forget_abs = sem("forget_abs")
            self.forget_ln = sem("forget_ln")
            self.cum_ready = sem("cum_ready")


def trunk(nc, x, norm_mix_g, norm_ffn_g, ab_w_in, a_q_gain, a_k_gain, a_lam_q1, a_lam_k1, a_lam_q2,
          a_lam_k2, a_subln_g, ab_w_out, c_w_in, c_b_f, c_q_gain, c_k_gain, c_w_out, moe_w_group,
          moe_b_group, moe_w_router, moe_b_router, moe_w_gate, moe_w_up, moe_w_down, out):
    with ExitStack() as ctx:
        def sb(name, shape, dt=F32):
            return ctx.enter_context(nc.sbuf_tensor(name, shape, dt))

        def sem(name):
            return ctx.enter_context(nc.semaphore(name))

        def rounded(name, shape, at):
            return nc.alloc_sbuf_tensor_at(name, shape, F32R, offset=at)

        ring, ring_at = [], []
        for slot in range(RING):
            ring.append(sb(f"ring{slot}", [P, UNIT]))
            ring_at.append(nc.sbuf_base - 4 * UNIT)
        x_sb = sb("x_sb", [P, NT, D])
        hn = sb("hn", [P, NT, D])
        oT = hn[:, :, :].rearrange("p a (b t) -> p (a b) t", t=T)
        hn_at = nc.sbuf_base - 4 * NT * D
        hT = sb("hT", [P, NC, T])
        hT_at = nc.sbuf_base - 4 * NC * T
        h_high = rounded("h_high", [P, NC, T], hn_at)
        h_low = rounded("h_low", [P, NC, T], hT_at)
        w_low = [rounded(f"w_low{u}", [P, NC, COLS], ring_at[u]) for u in range(UNITS)]
        w_high = [rounded(f"w_high{i}", [P, NC, COLS], ring_at[UNITS + i])
                  for i in range(RING - UNITS)]
        o_squares = hT[:, 0:A_HEADS, :]
        qkT = sb("qkT", [P, 16, T])
        v_sb = sb("v_sb", [P, NT, D])
        probs = sb("probs", [P, 4, SW])
        pT = sb("pT", [P, 4, SW])
        pT_flat = pT[:, :, :].rearrange("p a b -> p (a b)")
        squares = [pT_flat[:, COLS * i:COLS * (i + 1)] for i in range(2)]
        probs_flat = probs[:, :, :].rearrange("p a b -> p (a b)")
        ident = sb("ident", [P, P])
        ident_bf = sb("ident_bf", [P, P], BF16)
        ones_bf = sb("ones_bf", [P, P], BF16)
        before_bf = sb("before_bf", [P, P], BF16)
        neg_from = sb("neg_from", [P, P])
        neg_ones = sb("neg_ones", [P, P])
        strict = sb("strict", [P, P])
        mask_causal = sb("mask_causal", [P, SW], BF16)
        mask_strict = sb("mask_strict", [P, SW], BF16)
        dist = probs_flat[:, 0:SW]
        bias_a = sb("bias_a", [P, A_HEADS, SW], BF16)
        slide = sb("slide", [P, 62])
        slide_all = sb("slide_all", [P, 64])
        sel_head = sb("sel_head", [96, C_HEADS], BF16)
        slot_id = sb("slot_id", [P, 2, SLOTS])
        desc4 = sb("desc4", [P, 4])
        gain_mix = sb("gain_mix", [P, LAYERS, NC])
        gain_ffn = sb("gain_ffn", [P, LAYERS, NC])
        g_qk = sb("g_qk", [P, LAYERS, 2])
        g_sub = sb("g_sub", [P, 1])
        lam_in = probs_flat[:, SW:SW + 4 * HD].rearrange("p (a b) -> p a b", a=4)
        lam_prod = probs_flat[:, SW + 4 * HD:SW + 6 * HD].rearrange("p (a b) -> p a b", a=2)
        lam_s = sb("lam_s", [P, 4])
        neg_lam = sb("neg_lam", [P, 1])
        wf3 = sb("wf3", [P, NC, 96])
        b_f = sb("b_f", [96, 1])
        w_rt = sb("w_rt", [P, LAYERS, NC, NR])
        b_rt = sb("b_rt", [P, LAYERS, NR])
        ssq = sb("ssq", [P, NT])
        root_x = sb("root_x", [P, T])
        root_ln = sb("root_ln", [P, T])
        root_y = sb("root_y", [P, T])
        root_t = root_ln
        nmax = sb("nmax", [P, 2, 4])
        rsum = sb("rsum", [P, 2, 4])
        rinv = sb("rinv", [P, 2, 4])
        forget = [probs_flat[0:96, T * i:T * (i + 1)] for i in range(5)]
        cum = [sb(f"cum{i}", [96, T], BF16) for i in range(3)]
        cum_pos = sb("cum_pos", [96, T], BF16)
        cum_neg = sb("cum_neg", [96, T], BF16)
        v_flat = v_sb[:, :, :].rearrange("p a b -> p (a b)")
        lg = v_flat[:, 0:NT * NR].rearrange("p (t n) -> p t n", t=NT)
        rt = v_flat[:, 64:64 + 14 * NT * 4].rearrange("p (k t n) -> p k t n", k=14, t=NT)
        picked = v_flat[:, 192:224].rearrange("p (t g e) -> p t g e", t=NT, g=N_GROUPS)
        chosen_f = v_flat[:, 224:256].rearrange("p (t e) -> p t e", t=NT)
        weight_of = v_flat[:, 256:256 + NT * (ROUNDS * N_EXPERTS + 1)].rearrange("p (t e) -> p t e", t=NT)
        chosen_bf = sb("chosen_bf", [P, NT, N_EXPERTS], BF16)
        most = sb("most", [P, 2])
        slot_of = sb("slot_of", [P, NT, ROUNDS * N_EXPERTS + 1])
        last_quads = sb("last_quads", [P, LAYERS], I32)
        qk_flat = qkT[:, :, :].rearrange("p a b -> p (a b)")
        xT = qk_flat[:, 0:512].rearrange("p (c s) -> p c s", c=NC)
        take = qk_flat[:, 512:768].rearrange("p (t s) -> p t s", t=NT)
        give = qk_flat[:, 768:1024].rearrange("p (t s) -> p t s", t=NT)
        giveT = qk_flat[:, 1024:1280]
        gate_e = qk_flat[:, 1536:2048]
        sig = qk_flat[:, 2048:2560]
        hid = qk_flat[:, 2560:3072]
        hidT = qk_flat[:, 3072:3584].rearrange("p (s t) -> p s t", s=SUB)
        y_sb = qk_flat[:, 3584:4096]

        bank = [ctx.enter_context(nc.psum_tensor(f"bank{i}", [P, COLS], F32)) for i in range(8)]
        ACC, GATE, UP, Y, MISC = bank[0:4], bank[4], bank[5], bank[6], bank[7]
        O_BANK, SUM_BANK = bank[6], bank[7]

        pool_step = sem("pool_step")
        consts_made = sem("consts_made")
        act_step = sem("act_step")
        dve_step = sem("dve_step")
        x_loaded = sem("x_loaded")
        gains_loaded = sem("gains_loaded")
        params_loaded = sem("params_loaded")
        router_loaded = sem("router_loaded")
        forget_loaded = sem("forget_loaded")
        forget_zeroed = sem("forget_zeroed")
        tables_made = sem("tables_made")
        lam_sums = sem("lam_sums")
        lam_exp = sem("lam_exp")
        out_stored = sem("out_stored")
        wout_loaded = sem("wout_loaded")
        logits_psum = sem("logits_psum")
        rt_shift = sem("rt_shift")
        rt_exp = sem("rt_exp")
        rt_gap = sem("rt_gap")
        rt_gap_exp = sem("rt_gap_exp")
        chosen = sem("chosen")
        rank_psum = sem("rank_psum")
        layers = []
        for i in range(LAYERS):
            layers.append(LayerSignals(nc, ctx, i))
        CONSTS = 16
        GAINS, PARAMS = 16 * 8, 16 * 13
        ROUTER, FORGET, WIN = 16 * 12, 16 * 9, 16 * 2

        w_in = [ab_w_in[0], c_w_in[0]]
        w_out = [ab_w_out[0], c_w_out[0]]
        norm_steps = [sum(2 for k, _ in units if k == "norm") for units in PLAN]
        SUBLN = 4

        def is_b(layer, job):
            return layer == 0 and job >= A_HEADS

        def rows(w):
            return w.rearrange("(h p s) n -> h p s n", h=2, s=SUB)

        def win_view(u):
            return ring[u][:, :].rearrange("p (c n) -> p c n", c=NC)

        def wout_view(h):
            return ring[UNITS + h][:, :].rearrange("p (c n) -> p c n", n=D)

        def expert_rhs(u, s, half):
            return ring[u][:, s * D + HALF * half:s * D + HALF * (half + 1)]

        def maps_before(layer, job):
            return job + max(0, job - A_HEADS) if layer == 0 else 2 * job

        def roots_before(layer, which):
            names = ("mix", "qk", "sub", "ffn") if layer == 0 else ("mix", "qk", "ffn")
            return names.index(which) + 1

        def place(k, u):
            return (UNITS * k + u) % RING, (UNITS * k + u) // RING

        def turns(quad, k):
            return quad * QUAD + k

        def used(s, quad, k, u):
            slot, lap = place(k, u)
            return s.unit_used[slot], quad * LAPS + (lap + 1)

        def spread(column, shape):
            return column.to_broadcast(shape)

        def by_chunk(t, h, s):
            return hn[:, t, HALF * h:HALF * (h + 1)].rearrange("p (q s) -> p s q", s=SUB)[:, s, :]

        def gains(table, layer, h, n):
            g = table[:, layer, SUB * h:SUB * (h + 1)]
            return g.rearrange("p (c a) -> p c a", a=1).to_broadcast([P, SUB, n])

        def map_cols(i):
            return slice(0, P) if i == 0 else slice(P, SW)

        block = ctx.enter_context(nc.Block())

        @block.sync
        def _(sp):
            for t in range(NT):
                sp.dma_start(x_sb[:, t, :], x[0, t * P:(t + 1) * P, :]).then_inc(x_loaded, 16)

            def load(dst, src, signal):
                sp.dma_start(dst, src).then_inc(signal, 16)

            def load_win(layer, u):
                for h in range(2):
                    sp.dma_start(win_view(u)[:, SUB * h:SUB * (h + 1), :],
                                 rows(w_in[layer])[h, :, :, COLS * u:COLS * (u + 1)]
                                 ).then_inc(layers[layer].unit_loaded[u], 16)

            def load_wout(layer):
                for h in range(2):
                    sp.dma_start(wout_view(h), w_out[layer].rearrange("(h c p) n -> h p c n", h=2,
                                                                      p=P)[h]
                                 ).then_inc(wout_loaded, 16)

            def load_unit(layer, slot, u, e):
                w = (moe_w_gate, moe_w_up, moe_w_down)[u // 2][layer]
                src = w[bass.ds(e, 1)].rearrange("e (h p s) n -> (e h) p (s n)", h=2, s=SUB)[u % 2]
                sp.dma_start(ring[slot][:, :], src).then_inc(layers[layer].unit_loaded[slot], 16)

            for i in range(LAYERS):
                for g, dst in ((norm_mix_g, gain_mix), (norm_ffn_g, gain_ffn)):
                    for h in range(2):
                        load(dst[:, i, SUB * h:SUB * (h + 1)],
                             g[i].rearrange("(h p s) -> h p s", h=2, s=SUB)[h], gains_loaded)
            for u in range(UNITS):
                load_win(0, u)
            for i, (q, k) in enumerate(((a_q_gain, a_k_gain), (c_q_gain, c_k_gain))):
                for j, g in enumerate((q, k)):
                    for m in range(2):
                        load(g_qk[HD * m:HD * (m + 1), i, j:j + 1],
                             g[0].rearrange("(p a) -> p a", a=1), params_loaded)
            load(g_sub[:, :], a_subln_g[0].rearrange("(p a) -> p a", a=1), params_loaded)
            for j, g in enumerate((a_lam_q1, a_lam_k1, a_lam_q2, a_lam_k2)):
                load(lam_in[:, j, :], g[0].partition_broadcast(P), params_loaded)
            for i in range(LAYERS):
                load(b_rt[:, i, 0:N_GROUPS], moe_b_group[i].partition_broadcast(P), router_loaded)
                load(b_rt[:, i, N_GROUPS:NR], moe_b_router[i].partition_broadcast(P), router_loaded)
                for w, c, n in ((moe_w_group, 0, N_GROUPS), (moe_w_router, N_GROUPS, N_EXPERTS)):
                    for h in range(2):
                        load(w_rt[:, i, SUB * h:SUB * (h + 1), c:c + n], rows(w[i])[h],
                             router_loaded)
            sp.wait_ge(forget_zeroed, 2)
            for g in range(3):
                load(b_f[32 * g:32 * g + C_HEADS, :], c_b_f[0].rearrange("(p a) -> p a", a=1),
                     forget_loaded)
                for h in range(2):
                    load(wf3[:, SUB * h:SUB * (h + 1), 32 * g:32 * g + C_HEADS],
                         rows(c_w_in[0])[h, :, :, 3 * D:3 * D + C_HEADS], forget_loaded)
            for layer in range(LAYERS):
                s = layers[layer]
                for u in range(UNITS):
                    sp.wait_ge(s.proj_psum, 2 * u + 2)
                    load_unit(layer, u, u, 0)
                load_wout(layer)
                sp.wait_ge(s.out_psum, 4)
                for slot in range(UNITS, RING):
                    load_unit(layer, slot, slot - UNITS, 1)
                sp.wait_ge(s.slots_ready, 1)
                last_quad = sp.value_load(last_quads[0:1, layer:layer + 1],
                                          min_val=N_EXPERTS // QUAD - 1,
                                          max_val=ROUNDS * N_EXPERTS // QUAD - 1)
                with sp.Fori(0, last_quad) as quad:
                    first = (quad & (N_EXPERTS // QUAD - 1)) * QUAD
                    for i in range(LAPS * RING):
                        k, u = (RING + i) // UNITS, (RING + i) % UNITS
                        sp.wait_ge(s.unit_used[i % RING], quad * LAPS + (i // RING + 1))
                        sp.nop(nofuse=True)
                        if k < QUAD:
                            load_unit(layer, i % RING, u, first + k)
                        else:
                            load_unit(layer, i % RING, u,
                                      ((quad + 1) & (N_EXPERTS // QUAD - 1)) * QUAD + (k - QUAD))
                for i in range((LAPS - 1) * RING):
                    k, u = (RING + i) // UNITS, (RING + i) % UNITS
                    sp.wait_ge(s.unit_used[i % RING], last_quad * LAPS + (i // RING + 1))
                    load_unit(layer, i % RING, u, N_EXPERTS - QUAD + k)
                if layer + 1 < LAYERS:
                    for u in range(UNITS):
                        sp.wait_ge(s.unit_used[u], last_quad * LAPS + LAPS)
                        load_win(layer + 1, u)
            for q in range(4):
                sp.wait_ge(layers[-1].moe_out, q + 1)
                t, h = q // 2, q % 2
                sp.dma_start(out[0, t * P:(t + 1) * P, HALF * h:HALF * (h + 1)],
                             x_sb[:, t, HALF * h:HALF * (h + 1)]).then_inc(out_stored, 16)
            sp.wait_ge(out_stored, 64)

        @block.gpsimd
        def _(pool):
            steps = [0]

            def own(ins):
                steps[0] += 1
                ins.then_inc(pool_step, 1)
                pool.wait_ge(pool_step, steps[0])

            made_before = [0]

            def made(ins):
                made_before[0] += 1
                ins.then_inc(consts_made, 1)
                pool.wait_ge(consts_made, made_before[0])

            def select(out_ap, in_ap, pattern, cmp, base, mult, fill):
                return pool.affine_select(out=out_ap, in_=in_ap, pattern=pattern, compare_op=cmp,
                                          fill=fill, base=base, channel_multiplier=mult)

            own(pool.memset(ident[:, :], 0.0))
            made(select(ident[:, :], ident[:, :], [[-1, P]], ALU.not_equal, 0, 1, 1.0
                   ))
            own(pool.memset(ident_bf[:, :], 0.0))
            made(select(ident_bf[:, :], ident_bf[:, :], [[-1, P]], ALU.not_equal, 0, 1, 1.0
                   ))
            own(pool.memset(slide[:, :], 0.0))
            made(pool.memset(slide[0:HD, 30:31], 1.0))
            made(pool.memset(slide[HD:P, 31:32], 1.0))
            own(pool.memset(slide_all[:, :], 0.0))
            made(pool.memset(slide_all[:, 31:32], 1.0))
            made(pool.iota(dist[:, 0:P], [[-1, P]], base=0, channel_multiplier=1,
                      allow_small_or_imprecise_dtypes=True))
            made(pool.iota(dist[:, P:SW], [[-1, T]], base=P, channel_multiplier=1,
                      allow_small_or_imprecise_dtypes=True))
            own(pool.memset(mask_causal[:, :], 0.0))
            made(select(mask_causal[:, 0:P], mask_causal[:, 0:P], [[-1, P]], ALU.is_ge, 0, 1, NEG
                   ))
            made(select(mask_causal[:, 2 * P:SW], mask_causal[:, 2 * P:SW], [[-1, P]], ALU.is_ge, 0, 1,
                   NEG))
            own(pool.memset(mask_strict[:, :], 0.0))
            made(select(mask_strict[:, 0:P], mask_strict[:, 0:P], [[1, P]], ALU.is_gt, 0, -1, NEG
                   ))
            made(select(mask_strict[:, 2 * P:SW], mask_strict[:, 2 * P:SW], [[1, P]], ALU.is_gt, 0, -1,
                   NEG))
            own(pool.memset(neg_ones[:, :], -1.0))
            made(select(neg_from[:, :], neg_ones[:, :], [[-1, P]], ALU.is_ge, 0, 1, 0.0
                   ))
            own(pool.memset(ones_bf[:, :], 1.0))
            made(select(before_bf[:, :], ones_bf[:, :], [[1, P]], ALU.is_gt, 0, -1, 0.0
                   ))
            made(select(strict[:, :], ones_bf[:, :], [[1, P]], ALU.is_gt, 0, -1, 0.0
                   ))
            made(pool.iota(slot_id[:, :, :], [[0, 2], [1, SLOTS]], base=0, channel_multiplier=0,
                      allow_small_or_imprecise_dtypes=True))
            own(pool.memset(sel_head[:, :], 0.0))
            for g in range(3):
                part = sel_head[32 * g:32 * (g + 1), :]
                last = select(part, part, [[-1, C_HEADS]], ALU.not_equal, 0, 1, 1.0)
                own(last)
            made(pool.iota(desc4[:, :], [[-1, 4]], base=4, channel_multiplier=0,
                      allow_small_or_imprecise_dtypes=True))

        @block.scalar
        def _(act):
            act.preload_act_table_set("natural_log_exp_and_others")

            steps = [0]

            def own(ins):
                steps[0] += 1
                ins.then_inc(act_step, 1)
                act.wait_ge(act_step, steps[0])

            def sum_squares(s, t):
                act.activation(qk_flat[:, D * t:D * (t + 1)], x_sb[:, t, :], ACT.Square,
                               accum_out=ssq[:, t:t + 1]).then_inc(s.squares_summed, 1)

            def weights_high(s, u):
                act.wait_ge(s.unit_loaded[u], WIN)
                if u >= 2:
                    act.wait_ge(s.proj_psum, 2 * (u - 1))
                for h in range(2):
                    part = slice(SUB * h, SUB * (h + 1))
                    act.activation(w_high[u % 2][:, part, :], win_view(u)[:, part, :],
                                   ACT.Copy).then_inc(s.w_high, 1)

            def root_guess(s, n, r, c):
                act.wait_ge(s.rsq_in, n)
                own(act.activation(root_ln[0:r, 0:c], root_x[0:r, 0:c], ACT.Ln))
                act.activation(root_y[0:r, 0:c], root_ln[0:r, 0:c], ACT.Exp, scale=-0.5
                               ).then_inc(s.rsq_guess, 1)

            def slots_free(layer, j):
                s = layers[layer]
                if j >= 2 and is_b(layer, j - 2):
                    act.wait_ge(s.o_psum, j - 1)
                elif j >= 2:
                    act.wait_ge(s.t_psum, maps_before(layer, j - 1))

            def exponentials(layer, j):
                s = layers[layer]
                for m in range(2):
                    slot = 2 * (j % 2) + m
                    if is_b(layer, j):
                        act.wait_ge(s.scores_psum, 2 * j + m + 1)
                        if j >= 2 and is_b(layer, j - 2):
                            act.wait_ge(s.t_psum, maps_before(layer, j - 1))
                        elif j >= 2:
                            act.wait_ge(s.o_psum, j - 1)
                        z = pT[:, slot, :]
                        own(act.activation(z, bank[2 + slot][:, 0:SW], ACT.Abs))
                        own(act.activation(z, z, ACT.Exp, scale=-1.0))
                        act.activation(z, z, ACT.Ln, bias=1.0).then_inc(s.b_ln, 1)
                        continue
                    act.wait_ge(s.max_ready, 2 * j + m + 1)
                    if m == 0:
                        slots_free(layer, j)
                    b = bank[2 + slot]
                    for i in range(NT):
                        k = 2 * m + i
                        last = act.activation(probs[:, slot, map_cols(i)], b[:, map_cols(i)], ACT.Exp,
                                              bias=nmax[:, j % 2, k:k + 1],
                                              accum_out=rsum[:, j % 2, k:k + 1])
                    last.then_inc(s.exp_done, 1)

            def second(layer, j):
                s = layers[layer]
                if is_b(layer, j):
                    slots_free(layer, j)
                    for m in range(2):
                        slot = 2 * (j % 2) + m
                        act.wait_ge(s.t_psum, maps_before(layer, j) + m + 1)
                        act.activation(probs[:, slot, :], bank[2 + slot][:, 0:SW], ACT.Exp
                                       ).then_inc(s.exp_done, 1)
                    return
                act.wait_ge(s.t_psum, maps_before(layer, j) + 1)
                if j >= 2:
                    act.wait_ge(s.o_psum, j - 1)
                act.activation(pT[:, 2 * (j % 2), :], bank[0][:, 0:SW], ACT.Copy).then_inc(s.pt_act, 1)

            def output(layer, j):
                s = layers[layer]
                act.wait_ge(s.o_psum, j + 1)
                act.activation(oT[:, j, :], O_BANK[:, 0:T], ACT.Copy).then_inc(s.o_ready, 1)
                if layer == 0 and j < A_HEADS:
                    act.wait_ge(s.o_ready, j + 1)
                    act.activation(o_squares[:, j, :], oT[:, j, :], ACT.Square
                                   ).then_inc(s.o_squared, 1)

            for layer in range(LAYERS):
                s = layers[layer]
                for t in range(NT):
                    if layer == 0:
                        act.wait_ge(x_loaded, 16 * NT)
                    else:
                        act.wait_ge(layers[layer - 1].moe_out, 4)
                    sum_squares(s, t)
                root_guess(s, roots_before(layer, "mix"), P, NT)
                weights_high(s, 0)
                act.wait_ge(s.ht_psum, 4)
                act.wait_ge(s.ht_ready, 4)
                for h in range(2):
                    part = slice(SUB * h, SUB * (h + 1))
                    act.activation(h_high[:, part, :], hT[:, part, :], ACT.Copy
                                   ).then_inc(s.h_high, 1)
                done = 0
                for j in range(STEPS):
                    kind, first = PLAN[layer][j // 2]
                    if j % 2 == 0 and j // 2 + 1 < UNITS:
                        weights_high(s, j // 2 + 1)
                    if j == 0 and layer == 1:
                        act.wait_ge(s.forget_abs, 1)
                        own(act.activation(forget[2], forget[1], ACT.Exp, scale=-1.0))
                        act.activation(forget[3], forget[2], ACT.Ln, bias=1.0
                                       ).then_inc(s.forget_ln, 1)
                    if kind == "norm":
                        act.wait_ge(s.proj_out, j + 1)
                        if done >= 2:
                            act.wait_ge(s.sumsq_psum, done - 1)
                        c = first + 2 * (j % 2)
                        act.activation(squares[done % 2],
                                       qkT[:, c:c + 2, :].rearrange("p a b -> p (a b)"), ACT.Square
                                       ).then_inc(s.squared, 1)
                        done += 1
                    if j == norm_steps[layer]:
                        root_guess(s, roots_before(layer, "qk"), 32, T)
                        if layer == 0:
                            act.wait_ge(lam_sums, 1)
                            act.activation(lam_s[:, 2:4], lam_s[:, 0:2], ACT.Exp).then_inc(lam_exp, 1)
                for i in range(JOBS + 2):
                    if layer == 0 and i == SUBLN + 3:
                        root_guess(s, roots_before(layer, "sub"), 32, T)
                    if i < JOBS:
                        exponentials(layer, i)
                    if 1 <= i < JOBS + 1:
                        second(layer, i - 1)
                    if i >= 2:
                        output(layer, i - 2)
                for t in range(NT):
                    act.wait_ge(s.x_mixed, 2 * (t + 1))
                    sum_squares(s, t)
                root_guess(s, roots_before(layer, "ffn"), P, NT)
                act.wait_ge(rt_shift, layer + 1)
                act.activation(rt[:, 2], rt[:, 1], ACT.Exp).then_inc(rt_exp, 1)
                act.wait_ge(rt_gap, layer + 1)
                act.activation(rt[:, 12, :, 1:2], rt[:, 12, :, 0:1], ACT.Exp).then_inc(rt_gap_exp, 1)
                act.wait_ge(s.slots_ready, 1)
                last_quad = act.value_load(last_quads[0:1, layer:layer + 1],
                                          min_val=N_EXPERTS // QUAD - 1,
                                          max_val=ROUNDS * N_EXPERTS // QUAD - 1)
                with act.Fori(0, last_quad + 1) as quad:
                    for k in range(QUAD):
                        act.wait_ge(*used(s, quad, k, 1))
                        act.activation(gate_e, GATE[:, :], ACT.Exp, scale=-1.0).then_inc(s.gate_exp, 1)
                        act.wait_ge(s.giveT_psum, turns(quad, k + 1))
                        act.activation(giveT, GATE[:, 0:T], ACT.Copy).then_inc(s.giveT_ready, 1)
                        act.wait_ge(*used(s, quad, k, 5))
                        act.activation(y_sb, Y[:, :], ACT.Copy).then_inc(s.y_ready, 1)


        @block.vector
        def _(dve):
            steps = [0]

            def own(ins):
                steps[0] += 1
                ins.then_inc(dve_step, 1)
                dve.wait_ge(dve_step, steps[0])

            ts, tt, stt = nc.vector.tensor_scalar, nc.vector.tensor_tensor, nc.vector.scalar_tensor_tensor

            def root(s, n, src, r, c, count):
                xs, ys, tmp = root_x[0:r, 0:c], root_y[0:r, 0:c], root_t[0:r, 0:c]
                ts(xs, src, 1.0 / count, EPS, ALU.mult, ALU.add).then_inc(s.rsq_in, 1)
                dve.wait_ge(s.rsq_guess, n)
                own(stt(tmp, xs, -0.5, ys, ALU.mult, ALU.mult))
                own(tt(tmp, tmp, ys, ALU.mult))
                return stt(ys, tmp, 1.5, ys, ALU.add, ALU.mult)

            def normalise(layer, which, table):
                s = layers[layer]
                n = 0 if which == "mix" else 1
                dve.wait_ge(s.squares_summed, NT * (n + 1))
                own(root(s, roots_before(layer, which), ssq[:, :], P, NT, D))
                for t in range(NT):
                    ts(hn[:, t, :], x_sb[:, t, :], root_y[:, t:t + 1], None, ALU.mult
                       ).then_inc(s.hn_ready, 1)
                if layer == 0 and n == 0:
                    dve.wait_ge(gains_loaded, GAINS)
                for g in range(4):
                    t, h = g // 2, g % 2
                    dve.wait_ge(s.ht_psum, 4 * n + g + 1)
                    tt(hT[:, SUB * h:SUB * (h + 1), P * t:P * (t + 1)],
                       bank[2 + g][:, :].rearrange("p (c t) -> p c t", c=SUB),
                       gains(table, layer, h, P), ALU.mult).then_inc(s.ht_ready, 1)

            def make_tables():
                dve.wait_ge(params_loaded, PARAMS)
                dve.wait_ge(consts_made, CONSTS)
                own(ts(g_qk[:, :, 0:1], g_qk[:, :, 0:1], SCALE, None, ALU.mult))
                own(ts(g_sub[:, :], g_sub[:, :], 1.0 - LAM_INIT, None, ALU.mult))
                for m in range(2):
                    last = tt(lam_prod[:, m, :], lam_in[:, 2 * m, :], lam_in[:, 2 * m + 1, :], ALU.mult)
                own(last)
                nc.vector.tensor_reduce(lam_s[:, 0:2], lam_prod, AX_X, ALU.add).then_inc(lam_sums, 1)
                for h in range(A_HEADS):
                    slope = 2.0 ** (-8.0 * (h + 1) / A_HEADS)
                    stt(bias_a[:, h, :], dist, -slope, mask_causal[:, :], ALU.mult, ALU.add
                        ).then_inc(tables_made, 1)
                dve.wait_ge(lam_exp, 1)
                own(tt(neg_lam[:, :], lam_s[:, 3:4], lam_s[:, 2:3], ALU.subtract))
                own(ts(neg_lam[:, :], neg_lam[:, :], -LAM_INIT, None, ALU.add))

            def first(layer, j):
                s = layers[layer]
                if is_b(layer, j):
                    return
                for m in range(2):
                    slot = 2 * (j % 2) + m
                    dve.wait_ge(s.scores_psum, 2 * j + m + 1)
                    for i in range(NT):
                        k = 2 * m + i
                        last = nc.vector.tensor_reduce(nmax[:, j % 2, k:k + 1],
                                                       bank[2 + slot][:, map_cols(i)], AX_X, ALU.max,
                                                       negate=True)
                    last.then_inc(s.max_ready, 1)

            def second(layer, j):
                s = layers[layer]
                slot = 2 * (j % 2)
                if is_b(layer, j):
                    for m in range(2):
                        dve.wait_ge(s.b_ln, 2 * (j - A_HEADS) + m + 1)
                        z = pT[:, slot + m, :]
                        own(stt(z, bank[2 + slot + m][:, 0:SW], 0.0, z, ALU.max, ALU.add))
                        diagonal = z.rearrange("p (b k) -> p b k", b=3)[:, 0:3:2, :]
                        tt(diagonal, diagonal,
                           strict[:, :].rearrange("p (a k) -> p a k", a=1).to_broadcast([P, 2, P]),
                           ALU.mult).then_inc(s.p_ready, 1)
                    return
                dve.wait_ge(s.exp_done, 2 * j + 2)
                own(nc.vector.reciprocal(rinv[:, j % 2, :], rsum[:, j % 2, :]))
                if layer == 0:
                    own(ts(rinv[:, j % 2, 2:4], rinv[:, j % 2, 2:4], neg_lam[:, :], None, ALU.mult))
                    for i in range(NT):
                        p1 = probs[:, slot, map_cols(i)]
                        last = ts(p1, p1, rinv[:, j % 2, i:i + 1], None, ALU.mult)
                    own(last)
                    for i in range(NT):
                        p1, p2 = probs[:, slot, map_cols(i)], probs[:, slot + 1, map_cols(i)]
                        last = stt(p1, p2, rinv[:, j % 2, 2 + i:3 + i], p1, ALU.mult, ALU.add)
                    last.then_inc(s.p_ready, 1)
                    return
                for m in range(2):
                    for i in range(NT):
                        k = 2 * m + i
                        p1 = probs[:, slot + m, map_cols(i)]
                        last = ts(p1, p1, rinv[:, j % 2, k:k + 1], None, ALU.mult)
                    last.then_inc(s.p_ready, 1)

            def third(layer, j):
                s = layers[layer]
                if layer == 0:
                    return
                dve.wait_ge(s.t_psum, maps_before(layer, j) + 2)
                if j >= 2:
                    dve.wait_ge(s.o_psum, j - 1)
                nc.vector.tensor_copy(pT[:, 2 * (j % 2) + 1, :], bank[1][:, 0:SW]).then_inc(s.pt_dve, 1)

            def weights_low(s, u):
                for h in range(2):
                    part = slice(SUB * h, SUB * (h + 1))
                    dve.wait_ge(s.w_high, 2 * u + h + 1)
                    tt(w_low[u][:, part, :], win_view(u)[:, part, :],
                       w_high[u % 2][:, part, :].bitcast(F32), ALU.subtract).then_inc(s.w_low, 1)

            def forget_gate(s):
                z, az, _, ln1, lf = forget
                dve.wait_ge(s.forget_psum, 1)
                dve.wait_ge(forget_loaded, FORGET)
                own(ts(z, O_BANK[0:96, 0:T], b_f[:, :], None, ALU.add))
                stt(az, z, -1.0, z, ALU.mult, ALU.max).then_inc(s.forget_abs, 1)
                dve.wait_ge(s.forget_ln, 1)
                own(stt(lf, z, 0.0, ln1, ALU.min, ALU.subtract))
                own(nc.vector.tensor_tensor_scan(z, ones_bf[0:96, 0:1].to_broadcast([96, T]), lf, 0.0,
                                                 ALU.mult, ALU.add))
                own(nc.vector.tensor_copy(cum[0][:, :], z))
                own(tt(z, z, cum[0][:, :], ALU.subtract))
                own(nc.vector.tensor_copy(cum[1][:, :], z))
                own(tt(z, z, cum[1][:, :], ALU.subtract))
                own(nc.vector.tensor_copy(cum[2][:, :], z))
                for g in range(3):
                    r = slice(32 * g, 32 * (g + 1))
                    nc.vector.tensor_copy(cum_pos[r, :], cum[g][r, :])
                    last = ts(cum_neg[r, :], cum[g][r, :], -1.0, None, ALU.mult)
                last.then_inc(s.cum_ready, 1)

            def first_of(row_max, values, out_ap):
                own(tt(rt[:, 3], values, spread(row_max, [P, NT, 4]), ALU.is_equal))
                d = desc4[:, :].rearrange("p (a k) -> p a k", a=1).to_broadcast([P, NT, 4])
                own(tt(rt[:, 4], rt[:, 3], d, ALU.mult))
                own(nc.vector.tensor_reduce(rt[:, 5, :, 0:1], rt[:, 4], AX_X, ALU.max))
                own(tt(out_ap, d, spread(rt[:, 5, :, 0:1], [P, NT, 4]), ALU.is_equal))

            def route(layer):
                s = layers[layer]
                reduce = nc.vector.tensor_reduce
                dve.wait_ge(logits_psum, layer + 1)
                own(tt(lg[:, :, :], MISC[:, 0:NT * NR].rearrange("p (t n) -> p t n", t=NT),
                       b_rt[:, layer:layer + 1, :].to_broadcast([P, NT, NR]), ALU.add))
                groups = lg[:, :, 0:N_GROUPS]
                experts = lg[:, :, N_GROUPS:NR].rearrange("p t (g e) -> p t g e", g=N_GROUPS)
                own(reduce(rt[:, 0, :, 0:1], groups, AX_X, ALU.max))
                tt(rt[:, 1], groups, spread(rt[:, 0, :, 0:1], [P, NT, 4]), ALU.subtract
                   ).then_inc(rt_shift, 1)
                first_of(rt[:, 0, :, 0:1], groups, rt[:, 6])
                in_group = rt[:, 6].rearrange("p t (g a) -> p t g a", a=1).to_broadcast(
                    [P, NT, N_GROUPS, PER_GROUP])
                for t in range(NT):
                    last = tt(picked[:, t], experts[:, t], in_group[:, t], ALU.mult)
                own(last)
                own(reduce(rt[:, 7], picked[:, :, :, :].rearrange("p t g e -> p t e g"), AX_X, ALU.add))
                own(reduce(rt[:, 8, :, 0:1], rt[:, 7], AX_X, ALU.max))
                first_of(rt[:, 8, :, 0:1], rt[:, 7], rt[:, 9])
                own(stt(rt[:, 10], rt[:, 9], NEG, rt[:, 7], ALU.mult, ALU.add))
                own(reduce(rt[:, 8, :, 1:2], rt[:, 10], AX_X, ALU.max))
                first_of(rt[:, 8, :, 1:2], rt[:, 10], rt[:, 11])
                tt(rt[:, 12, :, 0:1], rt[:, 8, :, 1:2], rt[:, 8, :, 0:1], ALU.subtract
                   ).then_inc(rt_gap, 1)
                dve.wait_ge(rt_exp, layer + 1)
                own(reduce(rt[:, 13, :, 0:1], rt[:, 2], AX_X, ALU.add))
                dve.wait_ge(rt_gap_exp, layer + 1)
                own(stt(rt[:, 13, :, 1:2], rt[:, 12, :, 1:2], 1.0, rt[:, 13, :, 0:1], ALU.add, ALU.mult))
                own(nc.vector.reciprocal(rt[:, 13, :, 2:3], rt[:, 13, :, 1:2]))
                own(tt(rt[:, 13, :, 3:4], rt[:, 13, :, 2:3], rt[:, 12, :, 1:2], ALU.mult))
                own(tt(rt[:, 3], rt[:, 9], spread(rt[:, 13, :, 2:3], [P, NT, 4]), ALU.mult))
                own(tt(rt[:, 4], rt[:, 11], spread(rt[:, 13, :, 3:4], [P, NT, 4]), ALU.mult))
                own(tt(rt[:, 3], rt[:, 3], rt[:, 4], ALU.add))
                own(tt(rt[:, 4], rt[:, 9], rt[:, 11], ALU.add))
                for t in range(NT):
                    def over_groups(value):
                        return value[:, t:t + 1, :].to_broadcast([P, N_GROUPS, PER_GROUP])
                    tt(chosen_f[:, t].rearrange("p (g e) -> p g e", g=N_GROUPS), in_group[:, t],
                       over_groups(rt[:, 4]), ALU.mult)
                    last = tt(weight_of[:, t, 0:N_EXPERTS].rearrange("p (g e) -> p g e", g=N_GROUPS),
                              in_group[:, t], over_groups(rt[:, 3]), ALU.mult)
                own(last)
                nc.vector.tensor_copy(chosen_bf[:, :, :], chosen_f[:, :, :]).then_inc(chosen, 1)
                for r in range(1, ROUNDS):
                    nc.vector.tensor_copy(weight_of[:, :, N_EXPERTS * r:N_EXPERTS * (r + 1)],
                                          weight_of[:, :, 0:N_EXPERTS])
                nc.vector.tensor_copy(weight_of[:, :, ROUNDS * N_EXPERTS:], weight_of[:, :, 0:1])
                dve.wait_ge(rank_psum, layer + 1)
                own(stt(picked[:, :, :, :].rearrange("p t g e -> p t (g e)"),
                        Y[:, 0:NT * N_EXPERTS].rearrange("p (t e) -> p t e", t=NT), 1.0,
                        chosen_f[:, :, :], ALU.add, ALU.mult))
                for r in range(ROUNDS):
                    last = ts(slot_of[:, :, N_EXPERTS * r:N_EXPERTS * (r + 1)],
                              picked[:, :, :, :].rearrange("p t g e -> p t (g e)"),
                              -1.0 - SLOTS * r, None, ALU.add)
                own(last)
                own(reduce(most[:, 0:1], Y[:, NT * N_EXPERTS:(NT + 1) * N_EXPERTS], AX_X, ALU.max))
                own(ts(most[:, 1:2], most[:, 0:1], float(SLOTS), float((ROUNDS - 1) * N_EXPERTS // QUAD),
                       ALU.is_gt, ALU.mult))
                ts(last_quads[:, layer:layer + 1], most[:, 1:2], float(N_EXPERTS // QUAD - 1), None, ALU.add
                   ).then_inc(s.slots_ready, 1)

            own(nc.vector.memset(wf3[:, :, :], 0.0))
            nc.vector.memset(b_f[:, :], 0.0).then_inc(forget_zeroed, 1)
            nc.vector.memset(slot_of[:, :, ROUNDS * N_EXPERTS:], -1.0).then_inc(forget_zeroed, 1)

            for layer in range(LAYERS):
                s = layers[layer]
                normalise(layer, "mix", gain_mix)
                weights_low(s, 0)
                if layer == 1:
                    dve.wait_ge(s.forget_psum, 1)
                for h in range(2):
                    part = slice(SUB * h, SUB * (h + 1))
                    dve.wait_ge(s.h_high, h + 1)
                    tt(h_low[:, part, :], hT[:, part, :], h_high[:, part, :].bitcast(F32),
                       ALU.subtract).then_inc(s.h_low, 1)
                if layer == 1:
                    forget_gate(s)
                spreads = norm_steps[layer]
                applied = 0
                for j in range(STEPS):
                    kind, at = PLAN[layer][j // 2]
                    if j % 2 == 0 and j // 2 + 1 < UNITS:
                        weights_low(s, j // 2 + 1)
                    dve.wait_ge(s.proj_psum, j + 1)
                    if kind == "v":
                        dst = v_sb[:, j % 2, at:at + COLS]
                    else:
                        c = at + 2 * (j % 2)
                        dst = qkT[:, c:c + 2, :].rearrange("p a b -> p (a b)")
                    if kind == "scaled":
                        ts(dst, bank[j % 2][:, :], SCALE, None, ALU.mult).then_inc(s.proj_out, 1)
                    else:
                        nc.vector.tensor_copy(dst, bank[j % 2][:, :]).then_inc(s.proj_out, 1)
                    if j == norm_steps[layer]:
                        dve.wait_ge(s.sumsq_psum, norm_steps[layer])
                        root(s, roots_before(layer, "qk"), SUM_BANK[0:32, 0:T], 32, T, HD
                             ).then_inc(s.root_done, 1)
                        if layer == 0:
                            make_tables()
                    first_spread = STEPS - 2
                    if j >= first_spread:
                        for g in range(applied, min(spreads, applied + 4)):
                            dve.wait_ge(s.root_spread, g + 1)
                            is_k = 1 if 2 * g >= spreads else 0
                            q2 = qkT[:, 2 * g:2 * g + 2, :].rearrange("p a b -> p (a b)")
                            stt(q2, q2, g_qk[:, layer, is_k:is_k + 1], bank[2 + g % 4][:, :],
                                ALU.mult, ALU.mult).then_inc(s.root_applied, 1)
                            applied = g + 1
                for i in range(JOBS + 2):
                    if layer == 0 and i == SUBLN + 3:
                        dve.wait_ge(s.o_sumsq, SUBLN)
                        root(s, roots_before(layer, "sub"), SUM_BANK[0:32, 0:T], 32, T, P
                             ).then_inc(s.root_done, 1)
                    b_now = i < JOBS and is_b(layer, i)
                    if i < JOBS and not b_now:
                        first(layer, i)
                    if 1 <= i < JOBS + 1:
                        second(layer, i - 1)
                        third(layer, i - 1)
                    if b_now:
                        first(layer, i)
                if layer == 0:
                    for g in range(2):
                        dve.wait_ge(s.sub_spread, g + 1)
                        o2 = oT[:, 2 * g:2 * g + 2, :].rearrange("p a b -> p (a b)")
                        stt(o2, o2, g_sub[:, :], bank[g][:, :], ALU.mult, ALU.mult
                            ).then_inc(s.sub_applied, 1)
                for q in range(4):
                    dve.wait_ge(s.out_psum, q + 1)
                    xq = x_sb[:, q // 2, HALF * (q % 2):HALF * (q % 2 + 1)]
                    tt(xq, bank[2 + q][:, :], xq, ALU.add).then_inc(s.x_mixed, 1)
                if layer == 0:
                    dve.wait_ge(router_loaded, ROUTER)
                normalise(layer, "ffn", gain_ffn)
                route(layer)

                def make_take(n):
                    for t in range(NT):
                        last = ts(take[:, t, :], slot_id[:, :, :].rearrange("p a b -> p (a b)"),
                                  slot_of[:, t, bass.ds(n, 1)], None, ALU.is_equal)
                    last.then_inc(s.take_ready, 1)

                def make_give(n):
                    for t in range(NT):
                        last = ts(give[:, t, :], slot_id[:, :, :].rearrange("p a b -> p (a b)"),
                                  slot_of[:, t, bass.ds(n, 1)], weight_of[:, t, bass.ds(n, 1)],
                                  ALU.is_equal, ALU.mult)
                    last.then_inc(s.give_ready, 1)

                def leave_gathered():
                    for h, b in enumerate((MISC, Y)):
                        last = tt(xT[:, SUB * h:SUB * (h + 1), :],
                           b[:, :].rearrange("p (c t) -> p c t", c=SUB)[:, :, 0:SLOTS],
                           gains(gain_ffn, layer, h, SLOTS), ALU.mult)
                    last.then_inc(s.xt_ready, 1)

                dve.wait_ge(s.slots_ready, 1)
                last_quad = dve.value_load(last_quads[0:1, layer:layer + 1],
                                          min_val=N_EXPERTS // QUAD - 1,
                                          max_val=ROUNDS * N_EXPERTS // QUAD - 1)
                make_take(0)
                make_give(0)
                dve.wait_ge(s.gathered, 1)
                leave_gathered()
                with dve.Fori(0, last_quad + 1) as quad:
                    for k in range(QUAD):
                        make_take(turns(quad, k + 1))
                        dve.wait_ge(s.gate_exp, turns(quad, k + 1))
                        ts(sig, gate_e, 1.0, None, ALU.add).then_inc(s.gate_plus, 1)
                        dve.wait_ge(s.gate_plus, turns(quad, k + 1))
                        nc.vector.reciprocal(sig, sig).then_inc(s.gate_inv, 1)
                        dve.wait_ge(s.gate_inv, turns(quad, k + 1))
                        tt(sig, GATE[:, :], sig, ALU.mult).then_inc(s.gate_act, 1)
                        dve.wait_ge(s.gate_act, turns(quad, k + 1))
                        dve.wait_ge(*used(s, quad, k, 3))
                        tt(hid, UP[:, :], sig, ALU.mult).then_inc(s.hid_ready, 1)
                        dve.wait_ge(s.gathered, turns(quad, k + 2))
                        leave_gathered()
                        dve.wait_ge(s.giveT_psum, turns(quad, k + 1))
                        make_give(turns(quad, k + 1))
                        dve.wait_ge(s.hidT_psum, turns(quad, k + 1))
                        nc.vector.tensor_copy(hidT, MISC[:, :].rearrange("p (s t) -> p s t", s=SUB)
                                              ).then_inc(s.hidT_ready, 1)
                dve.wait_ge(s.scattered, last_quad * QUAD + QUAD)
                for q in range(4):
                    nc.vector.tensor_copy(x_sb[:, q // 2, HALF * (q % 2):HALF * (q % 2 + 1)],
                                          ACC[q][:, :]).then_inc(s.moe_out, 1)

        @block.tensor
        def _(pe):
            mm = nc.tensor.matmul

            def tokens_across(s, n):
                for g in range(4):
                    t, h = g // 2, g % 2
                    pe.wait_ge(s.hn_ready, NT * n + t + 1)
                    for c in range(SUB):
                        last = nc.tensor.transpose(bank[2 + g][:, P * c:P * (c + 1)],
                                                   by_chunk(t, h, c), ident[:, :])
                    last.then_inc(s.ht_psum, 1)

            def scores(layer, j):
                s = layers[layer]
                banks = [bank[2 + 2 * (j % 2) + m] for m in range(2)]
                if layer == 0:
                    cq, ck = (j, A_HEADS + j) if j < A_HEADS else (4 + j, 8 + j)
                else:
                    cq, ck = j, JOBS + j
                if j >= 2:
                    pe.wait_ge(s.exp_done, 2 * (j - 1))
                if is_b(layer, j):
                    for m in range(2):
                        r = slice(HD * m, HD * (m + 1))
                        mm(banks[m][:, 0:T], qkT[r, ck, 0:P], qkT[r, cq, 0:T], start=True,
                           stop=False, skip_group_check=True)
                    for m in range(2):
                        r = slice(HD * m, HD * (m + 1))
                        mm(banks[m][:, T:SW], qkT[r, ck, P:T], qkT[r, cq, P:T], start=False,
                           stop=False, skip_group_check=True).then_inc(s.scores_psum, 1)
                    return
                for m in range(2):
                    if layer == 0:
                        mm(banks[m][:, 0:SW], ident_bf[:, :], bias_a[:, j, :], start=True, stop=False,
                           skip_group_check=True)
                        continue
                    mm(banks[m][:, 0:SW], ident_bf[:, :], mask_causal[:, :], start=True, stop=False,
                       skip_group_check=True)
                    head = sel_head[:, 2 * j + m:2 * j + m + 1]
                    for i in range(NT):
                        keys = P * (i + 1)
                        mm(banks[m][:, map_cols(i)], head.to_broadcast([96, P]), cum_neg[:, 0:keys],
                           start=False, stop=False, skip_group_check=True)
                        mm(banks[m][:, map_cols(i)], cum_pos[:, P * i:P * (i + 1)],
                           head.to_broadcast([96, keys]), start=False, stop=False,
                           skip_group_check=True)
                for i in range(NT):
                    for m in range(2):
                        r = slice(HD * m, HD * (m + 1))
                        last = mm(banks[m][:, map_cols(i)], qkT[r, cq, P * i:P * (i + 1)],
                                  qkT[r, ck, 0:P * (i + 1)], start=False, stop=(i == NT - 1),
                                  skip_group_check=True)
                        if i == NT - 1:
                            last.then_inc(s.scores_psum, 1)

            def across(layer, j):
                s = layers[layer]
                n = maps_before(layer, j)
                for m in range(maps_before(layer, j + 1) - n):
                    slot = 2 * (j % 2) + m
                    pe.wait_ge(s.p_ready, n + m + 1)
                    if is_b(layer, j):
                        b, soft = bank[2 + slot], pT[:, slot, :]
                        mm(b[:, 0:SW], neg_from[:, :], soft, start=False, stop=False,
                           skip_group_check=True)
                        mm(b[:, P:T], neg_ones[:, :], soft[:, T:SW], start=False, stop=False,
                           skip_group_check=True)
                        mm(b[:, 0:SW], ident_bf[:, :], mask_strict[:, :], start=False, stop=True,
                           skip_group_check=True).then_inc(s.t_psum, 1)
                        continue
                    if j >= 1:
                        pe.wait_ge(s.pt_dve if m else s.pt_act, j)
                    for k in range(3):
                        last = nc.tensor.transpose(bank[m][:, P * k:P * (k + 1)],
                                                   probs[:, slot, P * k:P * (k + 1)], ident[:, :])
                    last.then_inc(s.t_psum, 1)

            def weighted_values(layer, j):
                s = layers[layer]
                if is_b(layer, j):
                    pe.wait_ge(s.exp_done, 2 * j + 2)
                else:
                    pe.wait_ge(s.pt_act, j + 1)
                    if layer == 1:
                        pe.wait_ge(s.pt_dve, j + 1)
                if j >= 1:
                    pe.wait_ge(s.o_ready, j)
                source = probs if is_b(layer, j) else pT
                slot = 2 * (j % 2)
                if layer == 0 and j < A_HEADS:
                    heads = [(slice(0, P), P * j, P)]
                else:
                    at = HALF + P * (j - A_HEADS) if layer == 0 else P * j
                    heads = [(slice(HD * m, HD * (m + 1)), at + HD * m, HD) for m in range(2)]
                for k in range(NT):
                    for m, (r, col, n) in enumerate(heads):
                        w = source[:, slot + m, 0:T] if k == 0 else source[:, slot + m, T:SW]
                        last = mm(O_BANK[r, P * k:T], v_sb[:, k, col:col + n], w, start=(k == 0),
                                  stop=(k == NT - 1), skip_group_check=True)
                last.then_inc(s.o_psum, 1)

            def sub_sum(s, j):
                pe.wait_ge(s.o_squared, j + 1)
                mm(SUM_BANK[0:32, 0:T], slide_all[:, 31 - j:63 - j], o_squares[:, j, :],
                   start=(j == 0), stop=(j == SUBLN - 1)).then_inc(s.o_sumsq, 1)

            pe.wait_ge(consts_made, CONSTS)
            for layer in range(LAYERS):
                s = layers[layer]
                tokens_across(s, 0)
                pe.wait_ge(s.ht_ready, 4)
                if layer == 1:
                    pe.wait_ge(forget_loaded, FORGET)
                    for c in range(NC):
                        last = mm(O_BANK[0:96, 0:T], wf3[:, c, :], hT[:, c, :], start=(c == 0),
                                  stop=(c == NC - 1))
                    last.then_inc(s.forget_psum, 1)
                normed, spreads = norm_steps[layer], 0

                def spread_roots(g0, g1):
                    for g in range(g0, g1):
                        if g >= 4:
                            pe.wait_ge(s.root_applied, g - 3)
                        for c in range(2):
                            for m in range(2):
                                k = 2 * (2 * g + c) + m
                                last = mm(bank[2 + g % 4][HD * m:HD * (m + 1), T * c:T * (c + 1)],
                                          ident[0:32, k:k + 1].to_broadcast([32, HD]),
                                          root_y[0:32, :], start=True, stop=True)
                        last.then_inc(s.root_spread, 1)

                for j in range(STEPS):
                    kind, at = PLAN[layer][j // 2]
                    u = j // 2
                    if j >= 2:
                        pe.wait_ge(s.proj_out, j - 1)
                    high, low = w_high[u % 2], w_low[u]
                    pe.wait_ge(s.w_high, 2 * u + 2)
                    pe.wait_ge(s.h_high, 2)
                    for n, (w, x_part) in enumerate(((high, h_high), (low, h_high), (high, h_low))):
                        if n == 1:
                            pe.wait_ge(s.w_low, 2 * u + 2)
                        if n == 2:
                            pe.wait_ge(s.h_low, 2)
                        for half in range(1 if kind == "v" else 2):
                            for c in range(NC):
                                if kind == "v":
                                    t = j % 2
                                    last = mm(bank[j % 2][:, :], x_part[:, c, P * t:P * (t + 1)],
                                              w[:, c, :], start=(n == 0 and c == 0),
                                              stop=(n == 2 and c == NC - 1))
                                    continue
                                col = P * (2 * (j % 2) + half)
                                last = mm(bank[j % 2][:, T * half:T * (half + 1)],
                                          w[:, c, col:col + P], x_part[:, c, :],
                                          start=(n == 0 and half == 0 and c == 0),
                                          stop=(n == 2 and c == NC - 1), skip_group_check=True)
                    last.then_inc(s.proj_psum, 1)
                    if 1 <= j <= normed:
                        pe.wait_ge(s.squared, j)
                        for half in range(2):
                            c = 2 * (j - 1) + half
                            last = mm(SUM_BANK[0:32, 0:T], slide[:, 30 - 2 * c:62 - 2 * c],
                                      squares[(j - 1) % 2][:, T * half:T * (half + 1)],
                                      start=(c == 0), stop=(c == 2 * normed - 1))
                        last.then_inc(s.sumsq_psum, 1)
                    if j >= STEPS - 2:
                        if j == STEPS - 2:
                            pe.wait_ge(s.root_done, 1)
                        upto = min(normed, spreads + 4)
                        spread_roots(spreads, upto)
                        spreads = upto
                if layer == 1:
                    pe.wait_ge(s.cum_ready, 1)
                else:
                    pe.wait_ge(tables_made, A_HEADS)
                pe.wait_ge(s.root_applied, normed)
                pe.wait_ge(s.proj_out, STEPS)
                for i in range(JOBS + 2):
                    if i < JOBS:
                        scores(layer, i)
                    if 1 <= i < JOBS + 1:
                        across(layer, i - 1)
                    if i >= 2:
                        weighted_values(layer, i - 2)
                    if layer == 0 and 3 <= i < 3 + SUBLN:
                        sub_sum(s, i - 3)
                if layer == 0:
                    pe.wait_ge(s.root_done, 2)
                    for g in range(2):
                        for c in range(2):
                            h = 2 * g + c
                            last = mm(bank[g][:, T * c:T * (c + 1)],
                                      ident[0:32, h:h + 1].to_broadcast([32, P]), root_y[0:32, :],
                                      start=True, stop=True)
                        last.then_inc(s.sub_spread, 1)
                    pe.wait_ge(s.sub_applied, 2)
                pe.wait_ge(wout_loaded, 32 * (layer + 1))
                pe.wait_ge(s.o_ready, JOBS)
                pe.wait_ge(s.exp_done, 2 * JOBS)
                for q in range(4):
                    t, h = q // 2, q % 2
                    for c in range(NC):
                        last = mm(bank[2 + q][:, :], oT[:, c, P * t:P * (t + 1)],
                                  wout_view(c // SUB)[:, c % SUB, HALF * h:HALF * (h + 1)], start=(c == 0),
                                  stop=(c == NC - 1))
                    last.then_inc(s.out_psum, 1)

                tokens_across(s, 1)
                pe.wait_ge(s.ht_ready, 8)
                if layer == 0:
                    pe.wait_ge(router_loaded, ROUTER)
                for i in range(NT):
                    for c in range(NC):
                        last = mm(MISC[:, NR * i:NR * (i + 1)], hT[:, c, P * i:P * (i + 1)],
                                  w_rt[:, layer, c, :], start=(c == 0), stop=(c == NC - 1))
                last.then_inc(logits_psum, 1)
                for q in range(4):
                    last = mm(ACC[q][:, :], ident[:, :],
                              x_sb[:, q // 2, HALF * (q % 2):HALF * (q % 2 + 1)], start=True,
                              stop=False, skip_group_check=True)
                pe.wait_ge(chosen, layer + 1)
                ranks = [(0, [(before_bf, 0)]), (1, [(ones_bf, 0), (before_bf, 1)]),
                         (2, [(ones_bf, 0), (ones_bf, 1)])]
                for k, terms in ranks:
                    for n, (w, t) in enumerate(terms):
                        last = mm(Y[:, N_EXPERTS * k:N_EXPERTS * (k + 1)], w[:, :], chosen_bf[:, t, :],
                                  start=(n == 0), stop=(n == len(terms) - 1))
                last.then_inc(rank_psum, 1)

                def gather():
                    for c in range(NC):
                        b = MISC if c < SUB else Y
                        k = c % SUB
                        for t in range(NT):
                            last = mm(b[:, P * k:P * (k + 1)], by_chunk(t, c // SUB, k),
                                      take[:, t, :], start=(t == 0), stop=(t == NT - 1))
                    last.then_inc(s.gathered, 1)

                def two_halves(b, left, quad, turn, units):
                    for h, u in enumerate(units):
                        slot, lap = place(turn, u)
                        pe.wait_ge(s.unit_loaded[slot], quad * (LAPS * 16)
                                   + ((WIN if slot < UNITS else 0) + 16 * (lap + 1)))
                        for k in range(SUB):
                            for half in range(2):
                                last = mm(b[SLOTS * half:SLOTS * (half + 1), :], left(h, k),
                                          expert_rhs(slot, k, half), start=(h == 0 and k == 0),
                                          stop=(h == 1 and k == SUB - 1))
                        last.then_inc(s.unit_used[slot], 1)

                pe.wait_ge(s.slots_ready, 1)
                last_quad = pe.value_load(last_quads[0:1, layer:layer + 1],
                                          min_val=N_EXPERTS // QUAD - 1,
                                          max_val=ROUNDS * N_EXPERTS // QUAD - 1)
                pe.wait_ge(s.take_ready, 1)
                gather()
                with pe.Fori(0, last_quad + 1) as quad:
                    for k in range(QUAD):
                        now, after = turns(quad, k + 1), turns(quad, k + 2)
                        pe.wait_ge(s.xt_ready, now)
                        tokens = lambda h, c: xT[:, SUB * h + c, :]
                        two_halves(GATE, tokens, quad, k, (0, 1))
                        two_halves(UP, tokens, quad, k, (2, 3))
                        pe.wait_ge(s.take_ready, after)
                        gather()
                        pe.wait_ge(s.give_ready, now)
                        pe.wait_ge(s.gate_act, now)
                        for t in range(NT):
                            last = nc.tensor.transpose(GATE[:, P * t:P * (t + 1)], give[:, t, :],
                                                       ident[:, :])
                        last.then_inc(s.giveT_psum, 1)
                        pe.wait_ge(s.hid_ready, now)
                        pe.wait_ge(s.xt_ready, after)
                        for c in range(SUB):
                            part = hid.rearrange("p (q s) -> p s q", s=SUB)[:, c, :]
                            last = nc.tensor.transpose(MISC[:, P * c:P * (c + 1)], part, ident[:, :])
                        last.then_inc(s.hidT_psum, 1)
                        pe.wait_ge(s.hidT_ready, now)
                        two_halves(Y, lambda h, c: hidT[:, c, SLOTS * h:SLOTS * (h + 1)], quad, k,
                                   (4, 5))
                        pe.wait_ge(s.y_ready, now)
                        pe.wait_ge(s.giveT_ready, now)
                        for t in range(NT):
                            for half in range(2):
                                r = slice(SLOTS * half, SLOTS * (half + 1))
                                last = mm(ACC[2 * t + half][:, :], giveT[r, P * t:P * (t + 1)],
                                          y_sb[r, :], start=False, stop=False,
                                          skip_group_check=True)
                        last.then_inc(s.scattered, 1)


INPUTS = ["x", "norm_mix_g", "norm_ffn_g", "ab_w_in", "a_q_gain", "a_k_gain", "a_lam_q1", "a_lam_k1",
          "a_lam_q2", "a_lam_k2", "a_subln_g", "ab_w_out", "c_w_in", "c_b_f", "c_q_gain", "c_k_gain",
          "c_w_out", "moe_w_group", "moe_b_group", "moe_w_router", "moe_b_router", "moe_w_gate",
          "moe_w_up", "moe_w_down"]


def kernel(**inputs):
    import numpy as np
    from concourse import bacc
    from concourse.bass_utils import run_bass_kernel_spmd

    nc = bacc.Bacc("TRN2", target_bir_lowering=False, num_devices=1)
    arrays, args = {}, []
    for name in INPUTS:
        a = np.ascontiguousarray(inputs[name])
        arrays[f"in_{name}"] = a
        args.append(nc.dram_tensor(f"in_{name}", a.shape, mybir.dt.from_np(a.dtype),
                                   kind="ExternalInput").ap())
    args.append(nc.dram_tensor("out_0", (1, T, D), F32, kind="ExternalOutput").ap())
    trunk(nc, *args)
    r = run_bass_kernel_spmd(nc, [arrays], core_ids=[0])
    return r.results[0]["out_0"]
```

```python
import math
from contextlib import ExitStack

import concourse.bass as bass
from concourse import mybir

F32 = mybir.dt.float32
F32R = mybir.dt.float32r
BF16 = mybir.dt.bfloat16
I32 = mybir.dt.int32
ALU = mybir.AluOpType
ACT = mybir.ActivationFunctionType
AX_X = mybir.AxisListType.X

P = 128
D = 1024
T = 256
NT = T // P
NC = D // P
HALF = D // 2
SUB = NC // 2
COLS = 512
UNITS = 6
UNIT = SUB * D
HD = 64
A_HEADS, B_HEADS, C_HEADS = 4, 8, 16
JOBS = 8
N_GROUPS, PER_GROUP = 4, 4
N_EXPERTS = N_GROUPS * PER_GROUP
NR = N_GROUPS + N_EXPERTS
RING = 8
SPARE = RING
QUAD = 4
QUAD_UNITS = QUAD * UNITS
PLACES = [(SPARE, 0) if i == RING else ((i - (i > RING)) % RING, (i - (i > RING)) // RING)
          for i in range(QUAD_UNITS)]
USES = [sum(1 for s, _ in PLACES if s == slot) for slot in range(RING + 1)]
SLOTS = 64
ROUNDS = T // SLOTS
EPS = 1e-6
NEG = -1e30
SW = 3 * P
LAYERS = 2
LAM_INIT = 0.8 - 0.6 * math.exp(-0.3 * 0)
STEPS = 2 * UNITS
SCALE = HD ** -0.5

EVEN_UNITS = [("norm", 0), ("norm", 4), ("v", 0), ("scaled", 8), ("plain", 12), ("v", HALF)]
ODD_UNITS = [("norm", 0), ("norm", 4), ("norm", 8), ("norm", 12), ("v", 0), ("v", HALF)]
PLAN = [EVEN_UNITS, ODD_UNITS]

class LayerSignals:

    def __init__(self, nc, ctx, layer):
        def sem(name):
            return ctx.enter_context(nc.semaphore(f"{name}_{layer}"))

        self.squares_summed = sem("squares_summed")
        self.rsq_in = sem("rsq_in")
        self.rsq_guess = sem("rsq_guess")
        self.hn_ready = sem("hn_ready")
        self.ht_psum = sem("ht_psum")
        self.ht_ready = sem("ht_ready")
        self.h_high = sem("h_high")
        self.h_low = sem("h_low")
        self.w_high = sem("w_high")
        self.w_low = sem("w_low")
        self.proj_psum = sem("proj_psum")
        self.proj_out = sem("proj_out")
        self.squared = sem("squared")
        self.sumsq_psum = sem("sumsq_psum")
        self.root_done = sem("root_done")
        self.root_spread = sem("root_spread")
        self.root_applied = sem("root_applied")
        self.scores_psum = sem("scores_psum")
        self.max_ready = sem("max_ready")
        self.exp_done = sem("exp_done")
        self.p_ready = sem("p_ready")
        self.t_psum = sem("t_psum")
        self.pt_act = sem("pt_act")
        self.o_psum = sem("o_psum")
        self.o_ready = sem("o_ready")
        self.out_psum = sem("out_psum")
        self.x_mixed = sem("x_mixed")
        self.slots_ready = sem("slots_ready")
        self.take_ready = sem("take_ready")
        self.gathered = sem("gathered")
        self.xt_ready = sem("xt_ready")
        self.gate_exp = sem("gate_exp")
        self.gate_plus = sem("gate_plus")
        self.gate_inv = sem("gate_inv")
        self.gate_act = sem("gate_act")
        self.hid_ready = sem("hid_ready")
        self.give_ready = sem("give_ready")
        self.giveT_psum = sem("giveT_psum")
        self.giveT_ready = sem("giveT_ready")
        self.hidT_psum = sem("hidT_psum")
        self.hidT_ready = sem("hidT_ready")
        self.y_ready = sem("y_ready")
        self.scattered = sem("scattered")
        self.moe_out = sem("moe_out")
        self.unit_loaded = [sem(f"unit_loaded{u}") for u in range(RING + 1)]
        self.unit_used = [sem(f"unit_used{u}") for u in range(RING + 1)]
        if layer % 2 == 0:
            self.b_ln = sem("b_ln")
            self.o_squared = sem("o_squared")
            self.o_sumsq = sem("o_sumsq")
            self.sub_spread = sem("sub_spread")
            self.sub_applied = sem("sub_applied")
        else:
            self.pt_dve = sem("pt_dve")
            self.forget_psum = sem("forget_psum")
            self.forget_abs = sem("forget_abs")
            self.forget_ln = sem("forget_ln")
            self.cum_ready = sem("cum_ready")


def trunk(nc, x, norm_mix_g, norm_ffn_g, ab_w_in, a_q_gain, a_k_gain, a_lam_q1, a_lam_k1, a_lam_q2,
          a_lam_k2, a_subln_g, ab_w_out, c_w_in, c_b_f, c_q_gain, c_k_gain, c_w_out, moe_w_group,
          moe_b_group, moe_w_router, moe_b_router, moe_w_gate, moe_w_up, moe_w_down, out):
    with ExitStack() as ctx:
        def sb(name, shape, dt=F32):
            return ctx.enter_context(nc.sbuf_tensor(name, shape, dt))

        def sem(name):
            return ctx.enter_context(nc.semaphore(name))

        def rounded(name, shape, at):
            return nc.alloc_sbuf_tensor_at(name, shape, F32R, offset=at)

        ring, ring_at = [], []
        for slot in range(RING):
            ring.append(sb(f"ring{slot}", [P, UNIT]))
            ring_at.append(nc.sbuf_base - 4 * UNIT)
        x_sb = sb("x_sb", [P, NT, D])
        hn = sb("hn", [P, NT, D])
        oT = hn[:, :, :].rearrange("p a (b t) -> p (a b) t", t=T)
        hn_at = nc.sbuf_base - 4 * NT * D
        hT = sb("hT", [P, NC, T])
        hT_at = nc.sbuf_base - 4 * NC * T
        assert hT_at - hn_at == 4 * NT * D and 4 * (NT * D + NC * T) == 4 * UNIT
        ring.append(nc.alloc_sbuf_tensor_at("ring_spare", [P, UNIT], F32, offset=hn_at))
        h_high = rounded("h_high", [P, NC, T], hn_at)
        h_low = rounded("h_low", [P, NC, T], hT_at)
        w_low = [rounded(f"w_low{u}", [P, NC, COLS], ring_at[u]) for u in range(UNITS)]
        w_high = [rounded(f"w_high{i}", [P, NC, COLS], ring_at[UNITS + i])
                  for i in range(RING - UNITS)]
        o_squares = hT[:, 0:A_HEADS, :]
        qkT = sb("qkT", [P, 16, T])
        v_sb = sb("v_sb", [P, NT, D])
        attention = sb("attention", [P, 8, SW])
        probs = attention[:, 0:4, :]
        pT = attention[:, 4:8, :]
        pT_flat = pT.rearrange("p a b -> p (a b)")
        fn = attention[:, :, :].rearrange("p a b -> p (a b)")[:, 0:NT * D].rearrange(
            "p (t d) -> p t d", t=NT)
        squares = [pT_flat[:, COLS * i:COLS * (i + 1)] for i in range(2)]
        probs_flat = probs.rearrange("p a b -> p (a b)")
        ident = sb("ident", [P, P])
        ident_bf = sb("ident_bf", [P, P], BF16)
        ones_bf = sb("ones_bf", [P, P], BF16)
        before_bf = sb("before_bf", [P, P], BF16)
        neg_from = sb("neg_from", [P, P])
        neg_ones = sb("neg_ones", [P, P])
        strict = sb("strict", [P, P])
        mask_causal = sb("mask_causal", [P, SW], BF16)
        mask_strict = sb("mask_strict", [P, SW], BF16)
        dist = probs_flat[:, 0:SW]
        bias_a = sb("bias_a", [P, A_HEADS, SW], BF16)
        slide = sb("slide", [P, 126])
        slide_all = sb("slide_all", [P, 64])
        sel_head = sb("sel_head", [96, 32], BF16)
        slot_id = sb("slot_id", [P, 2, SLOTS])
        desc4 = sb("desc4", [P, 4])
        gain_mix = sb("gain_mix", [P, LAYERS, NC])
        gain_ffn = sb("gain_ffn", [P, LAYERS, NC])
        g_qk = sb("g_qk", [P, LAYERS, 2])
        g_sub = sb("g_sub", [P, 1])
        lam_in = probs_flat[:, SW:SW + 4 * HD].rearrange("p (a b) -> p a b", a=4)
        lam_prod = probs_flat[:, SW + 4 * HD:SW + 6 * HD].rearrange("p (a b) -> p a b", a=2)
        lam_s = sb("lam_s", [P, 4])
        neg_lam = sb("neg_lam", [P, 1])
        wf3 = sb("wf3", [P, NC, 96])
        b_f = sb("b_f", [96, 1])
        w_rt = sb("w_rt", [P, LAYERS, NC, NR])
        b_rt = sb("b_rt", [P, LAYERS, NR])
        ssq = sb("ssq", [P, NT])
        root_x = sb("root_x", [P, T])
        root_ln = sb("root_ln", [P, T])
        root_y = sb("root_y", [P, T])
        root_t = root_ln
        nmax = sb("nmax", [P, 2, 4])
        rsum = sb("rsum", [P, 2, 4])
        rinv = sb("rinv", [P, 2, 4])
        forget = [probs_flat[0:96, T * i:T * (i + 1)] for i in range(5)]
        root_parts = probs_flat[0:96, 5 * T:5 * T + T // 2].bitcast(BF16)
        cum = [sb(f"cum{i}", [96, T], BF16) for i in range(3)]
        cum_pos = sb("cum_pos", [96, T], BF16)
        cum_neg = sb("cum_neg", [96, T], BF16)
        v_flat = v_sb[:, :, :].rearrange("p a b -> p (a b)")
        lg = v_flat[:, 0:NT * NR].rearrange("p (t n) -> p t n", t=NT)
        rt = v_flat[:, 64:64 + 14 * NT * 4].rearrange("p (k t n) -> p k t n", k=14, t=NT)
        picked = v_flat[:, 192:224].rearrange("p (t g e) -> p t g e", t=NT, g=N_GROUPS)
        chosen_f = v_flat[:, 224:256].rearrange("p (t e) -> p t e", t=NT)
        weight_of = v_flat[:, 256:256 + NT * (ROUNDS * N_EXPERTS + 1)].rearrange("p (t e) -> p t e", t=NT)
        chosen_bf = sb("chosen_bf", [P, NT, N_EXPERTS], BF16)
        most = sb("most", [P, 2])
        slot_of = sb("slot_of", [P, NT, ROUNDS * N_EXPERTS + 1])
        last_quads = sb("last_quads", [P, LAYERS], I32)
        qk_flat = qkT[:, :, :].rearrange("p a b -> p (a b)")
        xT = qk_flat[:, 0:512].rearrange("p (c s) -> p c s", c=NC)
        take = qk_flat[:, 512:768].rearrange("p (t s) -> p t s", t=NT)
        give = qk_flat[:, 768:1024].rearrange("p (t s) -> p t s", t=NT)
        giveT = qk_flat[:, 1024:1280]
        gate_e = qk_flat[:, 1536:2048]
        sig = qk_flat[:, 2048:2560]
        hid = qk_flat[:, 2560:3072]
        hidT = qk_flat[:, 3072:3584].rearrange("p (s t) -> p s t", s=SUB)
        y_sb = qk_flat[:, 3584:4096]

        bank = [ctx.enter_context(nc.psum_tensor(f"bank{i}", [P, COLS], F32)) for i in range(8)]
        ACC, GATE, UP, Y, MISC = bank[0:4], bank[4], bank[5], bank[6], bank[7]
        O_BANK, SUM_BANK = bank[6], bank[7]

        pool_step = sem("pool_step")
        consts_made = sem("consts_made")
        act_step = sem("act_step")
        dve_step = sem("dve_step")
        x_loaded = sem("x_loaded")
        gains_loaded = sem("gains_loaded")
        params_loaded = sem("params_loaded")
        router_loaded = sem("router_loaded")
        forget_loaded = sem("forget_loaded")
        forget_zeroed = sem("forget_zeroed")
        tables_made = sem("tables_made")
        lam_sums = sem("lam_sums")
        lam_exp = sem("lam_exp")
        out_stored = sem("out_stored")
        wout_loaded = sem("wout_loaded")
        logits_psum = sem("logits_psum")
        rt_shift = sem("rt_shift")
        rt_exp = sem("rt_exp")
        rt_gap = sem("rt_gap")
        rt_gap_exp = sem("rt_gap_exp")
        chosen = sem("chosen")
        rank_psum = sem("rank_psum")
        layers = []
        for i in range(LAYERS):
            layers.append(LayerSignals(nc, ctx, i))
        CONSTS = 20
        GAINS, PARAMS = 16 * 8, 16 * 13
        ROUTER, FORGET, WIN = 16 * 12, 16 * 9, 16 * 2

        w_in = [ab_w_in[0], c_w_in[0]]
        w_out = [ab_w_out[0], c_w_out[0]]
        norm_steps = [sum(2 for k, _ in units if k == "norm") for units in PLAN]
        SUBLN = 4

        def is_b(layer, job):
            return layer == 0 and job >= A_HEADS

        def score_banks(layer, j):
            first = (2, 4, 0)[(j - A_HEADS) % 3] if is_b(layer, j) else 2 + 2 * (j % 2)
            return bank[first:first + 2]

        def rows(w):
            return w.rearrange("(h p s) n -> h p s n", h=2, s=SUB)

        def whole(layer, u):
            return layer == 0 and u == 0

        def split(layer, u):
            return u if layer == 0 else u + 1

        def win_view(u):
            return ring[u][:, :].rearrange("p (c n) -> p c n", c=NC)

        def wout_view(h):
            return ring[UNITS + h][:, :].rearrange("p (c n) -> p c n", n=D)

        def expert_rhs(u, s, half):
            return ring[u][:, s * D + HALF * half:s * D + HALF * (half + 1)]

        def maps_before(layer, job):
            return job + max(0, job - A_HEADS) if layer == 0 else 2 * job

        def roots_before(layer, which):
            names = ("mix", "qk") + (("sub",) if layer == 0 else ()) + ("ffn0", "ffn1")
            return names.index(which) + 1

        def place(k, u):
            return PLACES[UNITS * k + u]

        def turns(quad, k):
            return quad * QUAD + k

        def used(s, quad, k, u):
            slot, lap = place(k, u)
            return s.unit_used[slot], quad * USES[slot] + (lap + 1)

        def spread_by(layer, j):
            groups, first = norm_steps[layer], max(norm_steps[layer] + 2, STEPS - norm_steps[layer])
            return max(0, -(-groups * (j - first + 1) // (STEPS - first)))

        def spread(column, shape):
            return column.to_broadcast(shape)

        def by_chunk(normed, t, h, s):
            return normed[:, t, HALF * h:HALF * (h + 1)].rearrange("p (q s) -> p s q", s=SUB)[:, s, :]

        def gains(table, layer, h, n):
            g = table[:, layer, SUB * h:SUB * (h + 1)]
            return g.rearrange("p (c a) -> p c a", a=1).to_broadcast([P, SUB, n])

        def map_cols(i):
            return slice(0, P) if i == 0 else slice(P, SW)

        block = ctx.enter_context(nc.Block())

        @block.sync
        def _(sp):
            for t in range(NT):
                sp.dma_start(x_sb[:, t, :], x[0, t * P:(t + 1) * P, :]).then_inc(x_loaded, 16)

            def load(dst, src, signal):
                sp.dma_start(dst, src).then_inc(signal, 16)

            def load_win(layer, u):
                for h in range(2):
                    sp.dma_start(win_view(u)[:, SUB * h:SUB * (h + 1), :],
                                 rows(w_in[layer])[h, :, :, COLS * u:COLS * (u + 1)]
                                 ).then_inc(layers[layer].unit_loaded[u], 16)

            def load_wout(layer):
                for h in range(2):
                    sp.dma_start(wout_view(h), w_out[layer].rearrange("(h c p) n -> h p c n", h=2,
                                                                      p=P)[h]
                                 ).then_inc(wout_loaded, 16)

            def load_unit(layer, slot, u, e):
                w = (moe_w_gate, moe_w_up, moe_w_down)[u // 2][layer]
                src = w[bass.ds(e, 1)].rearrange("e (h p s) n -> (e h) p (s n)", h=2, s=SUB)[u % 2]
                sp.dma_start(ring[slot][:, :], src).then_inc(layers[layer].unit_loaded[slot], 16)

            for i in range(LAYERS):
                for g, dst in ((norm_mix_g, gain_mix), (norm_ffn_g, gain_ffn)):
                    for h in range(2):
                        load(dst[:, i, SUB * h:SUB * (h + 1)],
                             g[i].rearrange("(h p s) -> h p s", h=2, s=SUB)[h], gains_loaded)
            for u in range(UNITS):
                load_win(0, u)
            for i, (q, k) in enumerate(((a_q_gain, a_k_gain), (c_q_gain, c_k_gain))):
                for j, g in enumerate((q, k)):
                    for m in range(2):
                        load(g_qk[HD * m:HD * (m + 1), i, j:j + 1],
                             g[0].rearrange("(p a) -> p a", a=1), params_loaded)
            load(g_sub[:, :], a_subln_g[0].rearrange("(p a) -> p a", a=1), params_loaded)
            for j, g in enumerate((a_lam_q1, a_lam_k1, a_lam_q2, a_lam_k2)):
                load(lam_in[:, j, :], g[0].partition_broadcast(P), params_loaded)
            for i in range(LAYERS):
                load(b_rt[:, i, 0:N_GROUPS], moe_b_group[i].partition_broadcast(P), router_loaded)
                load(b_rt[:, i, N_GROUPS:NR], moe_b_router[i].partition_broadcast(P), router_loaded)
                for w, c, n in ((moe_w_group, 0, N_GROUPS), (moe_w_router, N_GROUPS, N_EXPERTS)):
                    for h in range(2):
                        load(w_rt[:, i, SUB * h:SUB * (h + 1), c:c + n], rows(w[i])[h],
                             router_loaded)
            sp.wait_ge(forget_zeroed, 2)
            for g in range(3):
                load(b_f[32 * g:32 * g + C_HEADS, :], c_b_f[0].rearrange("(p a) -> p a", a=1),
                     forget_loaded)
                for h in range(2):
                    load(wf3[:, SUB * h:SUB * (h + 1), 32 * g:32 * g + C_HEADS],
                         rows(c_w_in[0])[h, :, :, 3 * D:3 * D + C_HEADS], forget_loaded)
            for layer in range(LAYERS):
                s = layers[layer]
                for u in range(UNITS):
                    sp.wait_ge(s.proj_psum, 2 * u + 2)
                    load_unit(layer, u, u, 0)
                load_wout(layer)
                sp.wait_ge(s.out_psum, 4)
                for slot in range(UNITS, RING):
                    load_unit(layer, slot, slot - UNITS, 1)
                sp.wait_ge(logits_psum, layer + 1)
                load_unit(layer, SPARE, RING - UNITS, 1)
                sp.wait_ge(s.slots_ready, 1)
                last_quad = sp.value_load(last_quads[0:1, layer:layer + 1],
                                          min_val=N_EXPERTS // QUAD - 1,
                                          max_val=ROUNDS * N_EXPERTS // QUAD - 1)
                with sp.Fori(0, last_quad) as quad:
                    first = (quad & (N_EXPERTS // QUAD - 1)) * QUAD
                    next_first = ((quad + 1) & (N_EXPERTS // QUAD - 1)) * QUAD
                    for i in [*range(RING + 1, QUAD_UNITS), *range(RING + 1)]:
                        slot, lap = PLACES[i]
                        k, u = i // UNITS, i % UNITS
                        if i > RING:
                            sp.wait_ge(s.unit_used[slot], quad * USES[slot] + lap)
                        else:
                            sp.wait_ge(s.unit_used[slot], quad * USES[slot] + USES[slot])
                        sp.nop(nofuse=True)
                        load_unit(layer, slot, u, (first if i > RING else next_first) + k)
                for i in range(RING + 1, QUAD_UNITS):
                    slot, lap = PLACES[i]
                    sp.wait_ge(s.unit_used[slot], last_quad * USES[slot] + lap)
                    load_unit(layer, slot, i % UNITS, N_EXPERTS - QUAD + i // UNITS)
                if layer + 1 < LAYERS:
                    for u in range(UNITS):
                        sp.wait_ge(s.unit_used[u], last_quad * USES[u] + USES[u])
                        load_win(layer + 1, u)
            for q in range(4):
                sp.wait_ge(layers[-1].moe_out, q + 1)
                t, h = q // 2, q % 2
                sp.dma_start(out[0, t * P:(t + 1) * P, HALF * h:HALF * (h + 1)],
                             x_sb[:, t, HALF * h:HALF * (h + 1)]).then_inc(out_stored, 16)
            sp.wait_ge(out_stored, 64)

        @block.gpsimd
        def _(pool):
            steps = [0]

            def own(ins):
                steps[0] += 1
                ins.then_inc(pool_step, 1)
                pool.wait_ge(pool_step, steps[0])

            made_before = [0]

            def made(ins):
                made_before[0] += 1
                ins.then_inc(consts_made, 1)
                pool.wait_ge(consts_made, made_before[0])

            def select(out_ap, in_ap, pattern, cmp, base, mult, fill):
                return pool.affine_select(out=out_ap, in_=in_ap, pattern=pattern, compare_op=cmp,
                                          fill=fill, base=base, channel_multiplier=mult)

            own(pool.memset(ident[:, :], 0.0))
            made(select(ident[:, :], ident[:, :], [[-1, P]], ALU.not_equal, 0, 1, 1.0))
            own(pool.memset(ident_bf[:, :], 0.0))
            made(select(ident_bf[:, :], ident_bf[:, :], [[-1, P]], ALU.not_equal, 0, 1, 1.0))
            own(pool.memset(slide[:, :], 0.0))
            for g in range(3):
                made(pool.memset(slide[0:HD, 30 + 32 * g:31 + 32 * g], 1.0))
                made(pool.memset(slide[HD:P, 31 + 32 * g:32 + 32 * g], 1.0))
            own(pool.memset(slide_all[:, :], 0.0))
            made(pool.memset(slide_all[:, 31:32], 1.0))
            made(pool.iota(dist[:, 0:P], [[-1, P]], base=0, channel_multiplier=1,
                      allow_small_or_imprecise_dtypes=True))
            made(pool.iota(dist[:, P:SW], [[-1, T]], base=P, channel_multiplier=1,
                      allow_small_or_imprecise_dtypes=True))
            own(pool.memset(mask_causal[:, :], 0.0))
            made(select(mask_causal[:, 0:P], mask_causal[:, 0:P], [[-1, P]], ALU.is_ge, 0, 1, NEG))
            made(select(mask_causal[:, 2 * P:SW], mask_causal[:, 2 * P:SW], [[-1, P]], ALU.is_ge, 0, 1,
                   NEG))
            own(pool.memset(mask_strict[:, :], 0.0))
            made(select(mask_strict[:, 0:P], mask_strict[:, 0:P], [[1, P]], ALU.is_gt, 0, -1, NEG))
            made(select(mask_strict[:, 2 * P:SW], mask_strict[:, 2 * P:SW], [[1, P]], ALU.is_gt, 0, -1,
                   NEG))
            own(pool.memset(neg_ones[:, :], -1.0))
            made(select(neg_from[:, :], neg_ones[:, :], [[-1, P]], ALU.is_ge, 0, 1, 0.0))
            own(pool.memset(ones_bf[:, :], 1.0))
            made(select(before_bf[:, :], ones_bf[:, :], [[1, P]], ALU.is_gt, 0, -1, 0.0))
            made(select(strict[:, :], ones_bf[:, :], [[1, P]], ALU.is_gt, 0, -1, 0.0))
            made(pool.iota(slot_id[:, :, :], [[0, 2], [1, SLOTS]], base=0, channel_multiplier=0,
                      allow_small_or_imprecise_dtypes=True))
            own(pool.memset(sel_head[:, :], 0.0))
            for g in range(3):
                part = sel_head[32 * g:32 * (g + 1), :]
                last = select(part, part, [[-1, 32]], ALU.not_equal, 0, 1, 1.0)
                own(last)
            made(pool.iota(desc4[:, :], [[-1, 4]], base=4, channel_multiplier=0,
                      allow_small_or_imprecise_dtypes=True))

        @block.scalar
        def _(act):
            act.preload_act_table_set("natural_log_exp_and_others")

            steps = [0]

            def own(ins):
                steps[0] += 1
                ins.then_inc(act_step, 1)
                act.wait_ge(act_step, steps[0])

            def sum_squares(s, t):
                act.activation(qk_flat[:, D * t:D * (t + 1)], x_sb[:, t, :], ACT.Square,
                               accum_out=ssq[:, t:t + 1]).then_inc(s.squares_summed, 1)

            def weights_high(s, u):
                act.wait_ge(s.unit_loaded[u], WIN)
                if u >= 2:
                    act.wait_ge(s.proj_psum, 2 * (u - 1))
                for h in range(2):
                    part = slice(SUB * h, SUB * (h + 1))
                    act.activation(w_high[u % 2][:, part, :], win_view(u)[:, part, :],
                                   ACT.Copy).then_inc(s.w_high, 1)

            def root_guess(s, n, r, c0, c1):
                act.wait_ge(s.rsq_in, n)
                own(act.activation(root_ln[0:r, c0:c1], root_x[0:r, c0:c1], ACT.Ln))
                act.activation(root_y[0:r, c0:c1], root_ln[0:r, c0:c1], ACT.Exp, scale=-0.5
                               ).then_inc(s.rsq_guess, 1)

            def slots_free(layer, j):
                s = layers[layer]
                if j >= 2 and is_b(layer, j - 2):
                    act.wait_ge(s.o_psum, j - 1)
                elif j >= 2:
                    act.wait_ge(s.t_psum, maps_before(layer, j - 1))

            def exponentials(layer, j):
                s = layers[layer]
                banks = score_banks(layer, j)
                if is_b(layer, j):
                    if j >= 2 and is_b(layer, j - 2):
                        act.wait_ge(s.t_psum, maps_before(layer, j - 1))
                    elif j >= 2:
                        act.wait_ge(s.o_psum, j - 1)
                    z = pT[:, 2 * (j % 2):2 * (j % 2) + 2, :]
                    for m in range(2):
                        act.wait_ge(s.scores_psum, 2 * j + m + 1)
                        last = act.activation(z[:, m, :], banks[m][:, 0:SW], ACT.Abs)
                    own(last)
                    own(act.activation(z, z, ACT.Exp, scale=-1.0))
                    act.activation(z, z, ACT.Ln, bias=1.0).then_inc(s.b_ln, 1)
                    return
                for m in range(2):
                    slot = 2 * (j % 2) + m
                    act.wait_ge(s.max_ready, 2 * j + m + 1)
                    if m == 0:
                        slots_free(layer, j)
                    b = banks[m]
                    for i in range(NT):
                        k = 2 * m + i
                        last = act.activation(probs[:, slot, map_cols(i)], b[:, map_cols(i)], ACT.Exp,
                                              bias=nmax[:, j % 2, k:k + 1],
                                              accum_out=rsum[:, j % 2, k:k + 1])
                    last.then_inc(s.exp_done, 1)

            def second(layer, j):
                s = layers[layer]
                if is_b(layer, j):
                    slots_free(layer, j)
                    for m in range(2):
                        slot = 2 * (j % 2) + m
                        act.wait_ge(s.t_psum, maps_before(layer, j) + m + 1)
                        act.activation(probs[:, slot, :], score_banks(layer, j)[m][:, 0:SW], ACT.Exp
                                       ).then_inc(s.exp_done, 1)
                    return
                act.wait_ge(s.t_psum, maps_before(layer, j) + 1)
                if j >= 2:
                    act.wait_ge(s.o_psum, j - 1)
                act.activation(pT[:, 2 * (j % 2), :], bank[0][:, 0:SW], ACT.Copy).then_inc(s.pt_act, 1)

            def output(layer, j):
                s = layers[layer]
                act.wait_ge(s.o_psum, j + 1)
                act.activation(oT[:, j, :], O_BANK[:, 0:T], ACT.Copy).then_inc(s.o_ready, 1)
                if layer == 0 and j < A_HEADS:
                    act.wait_ge(s.o_ready, j + 1)
                    act.activation(o_squares[:, j, :], oT[:, j, :], ACT.Square
                                   ).then_inc(s.o_squared, 1)

            for layer in range(LAYERS):
                s = layers[layer]
                for t in range(NT):
                    if layer == 0:
                        act.wait_ge(x_loaded, 16 * NT)
                    else:
                        act.wait_ge(layers[layer - 1].moe_out, 2 * (t + 1))
                    sum_squares(s, t)
                root_guess(s, roots_before(layer, "mix"), P, 0, NT)
                if not whole(layer, 0):
                    weights_high(s, 0)
                act.wait_ge(s.ht_psum, 4)
                act.wait_ge(s.ht_ready, 4)
                for h in range(2):
                    part = slice(SUB * h, SUB * (h + 1))
                    act.activation(h_high[:, part, :], hT[:, part, :], ACT.Copy
                                   ).then_inc(s.h_high, 1)
                done = 0
                for j in range(STEPS):
                    kind, first = PLAN[layer][j // 2]
                    if j % 2 == 0 and j // 2 + 1 < UNITS:
                        weights_high(s, j // 2 + 1)
                    if kind == "norm":
                        act.wait_ge(s.proj_out, j + 1)
                        if done >= 2:
                            act.wait_ge(s.sumsq_psum, done - 1)
                        c = first + 2 * (j % 2)
                        act.activation(squares[done % 2],
                                       qkT[:, c:c + 2, :].rearrange("p a b -> p (a b)"), ACT.Square
                                       ).then_inc(s.squared, 1)
                        done += 1
                    if j == 1 and layer == 1:
                        act.wait_ge(s.forget_abs, 1)
                        own(act.activation(forget[2], forget[1], ACT.Exp, scale=-1.0))
                        act.activation(forget[3], forget[2], ACT.Ln, bias=1.0
                                       ).then_inc(s.forget_ln, 1)
                    if j == norm_steps[layer]:
                        root_guess(s, roots_before(layer, "qk"), 96, 0, T)
                        if layer == 0:
                            act.wait_ge(lam_sums, 1)
                            act.activation(lam_s[:, 2:4], lam_s[:, 0:2], ACT.Exp).then_inc(lam_exp, 1)
                for i in range(JOBS + 2):
                    if i < JOBS:
                        exponentials(layer, i)
                    if 1 <= i < JOBS + 1:
                        second(layer, i - 1)
                    if i >= 2:
                        output(layer, i - 2)
                    if layer == 0 and i == JOBS:
                        root_guess(s, roots_before(layer, "sub"), 32, 0, T)
                for t in range(NT):
                    act.wait_ge(s.x_mixed, 2 * (t + 1))
                    sum_squares(s, t)
                    root_guess(s, roots_before(layer, f"ffn{t}"), P, t, t + 1)
                act.wait_ge(rt_shift, layer + 1)
                act.activation(rt[:, 2], rt[:, 1], ACT.Exp).then_inc(rt_exp, 1)
                act.wait_ge(rt_gap, layer + 1)
                act.activation(rt[:, 12, :, 1:2], rt[:, 12, :, 0:1], ACT.Exp).then_inc(rt_gap_exp, 1)
                act.wait_ge(s.slots_ready, 1)
                last_quad = act.value_load(last_quads[0:1, layer:layer + 1],
                                          min_val=N_EXPERTS // QUAD - 1,
                                          max_val=ROUNDS * N_EXPERTS // QUAD - 1)
                with act.Fori(0, last_quad + 1) as quad:
                    for k in range(QUAD):
                        act.wait_ge(*used(s, quad, k, 1))
                        act.activation(gate_e, GATE[:, :], ACT.Exp, scale=-1.0).then_inc(s.gate_exp, 1)
                        act.wait_ge(s.giveT_psum, turns(quad, k + 1))
                        act.activation(giveT, GATE[:, 0:T], ACT.Copy).then_inc(s.giveT_ready, 1)
                        act.wait_ge(*used(s, quad, k, 5))
                        act.activation(y_sb, Y[:, :], ACT.Copy).then_inc(s.y_ready, 1)


        @block.vector
        def _(dve):
            steps = [0]

            def own(ins):
                steps[0] += 1
                ins.then_inc(dve_step, 1)
                dve.wait_ge(dve_step, steps[0])

            ts, tt, stt = nc.vector.tensor_scalar, nc.vector.tensor_tensor, nc.vector.scalar_tensor_tensor

            def root(s, n, src, r, c0, c1, count):
                xs, ys, tmp = root_x[0:r, c0:c1], root_y[0:r, c0:c1], root_t[0:r, c0:c1]
                ts(xs, src, 1.0 / count, EPS, ALU.mult, ALU.add).then_inc(s.rsq_in, 1)
                dve.wait_ge(s.rsq_guess, n)
                own(stt(tmp, xs, -0.5, ys, ALU.mult, ALU.mult))
                own(tt(tmp, tmp, ys, ALU.mult))
                return stt(ys, tmp, 1.5, ys, ALU.add, ALU.mult)

            def leave_transposed(layer, n, table, groups, first_bank):
                s = layers[layer]
                for g in groups:
                    t, h = g // 2, g % 2
                    dve.wait_ge(s.ht_psum, 4 * n + g + 1)
                    tt(hT[:, SUB * h:SUB * (h + 1), P * t:P * (t + 1)],
                       bank[first_bank + g][:, :].rearrange("p (c t) -> p c t", c=SUB),
                       gains(table, layer, h, P), ALU.mult).then_inc(s.ht_ready, 1)

            def mix_norm(layer):
                s = layers[layer]
                dve.wait_ge(s.squares_summed, NT)
                own(root(s, roots_before(layer, "mix"), ssq[:, :], P, 0, NT, D))
                for t in range(NT):
                    ts(hn[:, t, :], x_sb[:, t, :], root_y[:, t:t + 1], None, ALU.mult
                       ).then_inc(s.hn_ready, 1)
                if layer == 0:
                    dve.wait_ge(gains_loaded, GAINS)
                leave_transposed(layer, 0, gain_mix, range(4), 2)

            def mixed_and_normed(layer):
                s = layers[layer]

                def add(q):
                    dve.wait_ge(s.out_psum, q + 1)
                    xq = x_sb[:, q // 2, HALF * (q % 2):HALF * (q % 2 + 1)]
                    tt(xq, bank[2 + q][:, :], xq, ALU.add).then_inc(s.x_mixed, 1)

                def norm(t):
                    dve.wait_ge(s.squares_summed, NT + t + 1)
                    own(root(s, roots_before(layer, f"ffn{t}"), ssq[:, t:t + 1], P, t, t + 1, D))
                    ts(fn[:, t, :], x_sb[:, t, :], root_y[:, t:t + 1], None, ALU.mult
                       ).then_inc(s.hn_ready, 1)

                add(0)
                add(1)
                norm(0)
                add(2)
                leave_transposed(layer, 1, gain_ffn, (0, 1), 0)
                add(3)
                norm(1)
                leave_transposed(layer, 1, gain_ffn, (2, 3), 0)

            def make_tables():
                dve.wait_ge(params_loaded, PARAMS)
                dve.wait_ge(consts_made, CONSTS)
                own(ts(g_qk[:, :, 0:1], g_qk[:, :, 0:1], SCALE, None, ALU.mult))
                own(ts(g_sub[:, :], g_sub[:, :], 1.0 - LAM_INIT, None, ALU.mult))
                for m in range(2):
                    last = tt(lam_prod[:, m, :], lam_in[:, 2 * m, :], lam_in[:, 2 * m + 1, :], ALU.mult)
                own(last)
                nc.vector.tensor_reduce(lam_s[:, 0:2], lam_prod, AX_X, ALU.add).then_inc(lam_sums, 1)
                for h in range(A_HEADS):
                    slope = 2.0 ** (-8.0 * (h + 1) / A_HEADS)
                    stt(bias_a[:, h, :], dist, -slope, mask_causal[:, :], ALU.mult, ALU.add
                        ).then_inc(tables_made, 1)
                dve.wait_ge(lam_exp, 1)
                own(tt(neg_lam[:, :], lam_s[:, 3:4], lam_s[:, 2:3], ALU.subtract))
                own(ts(neg_lam[:, :], neg_lam[:, :], -LAM_INIT, None, ALU.add))

            def first(layer, j):
                s = layers[layer]
                if is_b(layer, j):
                    return
                for m in range(2):
                    slot = 2 * (j % 2) + m
                    dve.wait_ge(s.scores_psum, 2 * j + m + 1)
                    for i in range(NT):
                        k = 2 * m + i
                        last = nc.vector.tensor_reduce(nmax[:, j % 2, k:k + 1],
                                                       score_banks(layer, j)[m][:, map_cols(i)],
                                                       AX_X, ALU.max,
                                                       negate=True)
                    last.then_inc(s.max_ready, 1)

            def second(layer, j):
                s = layers[layer]
                slot = 2 * (j % 2)
                if is_b(layer, j):
                    dve.wait_ge(s.b_ln, j - A_HEADS + 1)
                    for m in range(2):
                        z = pT[:, slot + m, :]
                        own(stt(z, score_banks(layer, j)[m][:, 0:SW], 0.0, z, ALU.max, ALU.add))
                        diagonal = z.rearrange("p (b k) -> p b k", b=3)[:, 0:3:2, :]
                        tt(diagonal, diagonal,
                           strict[:, :].rearrange("p (a k) -> p a k", a=1).to_broadcast([P, 2, P]),
                           ALU.mult).then_inc(s.p_ready, 1)
                    return
                dve.wait_ge(s.exp_done, 2 * j + 2)
                own(nc.vector.reciprocal(rinv[:, j % 2, :], rsum[:, j % 2, :]))
                if layer == 0:
                    own(ts(rinv[:, j % 2, 2:4], rinv[:, j % 2, 2:4], neg_lam[:, :], None, ALU.mult))
                    for i in range(NT):
                        p1 = probs[:, slot, map_cols(i)]
                        last = ts(p1, p1, rinv[:, j % 2, i:i + 1], None, ALU.mult)
                    own(last)
                    for i in range(NT):
                        p1, p2 = probs[:, slot, map_cols(i)], probs[:, slot + 1, map_cols(i)]
                        last = stt(p1, p2, rinv[:, j % 2, 2 + i:3 + i], p1, ALU.mult, ALU.add)
                    last.then_inc(s.p_ready, 1)
                    return
                for m in range(2):
                    for i in range(NT):
                        k = 2 * m + i
                        p1 = probs[:, slot + m, map_cols(i)]
                        last = ts(p1, p1, rinv[:, j % 2, k:k + 1], None, ALU.mult)
                    last.then_inc(s.p_ready, 1)

            def third(layer, j):
                s = layers[layer]
                if layer == 0:
                    return
                dve.wait_ge(s.t_psum, maps_before(layer, j) + 2)
                if j >= 2:
                    dve.wait_ge(s.o_psum, j - 1)
                nc.vector.tensor_copy(pT[:, 2 * (j % 2) + 1, :], bank[1][:, 0:SW]).then_inc(s.pt_dve, 1)

            def tokens_low(s):
                for h in range(2):
                    part = slice(SUB * h, SUB * (h + 1))
                    dve.wait_ge(s.h_high, h + 1)
                    tt(h_low[:, part, :], hT[:, part, :], h_high[:, part, :].bitcast(F32),
                       ALU.subtract).then_inc(s.h_low, 1)

            def weights_low(layer, u):
                s = layers[layer]
                for h in range(2):
                    part = slice(SUB * h, SUB * (h + 1))
                    dve.wait_ge(s.w_high, 2 * split(layer, u) + h - 1)
                    tt(w_low[u][:, part, :], win_view(u)[:, part, :],
                       w_high[u % 2][:, part, :].bitcast(F32), ALU.subtract).then_inc(s.w_low, 1)

            def forget_gate(s):
                z, az, _, ln1, lf = forget
                dve.wait_ge(s.forget_psum, 1)
                dve.wait_ge(forget_loaded, FORGET)
                own(ts(z, O_BANK[0:96, 0:T], b_f[:, :], None, ALU.add))
                stt(az, z, -1.0, z, ALU.mult, ALU.max).then_inc(s.forget_abs, 1)
                dve.wait_ge(s.forget_ln, 1)
                own(stt(lf, z, 0.0, ln1, ALU.min, ALU.subtract))
                own(nc.vector.tensor_tensor_scan(z, ones_bf[0:96, 0:1].to_broadcast([96, T]), lf, 0.0,
                                                 ALU.mult, ALU.add))
                own(nc.vector.tensor_copy(cum[0][:, :], z))
                own(tt(z, z, cum[0][:, :], ALU.subtract))
                own(nc.vector.tensor_copy(cum[1][:, :], z))
                own(tt(z, z, cum[1][:, :], ALU.subtract))
                own(nc.vector.tensor_copy(cum[2][:, :], z))
                for g in range(3):
                    r = slice(32 * g, 32 * (g + 1))
                    nc.vector.tensor_copy(cum_pos[r, :], cum[g][r, :])
                    last = ts(cum_neg[r, :], cum[g][r, :], -1.0, None, ALU.mult)
                last.then_inc(s.cum_ready, 1)

            def first_of(row_max, values, out_ap):
                own(tt(rt[:, 3], values, spread(row_max, [P, NT, 4]), ALU.is_equal))
                d = desc4[:, :].rearrange("p (a k) -> p a k", a=1).to_broadcast([P, NT, 4])
                own(tt(rt[:, 4], rt[:, 3], d, ALU.mult))
                own(nc.vector.tensor_reduce(rt[:, 5, :, 0:1], rt[:, 4], AX_X, ALU.max))
                own(tt(out_ap, d, spread(rt[:, 5, :, 0:1], [P, NT, 4]), ALU.is_equal))

            def route(layer):
                s = layers[layer]
                reduce = nc.vector.tensor_reduce
                dve.wait_ge(logits_psum, layer + 1)
                own(tt(lg[:, :, :], MISC[:, 0:NT * NR].rearrange("p (t n) -> p t n", t=NT),
                       b_rt[:, layer:layer + 1, :].to_broadcast([P, NT, NR]), ALU.add))
                groups = lg[:, :, 0:N_GROUPS]
                experts = lg[:, :, N_GROUPS:NR].rearrange("p t (g e) -> p t g e", g=N_GROUPS)
                own(reduce(rt[:, 0, :, 0:1], groups, AX_X, ALU.max))
                tt(rt[:, 1], groups, spread(rt[:, 0, :, 0:1], [P, NT, 4]), ALU.subtract
                   ).then_inc(rt_shift, 1)
                first_of(rt[:, 0, :, 0:1], groups, rt[:, 6])
                in_group = rt[:, 6].rearrange("p t (g a) -> p t g a", a=1).to_broadcast(
                    [P, NT, N_GROUPS, PER_GROUP])
                for t in range(NT):
                    last = tt(picked[:, t], experts[:, t], in_group[:, t], ALU.mult)
                own(last)
                own(reduce(rt[:, 7], picked[:, :, :, :].rearrange("p t g e -> p t e g"), AX_X, ALU.add))
                own(reduce(rt[:, 8, :, 0:1], rt[:, 7], AX_X, ALU.max))
                first_of(rt[:, 8, :, 0:1], rt[:, 7], rt[:, 9])
                own(stt(rt[:, 10], rt[:, 9], NEG, rt[:, 7], ALU.mult, ALU.add))
                own(reduce(rt[:, 8, :, 1:2], rt[:, 10], AX_X, ALU.max))
                first_of(rt[:, 8, :, 1:2], rt[:, 10], rt[:, 11])
                tt(rt[:, 12, :, 0:1], rt[:, 8, :, 1:2], rt[:, 8, :, 0:1], ALU.subtract
                   ).then_inc(rt_gap, 1)
                dve.wait_ge(rt_exp, layer + 1)
                own(reduce(rt[:, 13, :, 0:1], rt[:, 2], AX_X, ALU.add))
                dve.wait_ge(rt_gap_exp, layer + 1)
                own(stt(rt[:, 13, :, 1:2], rt[:, 12, :, 1:2], 1.0, rt[:, 13, :, 0:1], ALU.add, ALU.mult))
                own(nc.vector.reciprocal(rt[:, 13, :, 2:3], rt[:, 13, :, 1:2]))
                own(tt(rt[:, 13, :, 3:4], rt[:, 13, :, 2:3], rt[:, 12, :, 1:2], ALU.mult))
                own(tt(rt[:, 3], rt[:, 9], spread(rt[:, 13, :, 2:3], [P, NT, 4]), ALU.mult))
                own(tt(rt[:, 4], rt[:, 11], spread(rt[:, 13, :, 3:4], [P, NT, 4]), ALU.mult))
                own(tt(rt[:, 3], rt[:, 3], rt[:, 4], ALU.add))
                own(tt(rt[:, 4], rt[:, 9], rt[:, 11], ALU.add))
                for t in range(NT):
                    def over_groups(value):
                        return value[:, t:t + 1, :].to_broadcast([P, N_GROUPS, PER_GROUP])
                    tt(chosen_f[:, t].rearrange("p (g e) -> p g e", g=N_GROUPS), in_group[:, t],
                       over_groups(rt[:, 4]), ALU.mult)
                    last = tt(weight_of[:, t, 0:N_EXPERTS].rearrange("p (g e) -> p g e", g=N_GROUPS),
                              in_group[:, t], over_groups(rt[:, 3]), ALU.mult)
                own(last)
                nc.vector.tensor_copy(chosen_bf[:, :, :], chosen_f[:, :, :]).then_inc(chosen, 1)
                for r in range(1, ROUNDS):
                    nc.vector.tensor_copy(weight_of[:, :, N_EXPERTS * r:N_EXPERTS * (r + 1)],
                                          weight_of[:, :, 0:N_EXPERTS])
                nc.vector.tensor_copy(weight_of[:, :, ROUNDS * N_EXPERTS:], weight_of[:, :, 0:1])
                dve.wait_ge(rank_psum, layer + 1)
                own(stt(picked[:, :, :, :].rearrange("p t g e -> p t (g e)"),
                        Y[:, 0:NT * N_EXPERTS].rearrange("p (t e) -> p t e", t=NT), 1.0,
                        chosen_f[:, :, :], ALU.add, ALU.mult))
                for r in range(ROUNDS):
                    last = ts(slot_of[:, :, N_EXPERTS * r:N_EXPERTS * (r + 1)],
                              picked[:, :, :, :].rearrange("p t g e -> p t (g e)"),
                              -1.0 - SLOTS * r, None, ALU.add)
                own(last)
                own(reduce(most[:, 0:1], Y[:, NT * N_EXPERTS:(NT + 1) * N_EXPERTS], AX_X, ALU.max))
                own(ts(most[:, 1:2], most[:, 0:1], float(SLOTS), float((ROUNDS - 1) * N_EXPERTS // QUAD),
                       ALU.is_gt, ALU.mult))
                ts(last_quads[:, layer:layer + 1], most[:, 1:2], float(N_EXPERTS // QUAD - 1), None, ALU.add
                   ).then_inc(s.slots_ready, 1)

            own(nc.vector.memset(wf3[:, :, :], 0.0))
            nc.vector.memset(b_f[:, :], 0.0).then_inc(forget_zeroed, 1)
            nc.vector.memset(slot_of[:, :, ROUNDS * N_EXPERTS:], -1.0).then_inc(forget_zeroed, 1)

            for layer in range(LAYERS):
                s = layers[layer]
                mix_norm(layer)
                if not whole(layer, 0):
                    weights_low(layer, 0)
                    dve.wait_ge(s.forget_psum, 1)
                    tokens_low(s)
                spreads = norm_steps[layer]
                for j in range(STEPS):
                    kind, at = PLAN[layer][j // 2]
                    to_split = j // 2 + 1 if j % 2 == 0 and j // 2 + 1 < UNITS else None
                    if to_split and j > 0:
                        weights_low(layer, to_split)
                    for g in range(spread_by(layer, j - 1), spread_by(layer, j)):
                        dve.wait_ge(s.root_spread, g + 1)
                        is_k = 1 if 2 * g >= spreads else 0
                        q2 = qkT[:, 2 * g:2 * g + 2, :].rearrange("p a b -> p (a b)")
                        stt(q2, q2, g_qk[:, layer, is_k:is_k + 1], bank[2 + g % 4][:, :],
                            ALU.mult, ALU.mult).then_inc(s.root_applied, 1)
                    dve.wait_ge(s.proj_psum, j + 1)
                    if kind == "v":
                        dst = v_sb[:, j % 2, at:at + COLS]
                    else:
                        c = at + 2 * (j % 2)
                        dst = qkT[:, c:c + 2, :].rearrange("p a b -> p (a b)")
                    if kind == "scaled":
                        ts(dst, bank[j % 2][:, :], SCALE, None, ALU.mult).then_inc(s.proj_out, 1)
                    else:
                        nc.vector.tensor_copy(dst, bank[j % 2][:, :]).then_inc(s.proj_out, 1)
                    if to_split and j == 0:
                        weights_low(layer, to_split)
                    if whole(layer, 0) and j == 1:
                        tokens_low(s)
                    if layer == 1 and j == 1:
                        forget_gate(s)
                    if j == norm_steps[layer]:
                        dve.wait_ge(s.sumsq_psum, norm_steps[layer])
                        own(root(s, roots_before(layer, "qk"), SUM_BANK[0:96, 0:T], 96, 0, T, HD))
                        own(nc.vector.tensor_copy(root_parts[:, :], root_y[0:96, :]))
                        own(tt(root_t[0:96, :], root_y[0:96, :], root_parts[:, :], ALU.subtract))
                        for g in (1, 2):
                            r = slice(32 * g, 32 * (g + 1))
                            last = nc.vector.tensor_copy(root_parts[r, :], root_t[r, :])
                        own(last)
                        own(tt(root_t[64:96, :], root_t[64:96, :], root_parts[64:96, :],
                               ALU.subtract))
                        nc.vector.tensor_copy(root_parts[64:96, :], root_t[64:96, :]
                                              ).then_inc(s.root_done, 1)
                        if layer == 0:
                            make_tables()
                for i in range(JOBS + 2):
                    if 1 <= i < JOBS + 1:
                        second(layer, i - 1)
                    if i < JOBS:
                        first(layer, i)
                    if 1 <= i < JOBS + 1:
                        third(layer, i - 1)
                    if layer == 0 and i == JOBS:
                        dve.wait_ge(s.o_sumsq, SUBLN)
                        root(s, roots_before(layer, "sub"), SUM_BANK[0:32, 0:T], 32, 0, T, P
                             ).then_inc(s.root_done, 1)
                if layer == 0:
                    for g in range(2):
                        dve.wait_ge(s.sub_spread, g + 1)
                        o2 = oT[:, 2 * g:2 * g + 2, :].rearrange("p a b -> p (a b)")
                        stt(o2, o2, g_sub[:, :], bank[g][:, :], ALU.mult, ALU.mult
                            ).then_inc(s.sub_applied, 1)
                mixed_and_normed(layer)
                if layer == 0:
                    dve.wait_ge(router_loaded, ROUTER)
                route(layer)

                def make_take(n):
                    for t in range(NT):
                        last = ts(take[:, t, :], slot_id[:, :, :].rearrange("p a b -> p (a b)"),
                                  slot_of[:, t, bass.ds(n, 1)], None, ALU.is_equal)
                    last.then_inc(s.take_ready, 1)

                def make_give(n):
                    for t in range(NT):
                        last = ts(give[:, t, :], slot_id[:, :, :].rearrange("p a b -> p (a b)"),
                                  slot_of[:, t, bass.ds(n, 1)], weight_of[:, t, bass.ds(n, 1)],
                                  ALU.is_equal, ALU.mult)
                    last.then_inc(s.give_ready, 1)

                def leave_gathered():
                    for h, b in enumerate((MISC, Y)):
                        last = tt(xT[:, SUB * h:SUB * (h + 1), :],
                           b[:, :].rearrange("p (c t) -> p c t", c=SUB)[:, :, 0:SLOTS],
                           gains(gain_ffn, layer, h, SLOTS), ALU.mult)
                    last.then_inc(s.xt_ready, 1)

                make_take(0)
                make_give(0)
                dve.wait_ge(s.slots_ready, 1)
                last_quad = dve.value_load(last_quads[0:1, layer:layer + 1],
                                          min_val=N_EXPERTS // QUAD - 1,
                                          max_val=ROUNDS * N_EXPERTS // QUAD - 1)
                dve.wait_ge(s.gathered, 1)
                leave_gathered()
                with dve.Fori(0, last_quad + 1) as quad:
                    for k in range(QUAD):
                        make_take(turns(quad, k + 1))
                        dve.wait_ge(s.gate_exp, turns(quad, k + 1))
                        ts(sig, gate_e, 1.0, None, ALU.add).then_inc(s.gate_plus, 1)
                        dve.wait_ge(s.gate_plus, turns(quad, k + 1))
                        nc.vector.reciprocal(sig, sig).then_inc(s.gate_inv, 1)
                        dve.wait_ge(s.gate_inv, turns(quad, k + 1))
                        tt(sig, GATE[:, :], sig, ALU.mult).then_inc(s.gate_act, 1)
                        dve.wait_ge(s.gate_act, turns(quad, k + 1))
                        dve.wait_ge(*used(s, quad, k, 3))
                        tt(hid, UP[:, :], sig, ALU.mult).then_inc(s.hid_ready, 1)
                        dve.wait_ge(s.gathered, turns(quad, k + 2))
                        leave_gathered()
                        dve.wait_ge(s.hidT_psum, turns(quad, k + 1))
                        nc.vector.tensor_copy(hidT, UP[:, :].rearrange("p (s t) -> p s t", s=SUB)
                                              ).then_inc(s.hidT_ready, 1)
                        dve.wait_ge(s.giveT_psum, turns(quad, k + 1))
                        make_give(turns(quad, k + 1))
                for q in range(4):
                    dve.wait_ge(s.scattered, last_quad * (4 * QUAD) + (4 * (QUAD - 1) + q + 1))
                    nc.vector.tensor_copy(x_sb[:, q // 2, HALF * (q % 2):HALF * (q % 2 + 1)],
                                          ACC[q][:, :]).then_inc(s.moe_out, 1)

        @block.tensor
        def _(pe):
            mm = nc.tensor.matmul

            def tokens_across(s, n, groups, first_bank):
                for g in groups:
                    t, h = g // 2, g % 2
                    pe.wait_ge(s.hn_ready, NT * n + t + 1)
                    for c in range(SUB):
                        last = nc.tensor.transpose(bank[first_bank + g][:, P * c:P * (c + 1)],
                                                   by_chunk((hn, fn)[n], t, h, c), ident[:, :])
                    last.then_inc(s.ht_psum, 1)

            def scores(layer, j):
                s = layers[layer]
                banks = score_banks(layer, j)
                if layer == 0:
                    cq, ck = (j, A_HEADS + j) if j < A_HEADS else (4 + j, 8 + j)
                else:
                    cq, ck = j, JOBS + j
                if is_b(layer, j) and j == A_HEADS + 2:
                    pe.wait_ge(s.pt_act, A_HEADS)
                elif is_b(layer, j) and j > A_HEADS + 2:
                    pe.wait_ge(s.exp_done, 2 * (j - 2))
                elif j >= 2:
                    pe.wait_ge(s.exp_done, 2 * (j - 1))
                if is_b(layer, j):
                    for m in range(2):
                        r = slice(HD * m, HD * (m + 1))
                        mm(banks[m][:, 0:T], qkT[r, ck, 0:P], qkT[r, cq, 0:T], start=True,
                           stop=False, skip_group_check=True)
                    for m in range(2):
                        r = slice(HD * m, HD * (m + 1))
                        mm(banks[m][:, T:SW], qkT[r, ck, P:T], qkT[r, cq, P:T], start=False,
                           stop=False, skip_group_check=True).then_inc(s.scores_psum, 1)
                    return
                for m in range(2):
                    if layer == 0:
                        mm(banks[m][:, 0:SW], ident_bf[:, :], bias_a[:, j, :], start=True, stop=False,
                           skip_group_check=True)
                        continue
                    mm(banks[m][:, 0:SW], ident_bf[:, :], mask_causal[:, :], start=True, stop=False,
                       skip_group_check=True)
                    head = sel_head[:, 2 * j + m:2 * j + m + 1]
                    for i in range(NT):
                        keys = P * (i + 1)
                        mm(banks[m][:, map_cols(i)], head.to_broadcast([96, P]), cum_neg[:, 0:keys],
                           start=False, stop=False, skip_group_check=True)
                        mm(banks[m][:, map_cols(i)], cum_pos[:, P * i:P * (i + 1)],
                           head.to_broadcast([96, keys]), start=False, stop=False,
                           skip_group_check=True)
                for i in range(NT):
                    for m in range(2):
                        r = slice(HD * m, HD * (m + 1))
                        last = mm(banks[m][:, map_cols(i)], qkT[r, cq, P * i:P * (i + 1)],
                                  qkT[r, ck, 0:P * (i + 1)], start=False, stop=(i == NT - 1),
                                  skip_group_check=True)
                        if i == NT - 1:
                            last.then_inc(s.scores_psum, 1)

            def across(layer, j):
                s = layers[layer]
                n = maps_before(layer, j)
                for m in range(maps_before(layer, j + 1) - n):
                    slot = 2 * (j % 2) + m
                    pe.wait_ge(s.p_ready, n + m + 1)
                    if is_b(layer, j):
                        b, soft = score_banks(layer, j)[m], pT[:, slot, :]
                        mm(b[:, 0:SW], neg_from[:, :], soft, start=False, stop=False,
                           skip_group_check=True)
                        mm(b[:, P:T], neg_ones[:, :], soft[:, T:SW], start=False, stop=False,
                           skip_group_check=True)
                        mm(b[:, 0:SW], ident_bf[:, :], mask_strict[:, :], start=False, stop=True,
                           skip_group_check=True).then_inc(s.t_psum, 1)
                        continue
                    if j >= 1:
                        pe.wait_ge(s.pt_dve if m else s.pt_act, j)
                    for k in range(3):
                        last = nc.tensor.transpose(bank[m][:, P * k:P * (k + 1)],
                                                   probs[:, slot, P * k:P * (k + 1)], ident[:, :])
                    last.then_inc(s.t_psum, 1)

            def weighted_values(layer, j):
                s = layers[layer]
                if is_b(layer, j):
                    pe.wait_ge(s.exp_done, 2 * j + 2)
                else:
                    pe.wait_ge(s.pt_act, j + 1)
                    if layer == 1:
                        pe.wait_ge(s.pt_dve, j + 1)
                if j >= 1:
                    pe.wait_ge(s.o_ready, j)
                source = probs if is_b(layer, j) else pT
                slot = 2 * (j % 2)
                if layer == 0 and j < A_HEADS:
                    heads = [(slice(0, P), P * j, P)]
                else:
                    at = HALF + P * (j - A_HEADS) if layer == 0 else P * j
                    heads = [(slice(HD * m, HD * (m + 1)), at + HD * m, HD) for m in range(2)]
                for k in range(NT):
                    for m, (r, col, n) in enumerate(heads):
                        w = source[:, slot + m, 0:T] if k == 0 else source[:, slot + m, T:SW]
                        last = mm(O_BANK[r, P * k:T], v_sb[:, k, col:col + n], w, start=(k == 0),
                                  stop=(k == NT - 1), skip_group_check=True)
                last.then_inc(s.o_psum, 1)

            def sub_sum(s, j):
                pe.wait_ge(s.o_squared, j + 1)
                mm(SUM_BANK[0:32, 0:T], slide_all[:, 31 - j:63 - j], o_squares[:, j, :],
                   start=(j == 0), stop=(j == SUBLN - 1)).then_inc(s.o_sumsq, 1)

            pe.wait_ge(consts_made, CONSTS)
            for layer in range(LAYERS):
                s = layers[layer]
                tokens_across(s, 0, range(4), 2)
                pe.wait_ge(s.ht_ready, 4)
                if layer == 1:
                    pe.wait_ge(forget_loaded, FORGET)
                    for c in range(NC):
                        last = mm(O_BANK[0:96, 0:T], wf3[:, c, :], hT[:, c, :], start=(c == 0),
                                  stop=(c == NC - 1))
                    last.then_inc(s.forget_psum, 1)
                normed = norm_steps[layer]

                def spread_roots(g0, g1):
                    for g in range(g0, g1):
                        if g >= 4:
                            pe.wait_ge(s.root_applied, g - 3)
                        for c in range(2):
                            for m in range(2):
                                k = 2 * (2 * g + c) + m
                                last = mm(bank[2 + g % 4][HD * m:HD * (m + 1), T * c:T * (c + 1)],
                                          sel_head[:, k:k + 1].to_broadcast([96, HD]),
                                          root_parts[:, :], start=True, stop=True)
                        last.then_inc(s.root_spread, 1)

                for j in range(STEPS):
                    kind, at = PLAN[layer][j // 2]
                    u = j // 2
                    if spread_by(layer, j):
                        pe.wait_ge(s.root_done, 1)
                    spread_roots(spread_by(layer, j - 1), spread_by(layer, j))
                    if j >= 2:
                        pe.wait_ge(s.proj_out, j - 1)
                    high, low = w_high[u % 2], w_low[u]
                    products = [(high, h_high), (low, h_high), (high, h_low)]
                    if whole(layer, u):
                        pe.wait_ge(s.unit_loaded[u], WIN)
                        products = [(win_view(u), hT)]
                    else:
                        pe.wait_ge(s.w_high, 2 * split(layer, u))
                        pe.wait_ge(s.h_high, 2)
                    for n, (w, x_part) in enumerate(products):
                        if n == 1:
                            pe.wait_ge(s.w_low, 2 * split(layer, u))
                        if n == 2:
                            pe.wait_ge(s.h_low, 2)
                        final = n == len(products) - 1
                        for half in range(1 if kind == "v" else 2):
                            for c in range(NC):
                                if kind == "v":
                                    t = j % 2
                                    last = mm(bank[j % 2][:, :], x_part[:, c, P * t:P * (t + 1)],
                                              w[:, c, :], start=(n == 0 and c == 0),
                                              stop=(final and c == NC - 1))
                                    continue
                                col = P * (2 * (j % 2) + half)
                                last = mm(bank[j % 2][:, T * half:T * (half + 1)],
                                          w[:, c, col:col + P], x_part[:, c, :],
                                          start=(n == 0 and half == 0 and c == 0),
                                          stop=(final and c == NC - 1), skip_group_check=True)
                    last.then_inc(s.proj_psum, 1)
                    if 1 <= j <= normed:
                        pe.wait_ge(s.squared, j)
                        for half in range(2):
                            c = 2 * (j - 1) + half
                            last = mm(SUM_BANK[0:96, 0:T], slide[:, 30 - 2 * c:126 - 2 * c],
                                      squares[(j - 1) % 2][:, T * half:T * (half + 1)],
                                      start=(c == 0), stop=(c == 2 * normed - 1))
                        last.then_inc(s.sumsq_psum, 1)
                if layer == 1:
                    pe.wait_ge(s.cum_ready, 1)
                else:
                    pe.wait_ge(tables_made, A_HEADS)
                pe.wait_ge(s.root_applied, normed)
                pe.wait_ge(s.proj_out, STEPS)
                for i in range(JOBS + 2):
                    if i < JOBS:
                        scores(layer, i)
                    if i >= 2:
                        weighted_values(layer, i - 2)
                    if 1 <= i < JOBS + 1:
                        across(layer, i - 1)
                    if layer == 0 and 3 <= i < 3 + SUBLN:
                        sub_sum(s, i - 3)
                if layer == 0:
                    pe.wait_ge(s.root_done, 2)
                    for g in range(2):
                        for c in range(2):
                            h = 2 * g + c
                            last = mm(bank[g][:, T * c:T * (c + 1)],
                                      ident[0:32, h:h + 1].to_broadcast([32, P]), root_y[0:32, :],
                                      start=True, stop=True)
                        last.then_inc(s.sub_spread, 1)
                    pe.wait_ge(s.sub_applied, 2)
                pe.wait_ge(wout_loaded, 32 * (layer + 1))
                pe.wait_ge(s.o_ready, JOBS)
                pe.wait_ge(s.exp_done, 2 * JOBS)
                for q in range(4):
                    t, h = q // 2, q % 2
                    for c in range(NC):
                        last = mm(bank[2 + q][:, :], oT[:, c, P * t:P * (t + 1)],
                                  wout_view(c // SUB)[:, c % SUB, HALF * h:HALF * (h + 1)], start=(c == 0),
                                  stop=(c == NC - 1))
                    last.then_inc(s.out_psum, 1)
                    if q == 2:
                        tokens_across(s, 1, (0, 1), 0)
                if layer == 0:
                    pe.wait_ge(router_loaded, ROUTER)
                for i in range(NT):
                    if i == 1:
                        tokens_across(s, 1, (2, 3), 0)
                    pe.wait_ge(s.ht_ready, 4 + 2 * (i + 1))
                    for c in range(NC):
                        last = mm(MISC[:, NR * i:NR * (i + 1)], hT[:, c, P * i:P * (i + 1)],
                                  w_rt[:, layer, c, :], start=(c == 0), stop=(c == NC - 1))
                last.then_inc(logits_psum, 1)
                for q in range(4):
                    last = mm(ACC[q][:, :], ident[:, :],
                              x_sb[:, q // 2, HALF * (q % 2):HALF * (q % 2 + 1)], start=True,
                              stop=False, skip_group_check=True)
                pe.wait_ge(chosen, layer + 1)
                ranks = [(0, [(before_bf, 0)]), (1, [(ones_bf, 0), (before_bf, 1)]),
                         (2, [(ones_bf, 0), (ones_bf, 1)])]
                for k, terms in ranks:
                    for n, (w, t) in enumerate(terms):
                        last = mm(Y[:, N_EXPERTS * k:N_EXPERTS * (k + 1)], w[:, :], chosen_bf[:, t, :],
                                  start=(n == 0), stop=(n == len(terms) - 1))
                last.then_inc(rank_psum, 1)

                def gather():
                    for c in range(NC):
                        b = MISC if c < SUB else Y
                        k = c % SUB
                        for t in range(NT):
                            last = mm(b[:, P * k:P * (k + 1)], by_chunk(fn, t, c // SUB, k),
                                      take[:, t, :], start=(t == 0), stop=(t == NT - 1))
                    last.then_inc(s.gathered, 1)

                def two_halves(b, left, quad, turn, units):
                    for h, u in enumerate(units):
                        slot, lap = place(turn, u)
                        pe.wait_ge(s.unit_loaded[slot], quad * (USES[slot] * 16)
                                   + ((WIN if slot < UNITS else 0) + 16 * (lap + 1)))
                        for k in range(SUB):
                            for half in range(2):
                                last = mm(b[SLOTS * half:SLOTS * (half + 1), :], left(h, k),
                                          expert_rhs(slot, k, half), start=(h == 0 and k == 0),
                                          stop=(h == 1 and k == SUB - 1))
                        last.then_inc(s.unit_used[slot], 1)

                def scatter(count):
                    pe.wait_ge(s.y_ready, count)
                    pe.wait_ge(s.giveT_ready, count)
                    for t in range(NT):
                        for half in range(2):
                            r = slice(SLOTS * half, SLOTS * (half + 1))
                            last = mm(ACC[2 * t + half][:, :], giveT[r, P * t:P * (t + 1)],
                                      y_sb[r, :], start=False, stop=False, skip_group_check=True)
                            last.then_inc(s.scattered, 1)

                pe.wait_ge(s.take_ready, 1)
                gather()
                pe.wait_ge(s.slots_ready, 1)
                last_quad = pe.value_load(last_quads[0:1, layer:layer + 1],
                                          min_val=N_EXPERTS // QUAD - 1,
                                          max_val=ROUNDS * N_EXPERTS // QUAD - 1)
                with pe.Fori(0, last_quad + 1) as quad:
                    for k in range(QUAD):
                        now, after = turns(quad, k + 1), turns(quad, k + 2)
                        pe.wait_ge(s.xt_ready, now)
                        if k >= 1:
                            pe.wait_ge(s.giveT_ready, turns(quad, k))
                        tokens = lambda h, c: xT[:, SUB * h + c, :]
                        two_halves(GATE, tokens, quad, k, (0, 1))
                        pe.wait_ge(s.take_ready, after)
                        if k >= 1:
                            pe.wait_ge(s.y_ready, turns(quad, k))
                        gather()
                        if k >= 1:
                            scatter(turns(quad, k))
                        two_halves(UP, tokens, quad, k, (2, 3))
                        pe.wait_ge(s.give_ready, now)
                        pe.wait_ge(s.gate_act, now)
                        for t in range(NT):
                            last = nc.tensor.transpose(GATE[:, P * t:P * (t + 1)], give[:, t, :],
                                                       ident[:, :])
                        last.then_inc(s.giveT_psum, 1)
                        pe.wait_ge(s.hid_ready, now)
                        for c in range(SUB):
                            part = hid.rearrange("p (q s) -> p s q", s=SUB)[:, c, :]
                            last = nc.tensor.transpose(UP[:, P * c:P * (c + 1)], part, ident[:, :])
                        last.then_inc(s.hidT_psum, 1)
                        pe.wait_ge(s.xt_ready, after)
                        pe.wait_ge(s.hidT_ready, now)
                        two_halves(Y, lambda h, c: hidT[:, c, SLOTS * h:SLOTS * (h + 1)], quad, k,
                                   (4, 5))
                    scatter(turns(quad, QUAD))


INPUTS = ["x", "norm_mix_g", "norm_ffn_g", "ab_w_in", "a_q_gain", "a_k_gain", "a_lam_q1", "a_lam_k1",
          "a_lam_q2", "a_lam_k2", "a_subln_g", "ab_w_out", "c_w_in", "c_b_f", "c_q_gain", "c_k_gain",
          "c_w_out", "moe_w_group", "moe_b_group", "moe_w_router", "moe_b_router", "moe_w_gate",
          "moe_w_up", "moe_w_down"]


def kernel(**inputs):
    import numpy as np
    from concourse import bacc
    from concourse.bass_utils import run_bass_kernel_spmd

    nc = bacc.Bacc("TRN2", target_bir_lowering=False, num_devices=1)
    arrays, args = {}, []
    for name in INPUTS:
        a = np.ascontiguousarray(inputs[name])
        arrays[f"in_{name}"] = a
        args.append(nc.dram_tensor(f"in_{name}", a.shape, mybir.dt.from_np(a.dtype),
                                   kind="ExternalInput").ap())
    args.append(nc.dram_tensor("out_0", (1, T, D), F32, kind="ExternalOutput").ap())
    trunk(nc, *args)
    r = run_bass_kernel_spmd(nc, [arrays], core_ids=[0])
    return r.results[0]["out_0"]
```
